# Optimizing a Trainium2 kernel written in Bass

```python
import math
import jax, jax.numpy as jnp
from jax import lax
import numpy as np

D_MODEL = 1024
BATCH = 1
SEQ = 512
DEPTH = 1
DEC_BATCH = 8
DEC_SEQ = 1
PAST_LEN = 4096
PAGE_SIZE = 128

H_A = 4
DK_A = 128
DV_A = 128
CONV_W = 4
H_B = 4
DK_B = 128
DV_B = 256
ROPE_BASE = 10000.0
CHUNK = 64
N_KEYS = 128
N_EXPERTS = N_KEYS * N_KEYS
PEER_HEADS = 8
PEER_DQ = 256
PEER_TOPK = 16
PEER_BLOCK = 128
EPS = 1e-6

QA = H_A * DK_A
VA = H_A * DV_A
QB = H_B * DK_B
VB = H_B * DV_B
CONV_CH = 2 * QA + VA
IN_SIZES = (CONV_CH, VA, H_A, H_A, QB, QB, VB, VB, D_MODEL, D_MODEL)
IN_DIM = CONV_CH + VA + 2 * H_A + 2 * QB + 2 * VB + 2 * D_MODEL

kernel_name = "hybrid_deltanet_retention_peer_step"

def rmsnorm(x, g):
    xf = x.astype(jnp.float32)
    y = xf * lax.rsqrt(jnp.mean(xf * xf, axis=-1, keepdims=True) + EPS)
    return (y * g.astype(jnp.float32)).astype(x.dtype)

def l2norm(x):
    xf = x.astype(jnp.float32)
    return xf * lax.rsqrt(jnp.sum(xf * xf, axis=-1, keepdims=True) + EPS)

def split_cols(t, sizes):
    out, o = [], 0
    for s in sizes:
        out.append(t[..., o:o + s])
        o += s
    return out

def chunk_len(L):
    return CHUNK if L % CHUNK == 0 else L

def to_chunks(t, C):
    B, L = t.shape[0], t.shape[1]
    return t.reshape((B, L // C, C) + t.shape[2:]).swapaxes(2, 3)

def from_chunks(o):
    B, N, H, C, D = o.shape
    return o.swapaxes(2, 3).reshape(B, N * C, H, D)

def causal_conv(x, buf, w):
    L = x.shape[1]
    xp = jnp.concatenate([buf.astype(x.dtype), x], axis=1)
    out = xp[:, 0:L] * w[0]
    for i in range(1, CONV_W):
        out = out + xp[:, i:i + L] * w[i]
    return jax.nn.silu(out), xp[:, -(CONV_W - 1):]

def rope(x, pos):
    half = x.shape[-1] // 2
    inv = ROPE_BASE ** (-jnp.arange(half, dtype=jnp.float32) / half)
    ang = pos[:, None] * inv[None, :]
    cos = jnp.cos(ang)[None, :, None, :]
    sin = jnp.sin(ang)[None, :, None, :]
    x1, x2 = x[..., :half], x[..., half:]
    return jnp.concatenate([x1 * cos - x2 * sin, x2 * cos + x1 * sin], axis=-1)

def gated_delta(q, k, v, beta, logd, S0):
    f32 = jnp.float32
    C = chunk_len(q.shape[1])
    q, k, v = (to_chunks(t.astype(f32), C) for t in (q, k, v))
    beta, logd = to_chunks(beta, C), to_chunks(logd, C)
    G = jnp.cumsum(logd, axis=-1)
    tril = jnp.tril(jnp.ones((C, C), bool))
    strict = jnp.tril(jnp.ones((C, C), bool), -1)
    decay_in = jnp.exp(jnp.where(tril, G[..., :, None] - G[..., None, :], -jnp.inf))
    kb = k * beta[..., None]
    Lmat = jnp.where(strict, jnp.einsum('bnhid,bnhjd->bnhij', kb, k) * decay_in, 0.0)
    eye = jnp.eye(C, dtype=f32)
    T = lax.linalg.triangular_solve(Lmat + eye, jnp.broadcast_to(eye, Lmat.shape),
                                    left_side=True, lower=True, unit_diagonal=True)
    u = jnp.einsum('bnhij,bnhje->bnhie', T, v * beta[..., None])
    w = jnp.einsum('bnhij,bnhjd->bnhid', T, kb * jnp.exp(G)[..., None])
    qk = jnp.einsum('bnhid,bnhjd->bnhij', q, k) * decay_in
    qg = q * jnp.exp(G)[..., None]
    kd = k * jnp.exp(G[..., -1:] - G)[..., None]
    gC = jnp.exp(G[..., -1])

    def step(S, xs):
        u_c, w_c, qk_c, qg_c, kd_c, g_c = xs
        v_new = u_c - jnp.einsum('bhcd,bhde->bhce', w_c, S)
        o = jnp.einsum('bhcd,bhde->bhce', qg_c, S) + jnp.einsum('bhij,bhje->bhie', qk_c, v_new)
        S = S * g_c[..., None, None] + jnp.einsum('bhcd,bhce->bhde', kd_c, v_new)
        return S, o

    xs = tuple(jnp.moveaxis(t, 1, 0) for t in (u, w, qk, qg, kd, gC))
    S, o = lax.scan(step, S0.astype(f32), xs)
    return from_chunks(jnp.moveaxis(o, 0, 1)), S

def retention(q, k, v, S0):
    f32 = jnp.float32
    C = chunk_len(q.shape[1])
    q, k, v = (to_chunks(t.astype(f32), C) for t in (q, k, v))
    logg = jnp.log1p(-(2.0 ** (-5.0 - jnp.arange(H_B, dtype=f32))))
    idx = jnp.arange(C, dtype=f32)
    tril = jnp.tril(jnp.ones((C, C), bool))
    D = jnp.exp(jnp.where(tril[None], (idx[:, None] - idx[None, :])[None] * logg[:, None, None], -jnp.inf))
    q_dec = jnp.exp((idx[None, :] + 1.0) * logg[:, None])
    k_dec = jnp.exp((C - 1.0 - idx[None, :]) * logg[:, None])
    gC = jnp.exp(C * logg)
    inner = jnp.einsum('bnhij,bnhje->bnhie', jnp.einsum('bnhid,bnhjd->bnhij', q, k) * D, v)
    qd = q * q_dec[:, :, None]
    kd = k * k_dec[:, :, None]

    def step(S, xs):
        inner_c, qd_c, kd_c, v_c = xs
        o = inner_c + jnp.einsum('bhcd,bhde->bhce', qd_c, S)
        S = S * gC[:, None, None] + jnp.einsum('bhcd,bhce->bhde', kd_c, v_c)
        return S, o

    xs = tuple(jnp.moveaxis(t, 1, 0) for t in (inner, qd, kd, v))
    S, o = lax.scan(step, S0.astype(f32), xs)
    return from_chunks(jnp.moveaxis(o, 0, 1)), S

def token_mixers(xn, conv_buf, s_delta, s_ret, pos, w_in, conv_w, a_log, dt_bias,
                 gn_a, gn_b, w_br_a, w_br_b, w_out):
    f32 = jnp.float32
    B, L, _ = xn.shape
    proj = jnp.einsum('bld,de->ble', xn, w_in)
    qkv_a, gate_a, b_a, a_a, q_b, k_b, v_b, gate_b, sel_a, sel_b = split_cols(proj, IN_SIZES)
    qkv_a, conv_new = causal_conv(qkv_a, conv_buf, conv_w)
    q_a, k_a, v_a = split_cols(qkv_a, (QA, QA, VA))
    q_a = l2norm(q_a.reshape(B, L, H_A, DK_A)) * (DK_A ** -0.5)
    k_a = l2norm(k_a.reshape(B, L, H_A, DK_A))
    v_a = v_a.reshape(B, L, H_A, DV_A)
    beta = jax.nn.sigmoid(b_a.astype(f32))
    logd = -jnp.exp(a_log.astype(f32)) * jax.nn.softplus(a_a.astype(f32) + dt_bias.astype(f32))
    o_a, s_delta_new = gated_delta(q_a, k_a, v_a, beta, logd, s_delta)
    o_a = rmsnorm(o_a, gn_a) * jax.nn.silu(gate_a.reshape(B, L, H_A, DV_A).astype(f32))
    o_a = o_a.reshape(B, L, VA).astype(xn.dtype)
    q_b = rope(q_b.reshape(B, L, H_B, DK_B).astype(f32), pos)
    k_b = rope(k_b.reshape(B, L, H_B, DK_B).astype(f32), pos) * (DK_B ** -0.5)
    v_b = v_b.reshape(B, L, H_B, DV_B)
    o_b, s_ret_new = retention(q_b, k_b, v_b, s_ret)
    o_b = rmsnorm(o_b, gn_b) * jax.nn.silu(gate_b.reshape(B, L, H_B, DV_B).astype(f32))
    o_b = o_b.reshape(B, L, VB).astype(xn.dtype)
    merged = (jax.nn.sigmoid(sel_a) * jnp.einsum('blv,vd->bld', o_a, w_br_a)
              + jax.nn.sigmoid(sel_b) * jnp.einsum('blv,vd->bld', o_b, w_br_b))
    return jnp.einsum('bld,de->ble', merged, w_out), conv_new, s_delta_new, s_ret_new

def peer(h, w_q, keys, u_tab, v_tab):
    T = h.shape[0]
    nblk = -(-T // PEER_BLOCK)
    hp = jnp.pad(h, ((0, nblk * PEER_BLOCK - T), (0, 0))).reshape(nblk, PEER_BLOCK, D_MODEL)
    n_cand = PEER_TOPK * PEER_TOPK

    def block(xb):
        q = jnp.einsum('td,de->te', xb, w_q).reshape(PEER_BLOCK, PEER_HEADS, 2, PEER_DQ // 2)
        s = jnp.einsum('thpd,hpkd->thpk', q, keys).astype(jnp.float32)
        s_top, i_top = lax.top_k(s, PEER_TOPK)
        cand = (s_top[:, :, 0, :, None] + s_top[:, :, 1, None, :]).reshape(PEER_BLOCK, PEER_HEADS, n_cand)
        cand_idx = (i_top[:, :, 0, :, None] * N_KEYS + i_top[:, :, 1, None, :]).reshape(PEER_BLOCK, PEER_HEADS, n_cand)
        best, sel = lax.top_k(cand, PEER_TOPK)
        eidx = jnp.take_along_axis(cand_idx, sel, axis=-1)
        gate = jax.nn.softmax(best, axis=-1)
        act = jax.nn.gelu(jnp.einsum('td,thkd->thk', xb, u_tab[eidx]).astype(jnp.float32), approximate=False)
        coef = (gate * act).astype(xb.dtype)
        return jnp.einsum('thk,thkd->td', coef, v_tab[eidx])

    return lax.map(block, hp).reshape(nblk * PEER_BLOCK, D_MODEL)[:T]

def trunk(x, conv_buf, s_delta, s_ret, pos, layer_w, norm_final):
    (norm_mix, w_in, conv_w, a_log, dt_bias, gn_a, gn_b, w_br_a, w_br_b, w_out,
     norm_ffn, peer_wq, peer_keys, peer_u, peer_v) = layer_w
    B, L, _ = x.shape
    h = x
    convs, deltas, rets = [], [], []
    for l in range(DEPTH):
        m, c_new, sd_new, sr_new = token_mixers(
            rmsnorm(h, norm_mix[l]), conv_buf[l], s_delta[l], s_ret[l], pos,
            w_in[l], conv_w[l], a_log[l], dt_bias[l], gn_a[l], gn_b[l], w_br_a[l], w_br_b[l], w_out[l])
        h = h + m
        f = peer(rmsnorm(h, norm_ffn[l]).reshape(B * L, D_MODEL), peer_wq[l], peer_keys[l], peer_u[l], peer_v[l])
        h = h + f.reshape(B, L, D_MODEL)
        convs.append(c_new)
        deltas.append(sd_new)
        rets.append(sr_new)
    return rmsnorm(h, norm_final), jnp.stack(convs), jnp.stack(deltas), jnp.stack(rets)

def setup_inputs(seed: int = 0) -> dict:
    key = jax.random.key(seed)
    ks = jax.random.split(key, 24)

    def nrm(k, shape, scale):
        return jax.random.normal(k, shape, jnp.float32) * scale

    dt = jnp.exp(jax.random.uniform(ks[9], (DEPTH, H_A), jnp.float32, math.log(1e-3), math.log(1e-1)))
    return {
        "x_prompt": nrm(ks[0], (BATCH, SEQ, D_MODEL), 1.0),
        "x_sample": nrm(ks[1], (DEC_BATCH, DEC_SEQ, D_MODEL), 1.0),
        "state_conv_a": nrm(ks[2], (DEPTH, DEC_BATCH, CONV_W - 1, CONV_CH), 1.0),
        "state_delta": nrm(ks[3], (DEPTH, DEC_BATCH, H_A, DK_A, DV_A), DK_A ** -0.5),
        "state_ret": nrm(ks[4], (DEPTH, DEC_BATCH, H_B, DK_B, DV_B), 0.5),
        "norm_mix": 1.0 + nrm(ks[5], (DEPTH, D_MODEL), 0.02),
        "w_in": nrm(ks[6], (DEPTH, D_MODEL, IN_DIM), D_MODEL ** -0.5),
        "conv_w": nrm(ks[7], (DEPTH, CONV_W, CONV_CH), CONV_W ** -0.5),
        "a_log": jnp.log(jax.random.uniform(ks[8], (DEPTH, H_A), jnp.float32, 1.0, 16.0)),
        "dt_bias": dt + jnp.log(-jnp.expm1(-dt)),
        "gn_a": 1.0 + nrm(ks[10], (DEPTH, DV_A), 0.02),
        "gn_b": 1.0 + nrm(ks[11], (DEPTH, DV_B), 0.02),
        "w_br_a": nrm(ks[12], (DEPTH, VA, D_MODEL), VA ** -0.5),
        "w_br_b": nrm(ks[13], (DEPTH, VB, D_MODEL), VB ** -0.5),
        "w_out": nrm(ks[14], (DEPTH, D_MODEL, D_MODEL), D_MODEL ** -0.5),
        "norm_ffn": 1.0 + nrm(ks[15], (DEPTH, D_MODEL), 0.02),
        "peer_wq": nrm(ks[16], (DEPTH, D_MODEL, PEER_HEADS * PEER_DQ), D_MODEL ** -0.5),
        "peer_keys": nrm(ks[17], (DEPTH, PEER_HEADS, 2, N_KEYS, PEER_DQ // 2), (PEER_DQ // 2) ** -0.5),
        "peer_u": nrm(ks[18], (DEPTH, N_EXPERTS, D_MODEL), D_MODEL ** -0.5),
        "peer_v": nrm(ks[19], (DEPTH, N_EXPERTS, D_MODEL), PEER_HEADS ** -0.5),
        "norm_final": 1.0 + nrm(ks[20], (D_MODEL,), 0.02),
    }

def reference(x_prompt, x_sample, state_conv_a, state_delta, state_ret,
              norm_mix, w_in, conv_w, a_log, dt_bias, gn_a, gn_b, w_br_a, w_br_b, w_out,
              norm_ffn, peer_wq, peer_keys, peer_u, peer_v, norm_final):
    layer_w = (norm_mix, w_in, conv_w, a_log, dt_bias, gn_a, gn_b, w_br_a, w_br_b, w_out,
               norm_ffn, peer_wq, peer_keys, peer_u, peer_v)
    B, L = x_prompt.shape[0], x_prompt.shape[1]
    Bs, Ls = x_sample.shape[0], x_sample.shape[1]
    zero_conv = jnp.zeros((DEPTH, B, CONV_W - 1, CONV_CH), x_prompt.dtype)
    zero_delta = jnp.zeros((DEPTH, B, H_A, DK_A, DV_A), jnp.float32)
    zero_ret = jnp.zeros((DEPTH, B, H_B, DK_B, DV_B), jnp.float32)
    pos_p = jnp.arange(L, dtype=jnp.float32)
    y_prompt, conv_p, delta_p, ret_p = trunk(x_prompt, zero_conv, zero_delta, zero_ret, pos_p, layer_w, norm_final)
    pos_s = PAST_LEN + jnp.arange(Ls, dtype=jnp.float32)
    y_sample, conv_s, delta_s, ret_s = trunk(x_sample, state_conv_a, state_delta, state_ret, pos_s, layer_w, norm_final)
    return (y_prompt, y_sample,
            conv_p.astype(x_prompt.dtype), delta_p.astype(x_prompt.dtype), ret_p.astype(x_prompt.dtype),
            conv_s.astype(state_conv_a.dtype), delta_s.astype(state_delta.dtype), ret_s.astype(state_ret.dtype))


_drawn_inputs = setup_inputs


def setup_inputs(seed=0):
    import zlib

    import numpy as np

    out = dict(_drawn_inputs(seed))
    spreads = {}
    factors = {'gn_a': 30.494, 'gn_b': 33.738, 'norm_final': 25.67, 'norm_ffn': 13.162}
    for name, (base, spread) in spreads.items():
        noise = np.random.default_rng([zlib.crc32(name.encode()), seed]).standard_normal(out[name].shape)
        drawn = base * np.exp(spread * noise) if base else spread * noise
        out[name] = __import__('jax').numpy.asarray(drawn.astype(out[name].dtype))
    for name, factor in factors.items():
        out[name] = (out[name] * factor).astype(out[name].dtype)
    return out
```

```python
import numpy as np
from contextlib import ExitStack

import concourse.bass as bass
from concourse import mybir

F32 = mybir.dt.float32
F32R = mybir.dt.float32r
U32 = mybir.dt.uint32
ALU = mybir.AluOpType
ACT = mybir.ActivationFunctionType
AX = mybir.AxisListType
ds = bass.ds

P = 128
D = 1024
DC = D // P
NP_TOK = 512
NS = 8
T = NP_TOK + NS
HALF = T // 2
NT = 5
ROWS = [P, P, P, P, NS]
H = 4
DK = 128
DV_B = 256
QA = H * DK
CONV_W = 4
CONV_CH = 3 * QA
CT = CONV_CH // P
PAD = CONV_W - 1
VB = H * DV_B
IN_DIM = CONV_CH + QA + 2 * H + 2 * H * DK + 2 * VB + 2 * D
COL_GATE_A = CONV_CH
COL_BA = COL_GATE_A + QA
COL_QK_B = COL_BA + 2 * H
COL_V_B = COL_QK_B + 2 * H * DK
COL_GATE_B = COL_V_B + VB
COL_SEL_A = COL_GATE_B + VB
COL_SEL_B = COL_SEL_A + D
EPS = 1e-6
PAST_LEN = 4096
NK = 128
PH = 8
TOPK = 16
HP = 2 * PH
WCOLS = 256
LEVELS = 7
TB = 104
NB = T // TB
GJ = 2
TG = 4
FAR = -1e30
LOWEST = -3.0e38


def gammas():
    return 1.0 - 2.0 ** (-5.0 - np.arange(H, dtype=np.float64))


def constants():
    i = np.arange(P)
    j_, i_ = i[:, None], i[None, :]
    eye = np.eye(P, dtype=np.float32)
    upto = (j_ <= i_).astype(np.float32)
    neg = np.where(j_ <= i_, 0.0, FAR).astype(np.float32)
    masks = np.zeros((P, LEVELS, P), np.float32)
    for l in range(LEVELS):
        s = 1 << l
        masks[:, l] = ((j_ // (2 * s) == i_ // (2 * s)) & (i_ % (2 * s) >= s) & (j_ % (2 * s) < s))
    half = DK // 2
    inv = (np.float32(10000.0) ** (-np.arange(half, dtype=np.float32) / np.float32(half))).astype(np.float32)
    pos = np.concatenate([np.arange(NP_TOK), np.full(NS, PAST_LEN)]).astype(np.float32)
    ang = (inv[:, None] * pos[None, :]).astype(np.float32)
    cos, sin = np.cos(ang), np.sin(ang)
    rope = np.zeros((P, 2, T), np.float32)
    rope[:half, 0], rope[half:, 0] = cos, cos
    rope[:half, 1], rope[half:, 1] = sin, -sin
    lg = np.log(gammas())
    dec = np.zeros((P, H, P), np.float32)
    qdec = np.zeros((P, H, P), np.float32)
    kdec = np.zeros((P, H), np.float32)
    for h in range(H):
        dec[:, h] = np.where(j_ <= i_, np.exp(np.minimum((i_ - j_), P) * lg[h] * (j_ <= i_)), 0.0)
        qdec[:, h] = np.exp((i_ + 1.0) * lg[h])
        kdec[:, h] = np.exp((P - 1.0 - i) * lg[h])
    sq = np.concatenate([eye, upto, neg, np.broadcast_to(np.arange(P, dtype=np.float32), (P, P)),
                         np.ones((P, P), np.float32)], axis=1)
    eye8 = np.broadcast_to(np.eye(NS, dtype=np.float32).reshape(1, -1), (P, NS * NS))
    return {
        "c_square": np.ascontiguousarray(sq, np.float32),
        "c_masks": masks.reshape(P, -1),
        "c_rope": rope.reshape(P, -1),
        "c_ret": np.ascontiguousarray(np.concatenate([dec.reshape(P, -1), qdec.reshape(P, -1), kdec, eye8], axis=1), np.float32),
    }


def fence(eng, ins, sem, value):
    ins.then_inc(sem, 1)
    eng.wait_ge(sem, value)


class Own:

    def __init__(self, eng, sem):
        self.eng, self.sem, self.n = eng, sem, 0

    def fence(self, ins):
        self.n += 1
        fence(self.eng, ins, self.sem, self.n)


def wait(eng, sem, value):
    if isinstance(value, int) and value <= 0:
        return
    eng.wait_ge(sem, value)


class Core:

    def __init__(self, nc, ctx):
        self.nc, self.ctx = nc, ctx

    def sb(self, name, shape, dt=F32, ctx=None):
        return (ctx or self.ctx).enter_context(self.nc.sbuf_tensor(name, shape, dt))

    def sem(self, name):
        self.sems.append(self.nc.alloc_semaphore(name=name))
        return self.sems[-1]


def phase(build):
    def run(k, *args):
        k.sems = []
        build(k, *args)
        k.nc.clear_and_free_semaphores(k.sems)
        k.nc.all_engine_barrier()
    return run


def flat(t):
    return t[:, :, :].rearrange("p a b -> p (a b)")


@phase
def load_constants(k, a):
    nc = k.nc
    k.square = k.sb("square", [P, 5 * P])
    k.eye, k.upto, k.neg = (k.square[:, n * P:(n + 1) * P] for n in range(3))
    k.iota, k.ones = (k.square[:, n * P:(n + 1) * P] for n in (3, 4))
    k.eps = k.sb("eps", [P, 1])
    nvec = 2 * DC + CONV_W * CT
    k.vecs = k.sb("vecs", [P, nvec])
    vec_rows = k.sb("vec_rows", [nvec, P])
    k.a_neg = k.sb("a_neg", [P, H])
    k.dtb = k.sb("dtb", [P, H])
    loaded, turned, made = k.sem("const_loaded"), k.sem("vecs_turned"), k.sem("const_made")
    with nc.Block() as block:
        @block.sync
        def _(sp):
            sp.dma_start(k.square[:, :], a["c_square"]).then_inc(loaded, 16)
            sp.dma_start(vec_rows[0:DC, :], a["norm_mix"][0].rearrange("(c p) -> c p", p=P)).then_inc(loaded, 16)
            sp.dma_start(vec_rows[DC:2 * DC, :], a["norm_ffn"][0].rearrange("(c p) -> c p", p=P)).then_inc(loaded, 16)
            sp.dma_start(vec_rows[2 * DC:nvec, :], a["conv_w"][0].rearrange("i (c p) -> (i c) p", p=P)).then_inc(loaded, 16)
            sp.dma_start(k.a_neg[:, :], a["a_log"].to_broadcast([P, H])).then_inc(loaded, 16)
            sp.dma_start(k.dtb[:, :], a["dt_bias"].to_broadcast([P, H])).then_inc(loaded, 16)

        @block.tensor
        def _(pe):
            pe.wait_ge(loaded, 96)
            pe.transpose(k.pb[0][:, 0:nvec], vec_rows[:, :], k.eye[0:nvec, 0:nvec]).then_inc(turned, 1)

        @block.vector
        def _(dve):
            dve.memset(k.eps[:, :], EPS).then_inc(made, 1)
            dve.wait_ge(turned, 1)
            dve.tensor_copy(k.vecs[:, :], k.pb[0][:, 0:nvec]).then_inc(made, 1)

        @block.scalar
        def _(act):
            act.wait_ge(loaded, 96)
            act.activation(k.a_neg[:, :], k.a_neg[:, :], ACT.Exp).then_inc(made, 1)


@phase
def norm_and_turn(k, name, src, load, gain, hi, lo):
    nc = k.nc
    with ExitStack() as ctx:
        junk = k.sb(name + "_junk", [P, D], F32, ctx)
        ms = k.sb(name + "_ms", [P, NT], F32, ctx)
        rstd = k.sb(name + "_rstd", [P, NT], F32, ctx)
        xn = k.sb(name + "_xn", [P, 2, D], F32, ctx)
        xg = k.sb(name + "_xg", [P, 2, DC, P], F32, ctx)
        loaded, squared, rooted = k.sem(name + "_loaded"), k.sem(name + "_squared"), k.sem(name + "_rooted")
        dve_own, scaled = k.sem(name + "_dve_own"), k.sem(name + "_scaled")
        turned, gained, hi_done = k.sem(name + "_turned"), k.sem(name + "_gained"), k.sem(name + "_hi_done")
        lo_done, cleared = k.sem(name + "_lo_done"), k.sem(name + "_cleared")
        with nc.Block() as block:
            @block.sync
            def _(sp):
                if load is not None:
                    load(sp, loaded)

            @block.scalar
            def _(act):
                act.wait_ge(cleared, 1)
                if load is not None:
                    act.wait_ge(loaded, 32)
                for t, r in enumerate(ROWS):
                    fence(act, act.activation(junk[0:r, :], src[0:r, t, :], ACT.Square, scale=D ** -0.5,
                                              accum_out=ms[0:r, t:t + 1]), squared, t + 1)
                act.activation(ms[:, :], ms[:, :], ACT.Sqrt, bias=k.eps[:, :]).then_inc(rooted, 1)
                for t, r in enumerate(ROWS):
                    act.wait_ge(gained, 2 * t + 2)
                    act.activation(hi[:, :, t * P:t * P + r], xg[:, t % 2, :, 0:r], ACT.Copy).then_inc(hi_done, 1)

            @block.vector
            def _(dve):
                dve.memset(ms[:, :], 0.0).then_inc(cleared, 1)
                dve.wait_ge(rooted, 1)
                fence(dve, dve.reciprocal(rstd[:, :], ms[:, :]), dve_own, 1)

                def scale(t):
                    r = ROWS[t]
                    if t >= 2:
                        dve.wait_ge(turned, 2 * (t - 1))
                    dve.tensor_scalar(xn[0:r, t % 2, :], src[0:r, t, :], rstd[0:r, t:t + 1], None,
                                      ALU.mult).then_inc(scaled, 1)

                scale(0)
                for t, r in enumerate(ROWS):
                    if t + 1 < NT:
                        scale(t + 1)
                    for c in range(2):
                        dve.wait_ge(turned, 2 * t + c + 1)
                        g = gain[:, 4 * c:4 * c + 4].unsqueeze(2).to_broadcast([P, 4, r])
                        src_ps = k.pb[2 * (t % 2) + c][:, :].rearrange("p (c t) -> p c t", t=P)[:, :, 0:r]
                        dve.tensor_tensor(xg[:, t % 2, 4 * c:4 * c + 4, 0:r], src_ps, g,
                                          ALU.mult).then_inc(gained, 1)
                    dve.wait_ge(gained, 2 * t + 2)
                    dve.wait_ge(hi_done, t + 1)
                    dve.tensor_tensor(lo[:, :, t * P:t * P + r], xg[:, t % 2, :, 0:r],
                                      hi[:, :, t * P:t * P + r].bitcast(F32), ALU.subtract).then_inc(lo_done, 1)
                dve.wait_ge(lo_done, NT)

            @block.tensor
            def _(pe):
                for t, r in enumerate(ROWS):
                    pe.wait_ge(scaled, t + 1)
                    if t >= 2:
                        pe.wait_ge(gained, 2 * (t - 1))
                    for c in range(DC):
                        ins = pe.transpose(k.pb[2 * (t % 2) + c // 4][:, (c % 4) * P:(c % 4) * P + r],
                                           xn[0:r, t % 2, c * P:(c + 1) * P], k.eye[0:r, 0:r])
                        if c % 4 == 3:
                            ins.then_inc(turned, 1)


class Job:

    def __init__(self, w, steps, turned, hi, lo, out, func=ACT.Copy):
        self.w, self.steps, self.turned, self.hi, self.lo, self.out, self.func = w, steps, turned, hi, lo, out, func
        self.kc = w.shape[1]
        self.results = 2 if turned else NT


@phase
def stream(k, name, jobs):
    nc = k.nc
    with ExitStack() as ctx:
        raw = [k.sb(f"{name}_raw{b}", [P, DC, WCOLS], F32, ctx) for b in range(2)]
        whi = [k.sb(f"{name}_whi{b}", [P, DC, WCOLS], F32R, ctx) for b in range(2)]
        wlo = [k.sb(f"{name}_wlo{b}", [P, DC, WCOLS], F32R, ctx) for b in range(2)]
        w_loaded = [k.sem(f"{name}_w_loaded{b}") for b in range(2)]
        w_hi_done, w_lo_done = k.sem(name + "_w_hi_done"), k.sem(name + "_w_lo_done")
        products, taken = k.sem(name + "_products"), k.sem(name + "_taken")
        FREE_RAW, FREE_PS, FREE_W = 2, 2, 2 * NT

        def plan():
            chunk0, result0, before = 0, FREE_W, 2
            for job in jobs:
                yield job, chunk0, result0, min(before, job.results)
                chunk0, result0, before = chunk0 + 2 * job.steps, result0 + 2 * job.steps * job.results, job.results

        def w_free(eng, job, result0, least, i, b):
            if b == 0:
                eng.wait_ge(products, result0 + 2 * job.results * i - least)
            else:
                eng.wait_ge(products, result0 + 2 * job.results * i)

        with nc.Block() as block:
            @block.sync
            def _(sp):
                for job, chunk0, _r, _l in plan():
                    with sp.Fori(0, job.steps) as i:
                        for b in range(2):
                            sp.wait_ge(w_lo_done, chunk0 + 2 * i + b + 1)
                            sp.dma_start(raw[b][:, 0:job.kc, :],
                                         job.w[:, :, ds((2 * i + b) * WCOLS, WCOLS)]).then_inc(w_loaded[b], 16)

            @block.scalar
            def _(act):
                def split(job, chunk0, result0, least, i, b):
                    act.wait_ge(w_loaded[b], 16 * (i + chunk0 // 2 + 1))
                    w_free(act, job, result0, least, i, b)
                    act.activation(whi[b][:, 0:job.kc, :], raw[b][:, 0:job.kc, :], ACT.Copy).then_inc(w_hi_done, 1)

                def step(here, i, after):
                    job, chunk0, result0, least = here
                    for b in range(2):
                        for n in range(job.results):
                            q = b * job.results + n
                            if n == job.results // 2:
                                if b == 0:
                                    split(*here, i, 1)
                                elif after is not None:
                                    split(*after)
                            act.wait_ge(products, result0 + 2 * job.results * i + q + 1)
                            ps = k.pv[q % 2]
                            if job.turned:
                                act.activation(job.out(i, q), ps[:, :, 0:HALF], job.func).then_inc(taken, 1)
                            else:
                                act.activation(job.out(i, b, n), ps[0:ROWS[n], 0, 0:WCOLS], job.func).then_inc(taken, 1)

                plans = list(plan())
                split(*plans[0], 0, 0)
                for n, here in enumerate(plans):
                    last = here[0].steps - 1
                    if last:
                        with act.Fori(0, last) as i:
                            step(here, i, (*here, i + 1, 0))
                    step(here, last, (*plans[n + 1], 0, 0) if n + 1 < len(plans) else None)

            @block.vector
            def _(dve):
                dve.sem_inc(w_lo_done, FREE_RAW)
                for job, chunk0, result0, least in plan():
                    with dve.Fori(0, job.steps) as i:
                        for b in range(2):
                            dve.wait_ge(w_hi_done, chunk0 + 2 * i + b + 1)
                            w_free(dve, job, result0, least, i, b)
                            dve.tensor_tensor(wlo[b][:, 0:job.kc, :], raw[b][:, 0:job.kc, :],
                                              whi[b][:, 0:job.kc, :].bitcast(F32), ALU.subtract).then_inc(w_lo_done, 1)

            @block.gpsimd
            def _(pool):
                pool.sem_inc(taken, FREE_PS)
                pool.sem_inc(products, FREE_W)

            @block.tensor
            def _(pe):
                for job, chunk0, result0, least in plan():
                    with pe.Fori(0, job.steps) as i:
                        for b in range(2):
                            pe.wait_ge(w_lo_done, FREE_RAW + chunk0 + 2 * i + b + 1)
                            for n in range(job.results):
                                q = b * job.results + n
                                pe.wait_ge(taken, result0 - FREE_W + 2 * job.results * i + q + 1)
                                ps = k.pv[q % 2]
                                if job.turned:
                                    for h in range(2):
                                        ins = mm3(pe, ps[:, h, 0:HALF], job.kc,
                                                  lambda x, c: x[:, c, n * P:(n + 1) * P], whi[b], wlo[b],
                                                  lambda x, c: x[:, c, h * HALF:(h + 1) * HALF], job.hi, job.lo)
                                else:
                                    r = ROWS[n]
                                    ins = mm3(pe, ps[0:r, 0, 0:WCOLS], job.kc,
                                              lambda x, c: x[:, c, n * P:n * P + r], job.hi, job.lo,
                                              lambda x, c: x[:, c, :], whi[b], wlo[b])
                                ins.then_inc(products, 1)


def mm3(pe, out, kc, left, lhi, llo, right, rhi, rlo):
    for c in range(kc):
        pe.matmul(out, left(llo, c), right(rhi, c), start=(c == 0), stop=False)
        pe.matmul(out, left(lhi, c), right(rlo, c), start=False, stop=False)
        ins = pe.matmul(out, left(lhi, c), right(rhi, c), start=False, stop=(c == kc - 1))
    return ins


def columns(w, c0, n):
    return w.rearrange("(c p) n -> p c n", p=P)[:, :, c0:c0 + n]


def to_channels(dst, stride, off=0):
    d = dst[:, :, :].rearrange("p c t -> p (c t)")
    return lambda i, q: d[:, ds((4 * i + q) * stride + off, T)].rearrange("p (h t) -> p h t", h=2)


def to_tokens(dst, width):
    d = dst[:, :, :].rearrange("p t c -> p (t c)")
    return lambda i, b, n: d[0:ROWS[n], ds((2 * i + b) * WCOLS + n * width, WCOLS)]


@phase
def small_projection(k, a, hi, lo, ba):
    nc = k.nc
    n = 2 * H
    with ExitStack() as ctx:
        w = k.sb("ba_w", [P, DC, n], F32, ctx)
        whi = k.sb("ba_whi", [P, DC, n], F32R, ctx)
        wlo = k.sb("ba_wlo", [P, DC, n], F32R, ctx)
        loaded, split, product, copied = k.sem("ba_loaded"), k.sem("ba_split"), k.sem("ba_product"), k.sem("ba_copied")
        with nc.Block() as block:
            @block.sync
            def _(sp):
                sp.dma_start(w[:, :, :], columns(a["w_in"][0], COL_BA, n)).then_inc(loaded, 16)

            @block.vector
            def _(dve):
                dve.wait_ge(loaded, 16)
                fence(dve, dve.tensor_copy(whi[:, :, :], w[:, :, :]), split, 1)
                dve.tensor_tensor(wlo[:, :, :], w[:, :, :], whi[:, :, :].bitcast(F32), ALU.subtract).then_inc(split, 1)
                dve.wait_ge(product, 1)
                dve.tensor_copy(ba[:, 0:4, :], k.pb[0][:, 0:4 * n].rearrange("p (t c) -> p t c", c=n)).then_inc(copied, 1)
                dve.tensor_copy(ba[0:NS, 4, :], k.pb[1][0:NS, 0:n]).then_inc(copied, 1)
                dve.wait_ge(copied, 2)

            @block.tensor
            def _(pe):
                pe.wait_ge(split, 2)
                for t, r in enumerate(ROWS):
                    out = k.pb[0][:, t * n:(t + 1) * n] if t < 4 else k.pb[1][0:r, 0:n]
                    ins = mm3(pe, out, DC, lambda x, c: x[:, c, t * P:t * P + r], hi, lo,
                              lambda x, c: x[:, c, :], whi, wlo)
                ins.then_inc(product, 1)


@phase
def convolve(k, a, o, pre, k_tok, v_tok):
    nc = k.nc
    conv_w = k.vecs[:, 2 * DC:].rearrange("p (i c) -> p i c", c=CT)
    n_st = NS * PAD
    with ExitStack() as ctx:
        st = k.sb("conv_st", [n_st, CONV_CH], F32, ctx)
        stt = k.sb("conv_stt", [P, CT, NS, PAD], F32, ctx)
        taps = k.sb("conv_taps", [P, 2, NP_TOK], F32, ctx)
        samp = k.sb("conv_samp", [P, CT, NS], F32, ctx)
        part = k.sb("conv_part", [P, CT, NS], F32, ctx)
        sq = k.sb("l2_sq", [P, 2, T], F32, ctx)
        rn = k.sb("l2_rn", [P, 2, T], F32, ctx)
        last = k.sb("conv_last", [PAD + NS, CONV_CH], F32, ctx)
        loaded, st_turned, dve_own = k.sem("conv_loaded"), k.sem("conv_st_turned"), k.sem("conv_dve_own")
        conv_done, silu_done = k.sem("conv_done"), k.sem("silu_done")
        squared, summed, rooted = k.sem("l2_squared"), k.sem("l2_summed"), k.sem("l2_rooted")
        normed, tails = k.sem("l2_normed"), k.sem("conv_tails")
        tails_copied, stored = k.sem("conv_tails_copied"), k.sem("conv_stored")
        turned, copied = k.sem("kv_turned"), k.sem("kv_copied")

        with nc.Block() as block:
            @block.sync
            def _(sp):
                sp.dma_start(st[:, :], a["state_conv_a"][0].rearrange("b i c -> (b i) c")).then_inc(loaded, 16)
                sp.dma_start(o["conv_s"][0, :, 0:PAD - 1, :], a["state_conv_a"][0, :, 1:PAD, :]).then_inc(stored, 16)
                sp.wait_ge(tails_copied, 1)
                sp.dma_start(o["conv_p"][0, 0], last[0:PAD, :]).then_inc(stored, 16)
                sp.dma_start(o["conv_s"][0, :, PAD - 1, :], last[PAD:PAD + NS, :]).then_inc(stored, 16)
                sp.wait_ge(stored, 48)

            @block.tensor
            def _(pe):
                pe.wait_ge(loaded, 16)
                for c in range(CT):
                    ins = pe.transpose(k.pb[0][:, c * n_st:(c + 1) * n_st], st[:, c * P:(c + 1) * P],
                                       k.eye[0:n_st, 0:n_st])
                ins.then_inc(st_turned, 1)
                for c in range(CT):
                    ins = pe.transpose(k.pb[1 + c // 4][0:PAD + NS, (c % 4) * P:(c % 4 + 1) * P],
                                       pre[:, c, NP_TOK:NP_TOK + PAD + NS], k.eye[:, :])
                ins.then_inc(tails, 1)
                for n in range(2 * H):
                    pe.wait_ge(squared, n + 1)
                    if n >= 2:
                        pe.wait_ge(rooted, n - 1)
                    for h in range(2):
                        ins = pe.matmul(k.pv[2 + n % 2][:, h, 0:HALF], k.ones[:, :],
                                        sq[:, n % 2, h * HALF:(h + 1) * HALF], start=True, stop=True)
                    ins.then_inc(summed, 1)
                pe.wait_ge(silu_done, CT + 1)
                pe.wait_ge(normed, 2 * H)
                for q in range(2 * NT):
                    t, r, ch = q // 2, ROWS[q // 2], (H, 2 * H)[q % 2]
                    if q >= 2:
                        pe.wait_ge(copied, q - 1)
                    for h in range(H):
                        ins = pe.transpose(k.pb[q % 2][0:r, h * P:(h + 1) * P],
                                           pre[:, ch + h, t * P:t * P + r], k.eye[:, :])
                    ins.then_inc(turned, 1)

            def divide(dve, own, n):
                dve.wait_ge(rooted, n + 1)
                own.fence(dve.reciprocal(rn[:, n % 2, :], rn[:, n % 2, :]))
                if n < H:
                    dve.scalar_tensor_tensor(pre[:, n, 0:T], pre[:, n, 0:T], DK ** -0.5, rn[:, n % 2, :],
                                             ALU.mult, ALU.mult).then_inc(normed, 1)
                else:
                    dve.tensor_tensor(pre[:, n, 0:T], pre[:, n, 0:T], rn[:, n % 2, :], ALU.mult).then_inc(normed, 1)

            @block.vector
            def _(dve):
                own = Own(dve, dve_own)
                dve.wait_ge(st_turned, 1)
                own.fence(dve.tensor_copy(stt[:, :, :, :].rearrange("p c b i -> p (c b i)"), k.pb[0][:, 0:CT * n_st]))
                for i in range(CONV_W):
                    x = stt[:, :, :, i] if i < PAD else pre[:, :, PAD + NP_TOK:PAD + T]
                    w = conv_w[:, i, :].unsqueeze(2).to_broadcast([P, CT, NS])
                    if i == 0:
                        own.fence(dve.tensor_tensor(samp[:, :, :], x, w, ALU.mult))
                    else:
                        own.fence(dve.tensor_tensor(part[:, :, :], x, w, ALU.mult))
                        own.fence(dve.tensor_tensor(samp[:, :, :], samp[:, :, :], part[:, :, :], ALU.add))
                dve.wait_ge(tails, 1)
                for c in range(3):
                    ins = dve.tensor_copy(last[:, c * 4 * P:(c + 1) * 4 * P], k.pb[1 + c][0:PAD + NS, :])
                ins.then_inc(tails_copied, 1)
                for c in range(CT):
                    if c >= 2:
                        dve.wait_ge(silu_done, c - 1)
                    y = taps[:, c % 2, :]
                    own.fence(dve.tensor_scalar(y, pre[:, c, 0:NP_TOK], conv_w[:, 0, c:c + 1], None, ALU.mult))
                    for i in range(1, CONV_W):
                        ins = dve.scalar_tensor_tensor(y, pre[:, c, i:i + NP_TOK], conv_w[:, i, c:c + 1], y,
                                                       ALU.mult, ALU.add)
                        if i < PAD:
                            own.fence(ins)
                        else:
                            ins.then_inc(conv_done, 1)
                dve.wait_ge(silu_done, CT + 1)
                for n in range(2 * H):
                    if n >= 2:
                        dve.wait_ge(summed, n - 1)
                    dve.tensor_tensor(sq[:, n % 2, :], pre[:, n, 0:T], pre[:, n, 0:T], ALU.mult).then_inc(squared, 1)
                    if n >= 1:
                        divide(dve, own, n - 1)
                divide(dve, own, 2 * H - 1)
                dve.wait_ge(normed, 2 * H)
                for q in range(2 * NT):
                    r = ROWS[q // 2]
                    dve.wait_ge(turned, q + 1)
                    dve.tensor_copy((k_tok, v_tok)[q % 2][0:r, q // 2, :], k.pb[q % 2][0:r, :]).then_inc(copied, 1)
                dve.wait_ge(copied, 2 * NT)

            @block.scalar
            def _(act):
                act.wait_ge(tails_copied, 1)
                for c in range(CT):
                    act.wait_ge(conv_done, c + 1)
                    act.activation(pre[:, c, 0:NP_TOK], taps[:, c % 2, :], ACT.Silu).then_inc(silu_done, 1)
                act.wait_ge(silu_done, CT)
                act.activation(pre[:, :, NP_TOK:T], samp[:, :, :], ACT.Silu).then_inc(silu_done, 1)
                for n in range(2 * H):
                    act.wait_ge(summed, n + 1)
                    if n >= 2:
                        act.wait_ge(normed, n - 1)
                    act.activation(rn[:, n % 2, :].rearrange("p (h t) -> p h t", h=2),
                                   k.pv[2 + n % 2][:, :, 0:HALF], ACT.Sqrt, bias=k.eps[:, :]).then_inc(rooted, 1)


@phase
def decays(k, ba, beta, logd):
    nc = k.nc
    with ExitStack() as ctx:
        z = k.sb("dec_z", [P, NT, H], F32, ctx)
        m = k.sb("dec_m", [P, NT, H], F32, ctx)
        dve_own, act_own, z_done, ln_done = (k.sem("dec_" + n) for n in ("dve_own", "act_own", "z_done", "ln_done"))
        bc = lambda v, r, n: v[0:r, :].unsqueeze(1).to_broadcast([r, n, H])
        parts = [(P, slice(0, 4)), (NS, slice(4, 5))]
        with nc.Block() as block:
            @block.vector
            def _(dve):
                own = Own(dve, dve_own)
                for r, ts in parts:
                    n = ts.stop - ts.start
                    own.fence(dve.tensor_tensor(z[0:r, ts, :], ba[0:r, ts, H:2 * H], bc(k.dtb, r, n), ALU.add))
                    own.fence(dve.tensor_scalar(m[0:r, ts, :], z[0:r, ts, :], -1.0, None, ALU.mult))
                    own.fence(dve.tensor_tensor(m[0:r, ts, :], m[0:r, ts, :], z[0:r, ts, :], ALU.min))
                    dve.tensor_scalar(z[0:r, ts, :], z[0:r, ts, :], 0.0, None, ALU.max).then_inc(z_done, 1)
                dve.wait_ge(z_done, 2)
                dve.wait_ge(ln_done, 2)
                for r, ts in parts:
                    n = ts.stop - ts.start
                    own.fence(dve.tensor_tensor(z[0:r, ts, :], z[0:r, ts, :], m[0:r, ts, :], ALU.add))
                    own.fence(dve.scalar_tensor_tensor(logd[0:r, ts, :], z[0:r, ts, :], -1.0, bc(k.a_neg, r, n),
                                                       ALU.mult, ALU.mult))

            @block.scalar
            def _(act):
                own = Own(act, act_own)
                act.wait_ge(z_done, 2)
                for r, ts in parts:
                    act.activation(beta[0:r, ts, :], ba[0:r, ts, 0:H], ACT.Sigmoid)
                for r, ts in parts:
                    own.fence(act.activation(m[0:r, ts, :], m[0:r, ts, :], ACT.Exp))
                for r, ts in parts:
                    act.activation(m[0:r, ts, :], m[0:r, ts, :], ACT.Ln, bias=1.0).then_inc(ln_done, 1)
                act.wait_ge(ln_done, 2)


def head_bc(v, r, width):
    return v.unsqueeze(2).to_broadcast([r, v.shape[1], width])


@phase
def delta_prompt(k, a, o, pre, k_tok, v_tok, beta, logd):
    nc = k.nc
    NCH = 4
    with ExitStack() as ctx:
        masks = k.sb("masks", [P, LEVELS, P], F32, ctx)
        LT = k.sb("LT", [P, NCH, H, P], F32, ctx)
        X = k.sb("X", [P, NCH, H, P], F32, ctx)
        XT = k.sb("XT", [P, NCH, H, P], F32, ctx)
        QK = k.sb("QK", [P, NCH, H, P], F32, ctx)
        kbg = k.sb("kbg", [P, NCH, H, P], F32, ctx)
        B = k.sb("B", [P, 2, H, P], F32, ctx)
        Y = k.sb("Y", [P, 2, H, P], F32, ctx)
        dec = k.sb("dec", [P, H, P], F32, ctx)
        eg = k.sb("eg", [P, H, P], F32, ctx)
        G = k.sb("G", [P, NCH, H], F32, ctx)
        bg = k.sb("bg", [P, NCH, H], F32, ctx)
        kdg = k.sb("kdg", [P, NCH, H], F32, ctx)
        gC = k.sb("gC", [P, NCH, H], F32, ctx)
        S = k.sb("S_delta", [P, H, P], F32, ctx)
        vn = k.sb("vn", [P, H, P], F32, ctx)
        loaded, dve_own, act_own = k.sem("dp_loaded"), k.sem("dp_dve_own"), k.sem("dp_act_own")
        g_sum, g_copied, prep, dec_in, dec_out, prep_done = (k.sem("dp_" + n) for n in
            ("g_sum", "g_copied", "prep", "dec_in", "dec_out", "prep_done"))
        b_done, y_mm, y_done, z_mm, x_done, uw_mm, uw_done = (k.sem("dp_" + n) for n in
            ("b_done", "y_mm", "y_done", "z_mm", "x_done", "uw_mm", "uw_done"))
        ws_mm, vn_done, os_mm, s_done, o_done, stored, scaled = (k.sem("dp_" + n) for n in
            ("ws_mm", "vn_done", "os_mm", "s_done", "o_done", "stored", "scaled"))
        kd_done = k.sem("dp_kd_done")
        bank = lambda n: k.pb[n].rearrange("p (h t) -> p h t", h=H)
        tok = lambda x, t: x[:, t, :].rearrange("p (h e) -> p h e", h=H)
        with nc.Block() as block:
            @block.sync
            def _(sp):
                sp.dma_start(masks[:, :, :], a["c_masks"].rearrange("p (l t) -> p l t", l=LEVELS)).then_inc(loaded, 16)
                sp.wait_ge(s_done, NCH)
                sp.dma_start(o["delta_p"][0, 0].rearrange("h k v -> k h v"), S[:, :, :]).then_inc(stored, 16)
                sp.wait_ge(stored, 16)

            @block.tensor
            def _(pe):
                for t in range(NCH):
                    ins = pe.matmul(k.pb[7][:, t * H:(t + 1) * H], k.upto, logd[:, t, :], start=True, stop=True)
                ins.then_inc(g_sum, 1)
                for t in range(NCH):
                    if t >= 1:
                        pe.wait_ge(prep_done, t)
                    if t == 0:
                        pe.wait_ge(g_copied, 1)
                    c = slice(t * P, (t + 1) * P)
                    for h in range(H):
                        hs = slice(h * P, (h + 1) * P)
                        kc = pre[:, H + h, c]
                        pe.matmul(k.pb[0][:, hs], logd[:, t, h:h + 1].to_broadcast([P, P]), k.upto, start=True, stop=True)
                        pe.matmul(k.pb[1][:, hs], beta[:, t, h:h + 1].to_broadcast([P, P]), k.eye, start=True, stop=True)
                        pe.matmul(k.pb[2][:, hs], kc, kc, start=True, stop=True)
                        ins = pe.matmul(k.pb[3][:, hs], kc, pre[:, h, c], start=True, stop=True)
                    ins.then_inc(prep, 1)
                pe.wait_ge(prep_done, NCH)
                n = 0
                for l in range(LEVELS):
                    for t in range(NCH):
                        if l == 0:
                            if n >= 2:
                                pe.wait_ge(x_done, n - 1)
                            pe.wait_ge(b_done, n + 1)
                            for h in range(H):
                                ins = pe.matmul(bank(1 + 2 * (n % 2))[:, h, :], B[:, n % 2, h, :], k.eye,
                                                start=True, stop=True)
                            ins.then_inc(z_mm, 1)
                        else:
                            pe.wait_ge(b_done, n + 1)
                            pe.wait_ge(x_done, n - NCH + 1)
                            if n - NCH >= 2:
                                pe.wait_ge(y_done, n - NCH - 1)
                            for h in range(H):
                                ins = pe.matmul(bank(4 + n % 2)[:, h, :], B[:, n % 2, h, :], X[:, t, h, :],
                                                start=True, stop=True)
                            ins.then_inc(y_mm, 1)
                            pe.wait_ge(y_done, n - NCH + 1)
                            pe.wait_ge(x_done, n - 1)
                            for h in range(H):
                                pe.matmul(bank(2 * (n % 2))[:, h, :], Y[:, n % 2, h, :], XT[:, t, h, :],
                                          start=True, stop=True)
                                ins = pe.matmul(bank(1 + 2 * (n % 2))[:, h, :], XT[:, t, h, :], Y[:, n % 2, h, :], start=True, stop=True)
                            ins.then_inc(z_mm, 1)
                        n += 1
                pe.wait_ge(x_done, n)
                pe.wait_ge(scaled, NCH)
                for t in range(NCH):
                    if t >= 1:
                        pe.wait_ge(uw_done, 2 * t)
                    for h in range(H):
                        pe.matmul(bank(2)[:, h, :], XT[:, t, h, :], tok(v_tok, t)[:, h, :], start=True, stop=True)
                        ins = pe.matmul(bank(3)[:, h, :], kbg[:, t, h, :], XT[:, t, h, :], start=True, stop=True)
                    ins.then_inc(uw_mm, 1)
                pe.wait_ge(uw_done, 2 * NCH)
                pe.wait_ge(kd_done, NCH)
                for t in range(NCH):
                    c = slice(t * P, (t + 1) * P)
                    if t:
                        pe.wait_ge(s_done, t)
                        for h in range(H):
                            ins = pe.matmul(bank(4)[:, h, :], LT[:, t, h, :], S[:, h, :], start=True, stop=True)
                        ins.then_inc(ws_mm, 1)
                        pe.wait_ge(vn_done, t)
                        pe.wait_ge(o_done, t)
                    v = lambda h: vn[:, h, :] if t else X[:, 0, h, :]
                    for h in range(H):
                        if t:
                            pe.matmul(bank(5)[:, h, :], pre[:, h, c], S[:, h, :], start=True, stop=False)
                        pe.matmul(bank(5)[:, h, :], QK[:, t, h, :], v(h), start=not t, stop=True)
                        ins = pe.matmul(bank(6)[:, h, :], tok(k_tok, t)[:, h, :], v(h), start=True, stop=True)
                    ins.then_inc(os_mm, 1)

            @block.scalar
            def _(act):
                own = Own(act, act_own)
                act.wait_ge(g_copied, 1)
                act.activation(bg[:, :, :], G[:, :, :], ACT.Exp).then_inc(dec_out, 1)
                for t in range(NCH):
                    act.wait_ge(prep, t + 1)
                    if t >= 1:
                        act.wait_ge(prep_done, t)
                    act.activation(eg[:, :, :], bank(0), ACT.Exp).then_inc(dec_out, 1)
                    act.wait_ge(dec_in, t + 1)
                    act.activation(dec[:, :, :], dec[:, :, :], ACT.Exp).then_inc(dec_out, 1)
                act.wait_ge(prep_done, NCH)
                act.activation(kdg[:, :, :], kdg[:, :, :], ACT.Exp).then_inc(dec_out, 1)
                n = 0
                for l in range(1, LEVELS):
                    for t in range(NCH):
                        act.wait_ge(y_mm, n + 1)
                        if n >= 2:
                            act.wait_ge(z_mm, NCH + n - 1)
                        act.activation(Y[:, n % 2, :, :], bank(4 + n % 2), ACT.Copy).then_inc(y_done, 1)
                        n += 1
                act.wait_ge(x_done, LEVELS * NCH)
                for t in range(NCH):
                    act.wait_ge(uw_mm, t + 1)
                    act.activation(X[:, t, :, :], bank(2), ACT.Copy).then_inc(uw_done, 1)
                    act.wait_ge(uw_done, 2 * t + 1)
                    act.activation(LT[:, t, :, :], bank(3), ACT.Copy).then_inc(uw_done, 1)
                for t in range(NCH):
                    act.wait_ge(os_mm, t + 1)
                    act.activation(tok(v_tok, t), bank(5), ACT.Copy).then_inc(o_done, 1)
                act.wait_ge(o_done, NCH)

            @block.vector
            def _(dve):
                own = Own(dve, dve_own)
                dve.wait_ge(g_sum, 1)
                fence(dve, dve.tensor_copy(G[:, :, :].rearrange("p t h -> p (t h)"), k.pb[7][:, 0:NCH * H]), g_copied, 1)
                for t in range(NCH):
                    c = slice(t * P, (t + 1) * P)
                    dve.wait_ge(dec_out, 2 * t + 2)
                    dve.tensor_copy(gC[:, t, :], eg[:, :, P - 1])
                    own.fence(dve.tensor_tensor(dec[:, :, :], bank(0), head_bc(G[:, t, :], P, P), ALU.subtract))
                    dve.tensor_tensor(dec[:, :, :], dec[:, :, :], k.neg.unsqueeze(1).to_broadcast([P, H, P]),
                                      ALU.add).then_inc(dec_in, 1)
                    own.fence(dve.tensor_tensor(kdg[:, t, :], bank(0)[:, :, P - 1], G[:, t, :], ALU.subtract))
                    dve.wait_ge(dec_out, 2 * t + 3)
                    own.fence(dve.tensor_tensor(LT[:, t, :, :], bank(2), dec[:, :, :], ALU.mult))
                    own.fence(dve.tensor_tensor(LT[:, t, :, :], LT[:, t, :, :], bank(1), ALU.mult))
                    own.fence(dve.tensor_tensor(pre[:, 0:H, c], pre[:, 0:H, c], eg[:, :, :], ALU.mult))
                    fence(dve, dve.tensor_tensor(QK[:, t, :, :], bank(3), dec[:, :, :], ALU.mult), prep_done, t + 1)
                dve.wait_ge(prep_done, NCH)
                own.fence(dve.tensor_tensor(bg[:, :, :], bg[:, :, :], beta[:, 0:NCH, :], ALU.mult))
                dve.wait_ge(loaded, 16)
                n = 0
                for l in range(LEVELS):
                    def coupled(n):
                        if n >= 2:
                            dve.wait_ge(z_mm, n - 1)
                        dve.tensor_tensor(B[:, n % 2, :, :], LT[:, n % NCH, :, :],
                                          masks[:, n // NCH, :].unsqueeze(1).to_broadcast([P, H, P]),
                                          ALU.mult).then_inc(b_done, 1)
                    for t in range(NCH):
                        if n == 0:
                            coupled(0)
                        if n + 1 < LEVELS * NCH:
                            coupled(n + 1)
                        dve.wait_ge(z_mm, n + 1)
                        eye_h = k.eye.unsqueeze(1).to_broadcast([P, H, P])
                        if l == 0:
                            own.fence(dve.tensor_tensor(XT[:, t, :, :], eye_h, B[:, n % 2, :, :], ALU.subtract))
                            dve.tensor_tensor(X[:, t, :, :], eye_h, bank(1 + 2 * (n % 2)), ALU.subtract).then_inc(x_done, 1)
                        else:
                            own.fence(dve.tensor_tensor(XT[:, t, :, :], XT[:, t, :, :], bank(2 * (n % 2)), ALU.subtract))
                            dve.tensor_tensor(X[:, t, :, :], X[:, t, :, :], bank(1 + 2 * (n % 2)), ALU.subtract).then_inc(x_done, 1)
                        n += 1
                        if n == 1:
                            for u in range(NCH):
                                own.fence(dve.tensor_tensor(tok(v_tok, u), tok(v_tok, u), head_bc(beta[:, u, :], P, P), ALU.mult))
                                dve.tensor_tensor(kbg[:, u, :, :], tok(k_tok, u), head_bc(bg[:, u, :], P, P),
                                                  ALU.mult).then_inc(scaled, 1)
                            dve.wait_ge(scaled, NCH)
                dve.wait_ge(dec_out, 2 * NCH + 2)
                for u in range(NCH):
                    dve.tensor_tensor(tok(k_tok, u), tok(k_tok, u), head_bc(kdg[:, u, :], P, P),
                                      ALU.mult).then_inc(kd_done, 1)
                dve.wait_ge(uw_done, 2 * NCH)
                for t in range(NCH):
                    if t:
                        dve.wait_ge(ws_mm, t)
                        dve.tensor_tensor(vn[:, :, :], X[:, t, :, :], bank(4), ALU.subtract).then_inc(vn_done, 1)
                    dve.wait_ge(os_mm, t + 1)
                    if t:
                        own.fence(dve.tensor_tensor(S[:, :, :], S[:, :, :], head_bc(gC[:, t, :], P, P), ALU.mult))
                        dve.tensor_tensor(S[:, :, :], S[:, :, :], bank(6), ALU.add).then_inc(s_done, 1)
                    else:
                        dve.tensor_copy(S[:, :, :], bank(6)).then_inc(s_done, 1)
                    dve.wait_ge(s_done, t + 1)


@phase
def clear_pad(k, pre):
    done = k.sem("pad_done")
    with k.nc.Block() as block:
        @block.vector
        def _(dve):
            fence(dve, dve.memset(pre[:, :, 0:PAD], 0.0), done, 1)


@phase
def spill(k, name, dst, src):
    done = k.sem(name)
    with k.nc.Block() as block:
        @block.sync
        def _(sp):
            for d, s_ in zip(dst, src):
                sp.dma_start(d, s_).then_inc(done, 16)
            sp.wait_ge(done, 16 * len(dst))


@phase
def load_sample_consts(k, a, ctx):
    nc = k.nc
    n = 2 * H * P + H + NS * NS
    k.ret = k.sb("ret_tables", [P, n], F32, ctx)
    k.ret_dec = k.ret[:, 0:H * P].rearrange("p (h t) -> p h t", h=H)
    k.ret_qdec = k.ret[:, H * P:2 * H * P].rearrange("p (h t) -> p h t", h=H)
    k.ret_kdec = k.ret[:, 2 * H * P:2 * H * P + H]
    k.eye8 = k.ret[:, 2 * H * P + H:n].rearrange("p (a b) -> p a b", a=NS)
    loaded = k.sem("ret_loaded")
    with nc.Block() as block:
        @block.sync
        def _(sp):
            sp.dma_start(k.ret[:, :], a["c_ret"]).then_inc(loaded, 16)
            sp.wait_ge(loaded, 16)


@phase
def delta_sample(k, a, o, pre, v_tok, beta, logd):
    nc = k.nc
    BH = NS * H
    with ExitStack() as ctx:
        S = k.sb("S_ds", [P, NS, H, P], F32, ctx)
        bgs = k.sb("ds_bg", [NS, 2, NS, H], F32, ctx)
        bg = k.sb("ds_bgbc", [P, 2, NS, H], F32, ctx)
        eg = k.sb("ds_eg", [NS, H], F32, ctx)
        kb = k.sb("ds_kb", [P, NS, H], F32, ctx)
        qm = k.sb("ds_qm", [P, H, NS, NS], F32, ctx)
        dlt = k.sb("ds_dlt", [P, 2, H, P], F32, ctx)
        loaded, own_s, e_done, spread, sums, ready, kv, upd, dv, omm, stored, taken = (k.sem("ds_" + n) for n in
            ("loaded", "own", "e_done", "spread", "sums", "ready", "kv", "upd", "dv", "omm", "stored", "taken"))
        ch = lambda c: pre[:, c:c + H, NP_TOK:T]
        with nc.Block() as block:
            @block.sync
            def _(sp):
                sp.dma_start(S[:, :, :, :].rearrange("p b h v -> p (b h) v"),
                             a["state_delta"][0].rearrange("b h k v -> k (b h) v")).then_inc(loaded, 16)
                sp.wait_ge(upd, NS)
                sp.dma_start(o["delta_s"][0].rearrange("b h k v -> k (b h) v"),
                             S[:, :, :, :].rearrange("p b h v -> p (b h) v")).then_inc(stored, 16)
                sp.wait_ge(stored, 16)

            @block.scalar
            def _(act):
                act.activation(eg[:, :], logd[0:NS, 4, :], ACT.Exp).then_inc(e_done, 1)

            @block.vector
            def _(dve):
                own = Own(dve, own_s)
                dve.wait_ge(e_done, 1)
                for n, src in enumerate((eg[:, :], beta[0:NS, 4, :])):
                    ins = dve.tensor_tensor(bgs[:, n, :, :], src.unsqueeze(1).to_broadcast([NS, NS, H]),
                                            k.eye[0:NS, 0:NS].unsqueeze(2).to_broadcast([NS, NS, H]), ALU.mult)
                ins.then_inc(spread, 1)
                dve.wait_ge(sums, 1)
                own.fence(dve.tensor_copy(bg[:, :, :, :].rearrange("p n b h -> p (n b h)"), k.pb[0][:, 0:2 * BH]))
                own.fence(dve.tensor_tensor(kb[:, :, :], ch(H).rearrange("p h b -> p b h"), bg[:, 1, :, :], ALU.mult))
                for h in range(H):
                    own.fence(dve.tensor_tensor(qm[:, h, :, :], pre[:, h, NP_TOK:T].unsqueeze(2).to_broadcast([P, NS, NS]),
                                                k.eye8, ALU.mult))
                dve.wait_ge(loaded, 16)
                for b in range(NS):
                    dve.tensor_tensor(S[:, b, :, :], S[:, b, :, :], head_bc(bg[:, 0, b, :], P, P),
                                      ALU.mult).then_inc(ready, 1)
                for b in range(NS):
                    x = dlt[:, b % 2, :, :]
                    dve.wait_ge(kv, b + 1)
                    ks = k.pb[2 + 2 * (b % 2)].rearrange("p (h e) -> p h e", h=H)
                    vv = k.pb[3 + 2 * (b % 2)].rearrange("p (h e) -> p h e", h=H)
                    own.fence(dve.tensor_copy(x, vv))
                    fence(dve, dve.tensor_tensor(x, x, ks, ALU.subtract), dv, b + 1)
                    own.fence(dve.tensor_tensor(x, x, head_bc(kb[:, b, :], P, P), ALU.mult))
                    fence(dve, dve.tensor_tensor(S[:, b, :, :], S[:, b, :, :], x, ALU.add), upd, b + 1)
                dve.wait_ge(omm, 1)
                fence(dve, dve.tensor_copy(v_tok[0:NS, 4, :], k.pb[1][0:NS, :]), taken, 1)

            @block.tensor
            def _(pe):
                pe.wait_ge(spread, 1)
                pe.matmul(k.pb[0][:, 0:2 * BH], k.ones[0:NS, :], bgs[:, :, :, :].rearrange("p n b h -> p (n b h)"),
                          start=True, stop=True).then_inc(sums, 1)
                for b in range(NS):
                    pe.wait_ge(ready, b + 1)
                    if b >= 2:
                        pe.wait_ge(dv, b - 1)
                    for h in range(H):
                        col = pre[:, H + h, NP_TOK + b:NP_TOK + b + 1].to_broadcast([P, P])
                        pe.matmul(k.pb[2 + 2 * (b % 2)][:, h * P:(h + 1) * P], col, S[:, b, h, :], start=True, stop=True)
                    pe.matmul(k.pb[3 + 2 * (b % 2)], k.eye[0:NS, b:b + 1].to_broadcast([NS, P]), v_tok[0:NS, 4, :],
                              start=True, stop=True).then_inc(kv, 1)
                pe.wait_ge(upd, NS)
                for h in range(H):
                    for b in range(NS):
                        ins = pe.matmul(k.pb[1][0:NS, h * P:(h + 1) * P], qm[:, h, b, :], S[:, b, h, :],
                                        start=(b == 0), stop=(b == NS - 1))
                ins.then_inc(omm, 1)


@phase
def gate_and_turn(k, a, name, o_tok, gate, gn, width, hi, lo, c0):
    nc = k.nc
    W = H * width
    nb = W // 512
    with ExitStack() as ctx:
        g = k.sb(name + "_gain", [P, width], F32, ctx)
        sq = k.sb(name + "_sq", [P, W], F32, ctx)
        ss = k.sb(name + "_ss", [P, NT, H], F32, ctx)
        loaded, gained, own_s, summed, rooted, ready, turned, hi_done, lo_done = (k.sem(name + "_" + n) for n in
            ("loaded", "gained", "own", "summed", "rooted", "ready", "turned", "hi_done", "lo_done"))
        heads = lambda x, t, r: x[0:r, t, :].rearrange("p (h e) -> p h e", h=H)
        with nc.Block() as block:
            @block.sync
            def _(sp):
                sp.dma_start(g[:, :], gn.to_broadcast([P, width])).then_inc(loaded, 16)

            @block.gpsimd
            def _(pool):
                pool.wait_ge(loaded, 16)
                for t, r in enumerate(ROWS):
                    pool.tensor_tensor(heads(gate, t, r), heads(gate, t, r),
                                       g[0:r, :].unsqueeze(1).to_broadcast([r, H, width]), ALU.mult).then_inc(gained, 1)

            @block.vector
            def _(dve):
                own = Own(dve, own_s)
                own.fence(dve.memset(ss[:, :, :], 1.0))
                for t, r in enumerate(ROWS):
                    own.fence(dve.tensor_tensor(sq[0:r, :], o_tok[0:r, t, :], o_tok[0:r, t, :], ALU.mult))
                    own.fence(dve.tensor_reduce(ss[0:r, t, :], sq[0:r, :].rearrange("p (h e) -> p h e", h=H), AX.X, ALU.add))
                dve.sem_inc(summed, 1)
                dve.wait_ge(rooted, 1)
                own.fence(dve.reciprocal(ss[:, :, :], ss[:, :, :]))
                for t, r in enumerate(ROWS):
                    own.fence(dve.tensor_tensor(heads(o_tok, t, r), heads(o_tok, t, r), head_bc(ss[0:r, t, :], r, width), ALU.mult))
                    dve.wait_ge(gained, t + 1)
                    dve.tensor_tensor(o_tok[0:r, t, :], o_tok[0:r, t, :], gate[0:r, t, :], ALU.mult).then_inc(ready, 1)
                q = 0
                for t, r in enumerate(ROWS):
                    for c in range(nb):
                        dve.wait_ge(hi_done, q + 1)
                        cc = slice(c0 + 4 * c, c0 + 4 * c + 4)
                        ps = k.pb[q % 4].rearrange("p (c t) -> p c t", c=4)[:, :, 0:r]
                        dve.tensor_tensor(lo[:, cc, t * P:t * P + r], ps, hi[:, cc, t * P:t * P + r].bitcast(F32),
                                          ALU.subtract).then_inc(lo_done, 1)
                        q += 1
                dve.wait_ge(lo_done, q)

            @block.scalar
            def _(act):
                act.wait_ge(summed, 1)
                act.activation(ss[:, :, :], ss[:, :, :], ACT.Sqrt, scale=1.0 / width, bias=k.eps[:, :]).then_inc(rooted, 1)
                q = 0
                for t, r in enumerate(ROWS):
                    for c in range(nb):
                        act.wait_ge(turned, q + 1)
                        cc = slice(c0 + 4 * c, c0 + 4 * c + 4)
                        act.activation(hi[:, cc, t * P:t * P + r], k.pb[q % 4].rearrange("p (c t) -> p c t", c=4)[:, :, 0:r],
                                       ACT.Copy).then_inc(hi_done, 1)
                        q += 1

            @block.tensor
            def _(pe):
                q = 0
                for t, r in enumerate(ROWS):
                    pe.wait_ge(ready, t + 1)
                    for c in range(nb):
                        if q >= 4:
                            pe.wait_ge(lo_done, q - 3)
                        for n in range(4):
                            ins = pe.transpose(k.pb[q % 4][:, n * P:n * P + r],
                                               o_tok[0:r, t, (4 * c + n) * P:(4 * c + n + 1) * P], k.eye[0:r, 0:r])
                        ins.then_inc(turned, 1)
                        q += 1


@phase
def rotate(k, a, qk_b, kb_tok):
    nc = k.nc
    with ExitStack() as ctx:
        rope = k.sb("rope", [P, 2, T], F32, ctx)
        rot = k.sb("rope_rot", [P, 2, T], F32, ctx)
        loaded, own_s, roped, turned, copied = (k.sem("rope_" + n) for n in ("loaded", "own", "roped", "turned", "copied"))
        with nc.Block() as block:
            @block.sync
            def _(sp):
                sp.dma_start(rope[:, :, :], a["c_rope"].rearrange("p (n t) -> p n t", n=2)).then_inc(loaded, 16)

            @block.vector
            def _(dve):
                own = Own(dve, own_s)
                hh = P // 2
                dve.wait_ge(loaded, 16)
                for n in range(2 * H):
                    x, sc = qk_b[:, n, :], (1.0 if n < H else DK ** -0.5)
                    dve.scalar_tensor_tensor(rot[hh:P, 0, :], qk_b[0:hh, n, :], sc, rope[0:hh, 1, :], ALU.mult, ALU.mult)
                    dve.scalar_tensor_tensor(rot[0:hh, 0, :], qk_b[hh:P, n, :], sc, rope[hh:P, 1, :], ALU.mult, ALU.mult)
                    own.fence(dve.scalar_tensor_tensor(rot[:, 1, :], x, sc, rope[:, 0, :], ALU.mult, ALU.mult))
                    fence(dve, dve.tensor_tensor(x, rot[:, 1, :], rot[:, 0, :], ALU.add), roped, n + 1)
                for t in range(4):
                    dve.wait_ge(turned, t + 1)
                    dve.tensor_tensor(kb_tok[:, t, :].rearrange("p (h d) -> p h d", h=H),
                                      k.pb[t % 2].rearrange("p (h d) -> p h d", h=H), head_bc(k.ret_kdec, P, P),
                                      ALU.mult).then_inc(copied, 1)
                dve.wait_ge(copied, 4)

            @block.tensor
            def _(pe):
                pe.wait_ge(roped, 2 * H)
                for t in range(4):
                    if t >= 2:
                        pe.wait_ge(copied, t - 1)
                    for h in range(H):
                        ins = pe.transpose(k.pb[t % 2][:, h * P:(h + 1) * P], qk_b[:, H + h, t * P:(t + 1) * P], k.eye)
                    ins.then_inc(turned, 1)


@phase
def retention_prompt(k, a, o, qk_b, v_b, kb_tok):
    nc = k.nc
    NCH = 4
    with ExitStack() as ctx:
        A = k.sb("rp_A", [P, 2, H, P], F32, ctx)
        qd = k.sb("rp_qd", [P, 2, H, P], F32, ctx)
        S = k.sb("rp_S", [P, H, DV_B], F32, ctx)
        qk_mm, a_done, own_s, os_mm, s_done, o_done, stored = (k.sem("rp_" + n) for n in
            ("qk_mm", "a_done", "own", "os_mm", "s_done", "o_done", "stored"))
        v = lambda t, h: v_b[:, t, h * DV_B:(h + 1) * DV_B]
        with nc.Block() as block:
            @block.sync
            def _(sp):
                sp.wait_ge(s_done, NCH)
                sp.dma_start(o["ret_p"][0, 0].rearrange("h k v -> k h v"), S[:, :, :]).then_inc(stored, 16)
                sp.wait_ge(stored, 16)

            @block.tensor
            def _(pe):
                def scores(t):
                    if t >= 2:
                        pe.wait_ge(a_done, t - 1)
                    for h in range(H):
                        c = slice(t * P, (t + 1) * P)
                        ins = pe.matmul(k.pb[t % 2][:, h * P:(h + 1) * P], qk_b[:, H + h, c], qk_b[:, h, c], start=True, stop=True)
                    ins.then_inc(qk_mm, 1)

                scores(0)
                for t in range(NCH):
                    if t + 1 < NCH:
                        scores(t + 1)
                    pe.wait_ge(a_done, t + 1)
                    if t:
                        pe.wait_ge(s_done, t)
                        pe.wait_ge(o_done, t)
                    for h in range(H):
                        po = k.pb[4 + h // 2][:, (h % 2) * DV_B:(h % 2 + 1) * DV_B]
                        ps = k.pb[6 + h // 2][:, (h % 2) * DV_B:(h % 2 + 1) * DV_B]
                        if t:
                            pe.matmul(po, qd[:, t % 2, h, :], S[:, h, :], start=True, stop=False)
                        pe.matmul(po, A[:, t % 2, h, :], v(t, h), start=not t, stop=True)
                        ins = pe.matmul(ps, kb_tok[:, t, h * P:(h + 1) * P], v(t, h), start=True, stop=True)
                    ins.then_inc(os_mm, 1)

            @block.vector
            def _(dve):
                own = Own(dve, own_s)
                gC = gammas() ** P

                def prep(t):
                    if t >= 2:
                        dve.wait_ge(os_mm, t - 1)
                    dve.tensor_tensor(qd[:, t % 2, :, :], qk_b[:, 0:H, t * P:(t + 1) * P], k.ret_qdec, ALU.mult)
                    dve.wait_ge(qk_mm, t + 1)
                    dve.tensor_tensor(A[:, t % 2, :, :], k.pb[t % 2].rearrange("p (h i) -> p h i", h=H), k.ret_dec,
                                      ALU.mult).then_inc(a_done, 1)

                prep(0)
                for t in range(NCH):
                    if t + 1 < NCH:
                        prep(t + 1)
                    dve.wait_ge(os_mm, t + 1)
                    for h in range(H):
                        ps = k.pb[6 + h // 2][:, (h % 2) * DV_B:(h % 2 + 1) * DV_B]
                        if t:
                            ins = dve.scalar_tensor_tensor(S[:, h, :], S[:, h, :], float(gC[h]), ps, ALU.mult, ALU.add)
                        else:
                            ins = dve.tensor_copy(S[:, h, :], ps)
                    fence(dve, ins, s_done, t + 1)

            @block.scalar
            def _(act):
                for t in range(NCH):
                    act.wait_ge(os_mm, t + 1)
                    act.activation(v_b[:, t, :].rearrange("p (n e) -> p n e", n=2), k.pv[2][:, :, :], ACT.Copy).then_inc(o_done, 1)
                act.wait_ge(o_done, NCH)


@phase
def retention_sample(k, a, o, qk_b, v_b):
    nc = k.nc
    with ExitStack() as ctx:
        S = k.sb("S_rs", [P, NS, H, DV_B], F32, ctx)
        qm = k.sb("rs_qm", [P, H, NS, NS], F32, ctx)
        x = k.sb("rs_x", [P, 2, H, DV_B], F32, ctx)
        loaded, own_s, vv, upd, xd, omm, stored, taken = (k.sem("rs_" + n) for n in
            ("loaded", "own", "vv", "upd", "xd", "omm", "stored", "taken"))
        with nc.Block() as block:
            @block.sync
            def _(sp):
                sp.dma_start(S[:, :, :, :].rearrange("p b h v -> p (b h) v"),
                             a["state_ret"][0].rearrange("b h k v -> k (b h) v")).then_inc(loaded, 16)
                sp.wait_ge(upd, NS)
                sp.dma_start(o["ret_s"][0].rearrange("b h k v -> k (b h) v"),
                             S[:, :, :, :].rearrange("p b h v -> p (b h) v")).then_inc(stored, 16)
                sp.wait_ge(stored, 16)

            @block.vector
            def _(dve):
                own = Own(dve, own_s)
                gm = gammas()
                for h in range(H):
                    own.fence(dve.tensor_tensor(qm[:, h, :, :], qk_b[:, h, NP_TOK:T].unsqueeze(2).to_broadcast([P, NS, NS]),
                                                k.eye8, ALU.mult))
                dve.wait_ge(loaded, 16)
                for h in range(H):
                    ins = dve.tensor_scalar(S[:, :, h, :], S[:, :, h, :], float(gm[h]), None, ALU.mult)
                own.fence(ins)
                for b in range(NS):
                    dve.wait_ge(vv, b + 1)
                    for n in range(2):
                        kc = head_bc(qk_b[:, H + 2 * n:H + 2 * n + 2, NP_TOK + b], P, DV_B)
                        ins = dve.tensor_tensor(x[:, b % 2, 2 * n:2 * n + 2, :],
                                                k.pv[b % 2][:, n, :].rearrange("p (h e) -> p h e", h=2), kc, ALU.mult)
                    fence(dve, ins, xd, b + 1)
                    fence(dve, dve.tensor_tensor(S[:, b, :, :], S[:, b, :, :], x[:, b % 2, :, :], ALU.add), upd, b + 1)
                dve.wait_ge(omm, 1)
                fence(dve, dve.tensor_copy(v_b[0:NS, 4, :].rearrange("p (n e) -> p n e", n=2), k.pv[2][0:NS, :, :]), taken, 1)

            @block.tensor
            def _(pe):
                for b in range(NS):
                    if b >= 2:
                        pe.wait_ge(xd, b - 1)
                    for n in range(2):
                        ins = pe.matmul(k.pv[b % 2][:, n, :], k.eye[0:NS, b:b + 1].to_broadcast([NS, P]),
                                        v_b[0:NS, 4, n * 512:(n + 1) * 512], start=True, stop=True)
                    ins.then_inc(vv, 1)
                pe.wait_ge(upd, NS)
                for h in range(H):
                    for b in range(NS):
                        ins = pe.matmul(k.pv[2][0:NS, h // 2, (h % 2) * DV_B:(h % 2 + 1) * DV_B], qm[:, h, b, :],
                                        S[:, b, h, :], start=(b == 0), stop=(b == NS - 1))
                ins.then_inc(omm, 1)


@phase
def merge(k, sa, sb_, ba_, bb, hi, lo):
    nc = k.nc
    own_s, hi_s, own_p = k.sem("mg_own"), k.sem("mg_hi"), k.sem("mg_pool")
    with nc.Block() as block:
        @block.vector
        def _(dve):
            own = Own(dve, own_s)
            for c in range(DC):
                own.fence(dve.tensor_tensor(sa[:, c, :], sa[:, c, :], ba_[:, c, :], ALU.mult))
                dve.wait_ge(own_p, c + 1)
                own.fence(dve.tensor_tensor(sa[:, c, :], sa[:, c, :], sb_[:, c, :], ALU.add))
                own.fence(dve.tensor_copy(hi[:, c, :], sa[:, c, :]))
                own.fence(dve.tensor_tensor(lo[:, c, :], sa[:, c, :], hi[:, c, :].bitcast(F32), ALU.subtract))

        @block.gpsimd
        def _(pool):
            for c in range(DC):
                pool.tensor_tensor(sb_[:, c, :], sb_[:, c, :], bb[:, c, :], ALU.mult).then_inc(own_p, 1)


def load_tokens(a, dst):
    def go(sp, loaded):
        sp.dma_start(dst[:, 0:4, :], a["x_prompt"][0].rearrange("(t p) d -> p t d", p=P)).then_inc(loaded, 16)
        sp.dma_start(dst[0:NS, 4, :], a["x_sample"][:, 0, :]).then_inc(loaded, 16)
    return go


@phase
def add_tokens(k, a, h_tok):
    nc = k.nc
    with ExitStack() as ctx:
        x = k.sb("res_x", [P, NT, D], F32, ctx)
        loaded, done = k.sem("res_loaded"), k.sem("res_done")
        with nc.Block() as block:
            @block.sync
            def _(sp):
                load_tokens(a, x)(sp, loaded)

            @block.vector
            def _(dve):
                dve.wait_ge(loaded, 32)
                for t, r in enumerate(ROWS):
                    dve.tensor_tensor(h_tok[0:r, t, :], h_tok[0:r, t, :], x[0:r, t, :], ALU.add).then_inc(done, 1)
                dve.wait_ge(done, NT)


@phase
def retrieve(k, a, q, gi, gj, gate_hi, gate_lo):
    nc = k.nc
    HK = PH * TOPK
    with ExitStack() as ctx:
        keys = k.sb("keys", [P, HP, NK], F32, ctx)
        keysT = k.sb("keysT", [P, HP, NK], F32, ctx)
        s = k.sb("scores", [P, 2, HP, NK], F32, ctx)
        top = k.sb("top", [P, HP, TOPK], F32, ctx)
        top_i = k.sb("top_i", [P, HP, TOPK], U32, ctx)
        top_f = k.sb("top_f", [P, HP, TOPK], F32, ctx)
        cand = k.sb("cand", [P, PH, TOPK, TOPK], F32, ctx)
        best = k.sb("best", [P, PH, TOPK], F32, ctx)
        sel = k.sb("sel", [P, PH, TOPK], U32, ctx)
        pick = k.sb("pick", [P, 2, HK], U32, ctx)
        pick_f = k.sb("pick_f", [P, 2, HK], F32, ctx)
        hot = k.sb("hot", [P, PH, TOPK, TOPK], F32, ctx)
        res = k.sb("res", [P, 3, HK], F32, ctx)
        tot = k.sb("tot", [P, PH], F32, ctx)
        gate = k.sb("gate", [P, T], F32, ctx)
        loaded, kt, kt_done, s_mm, s_done, own_s, shifted, expd, ready, turned, taken, s_free = (k.sem("rt_" + n) for n in
            ("loaded", "kt", "kt_done", "s_mm", "s_done", "own", "shifted", "expd", "ready", "turned", "taken", "s_free"))
        with nc.Block() as block:
            @block.sync
            def _(sp):
                sp.dma_start(keys[:, :, :], a["peer_keys"][0].rearrange("h p k d -> k (h p) d")).then_inc(loaded, 16)

            def turn(pe, t):
                r = ROWS[t]
                pe.wait_ge(ready, t + 1)
                if t:
                    pe.wait_ge(taken, t)
                for n in range(3):
                    ins = pe.transpose(k.pb[4][:, n * P:n * P + r], res[0:r, n, :], k.eye[0:r, 0:r])
                ins.then_inc(turned, 1)

            @block.tensor
            def _(pe):
                pe.wait_ge(loaded, 16)
                for n in range(HP):
                    if n >= 8 and n % 4 == 0:
                        pe.wait_ge(kt_done, n // 4 - 1)
                    ins = pe.transpose(k.pb[(n // 4) % 2][:, (n % 4) * P:(n % 4 + 1) * P], keys[:, n, :], k.eye)
                    if n % 4 == 3:
                        ins.then_inc(kt, 1)
                pe.wait_ge(kt_done, HP // 4)
                for t, r in enumerate(ROWS):
                    if t:
                        pe.wait_ge(s_done, 2 * t)
                    for n in range(HP):
                        ins = pe.matmul(k.pb[n // 4][0:r, (n % 4) * P:(n % 4 + 1) * P], q[:, n, t * P:t * P + r],
                                        keysT[:, n, :], start=True, stop=True)
                        if n % 8 == 7:
                            ins.then_inc(s_mm, 1)
                    if t:
                        turn(pe, t - 1)
                turn(pe, NT - 1)

            @block.scalar
            def _(act):
                for n in range(HP // 4):
                    act.wait_ge(kt, n + 1)
                    act.activation(keysT[:, 4 * n:4 * n + 4, :].rearrange("p a b -> p (a b)"), k.pb[n % 2], ACT.Copy).then_inc(kt_done, 1)
                for t, r in enumerate(ROWS):
                    for n in range(2):
                        act.wait_ge(s_mm, 2 * t + n + 1)
                        if t >= 2:
                            act.wait_ge(s_free, t - 1)
                        act.activation(s[0:r, t % 2, 8 * n:8 * n + 8, :].rearrange("p (b a) c -> p b (a c)", b=2),
                                       k.pv[n][0:r, :, :], ACT.Copy).then_inc(s_done, 1)
                    act.wait_ge(shifted, t + 1)
                    act.activation(res[0:r, 2, :].rearrange("p (h k) -> p h k", h=PH), best[0:r, :, :], ACT.Exp).then_inc(expd, 1)

            @block.vector
            def _(dve):
                own = Own(dve, own_s)

                def two_eights(rows, n, vals, idx, src):
                    for half in (slice(0, 8), slice(8, 16)):
                        for m in range(n):
                            ins = dve.max(vals(m)[:, half], src(m))
                        own.fence(ins)
                        for m in range(n):
                            ins = dve.max_index(idx(m)[:, half], vals(m)[:, half], src(m))
                        if half.start == 0:
                            own.fence(ins)
                            for m in range(n):
                                ins = dve.match_replace(src(m), vals(m)[:, half], src(m), LOWEST)
                            own.fence(ins)
                    return ins

                for t, r in enumerate(ROWS):
                    dve.wait_ge(s_done, 2 * t + 2)
                    two_eights(r, HP, lambda m: top[0:r, m, :], lambda m: top_i[0:r, m, :],
                               lambda m: s[0:r, t % 2, m, :]).then_inc(s_free, 1)
                    dve.wait_ge(s_free, t + 1)
                    dve.tensor_copy(top_f[0:r, :, :], top_i[0:r, :, :])
                    tv = top[0:r, :, :].rearrange("p (h n) k -> p h n k", n=2)
                    own.fence(dve.tensor_tensor(cand[0:r, :, :, :],
                                                tv[:, :, 0, :].unsqueeze(3).to_broadcast([r, PH, TOPK, TOPK]),
                                                tv[:, :, 1, :].unsqueeze(2).to_broadcast([r, PH, TOPK, TOPK]), ALU.add))
                    cf = cand[0:r, :, :, :].rearrange("p h a b -> p h (a b)")
                    own.fence(two_eights(r, PH, lambda m: best[0:r, m, :], lambda m: sel[0:r, m, :], lambda m: cf[:, m, :]))
                    dve.tensor_tensor(hot[0:r, 0, :, 0:PH].rearrange("p k h -> p h k"), best[0:r, :, :],
                                      best[0:r, :, 0:1].to_broadcast([r, PH, TOPK]), ALU.subtract)
                    sf = sel[0:r, :, :].rearrange("p h k -> p (h k)")
                    dve.tensor_scalar(pick[0:r, 0, :], sf, 4, None, ALU.logical_shift_right)
                    own.fence(dve.tensor_scalar(pick[0:r, 1, :], sf, TOPK - 1, None, ALU.bitwise_and))
                    if t:
                        dve.wait_ge(turned, t)
                    dve.tensor_copy(best[0:r, :, :], hot[0:r, 0, :, 0:PH].rearrange("p k h -> p h k")).then_inc(shifted, 1)
                    dve.wait_ge(shifted, t + 1)
                    own.fence(dve.tensor_copy(pick_f[0:r, :, :], pick[0:r, :, :]))
                    tf = top_f[0:r, :, :].rearrange("p (h n) k -> p h n k", n=2)
                    for n in range(2):
                        own.fence(dve.tensor_tensor(hot[0:r, :, :, :].rearrange("p h k a -> p (h k) a"),
                                                    pick_f[0:r, n, :].unsqueeze(2).to_broadcast([r, HK, TOPK]),
                                                    k.iota[0:r, 0:TOPK].unsqueeze(1).to_broadcast([r, HK, TOPK]), ALU.is_equal))
                        own.fence(dve.tensor_tensor(hot[0:r, :, :, :], hot[0:r, :, :, :],
                                                    tf[:, :, n, :].unsqueeze(2).to_broadcast([r, PH, TOPK, TOPK]), ALU.mult))
                        own.fence(dve.tensor_reduce(res[0:r, n, :], hot[0:r, :, :, :].rearrange("p h k a -> p (h k) a"),
                                                    AX.X, ALU.add))
                    dve.wait_ge(expd, t + 1)
                    g = res[0:r, 2, :].rearrange("p (h k) -> p h k", h=PH)
                    own.fence(dve.tensor_reduce(tot[0:r, :], g, AX.X, ALU.add))
                    own.fence(dve.reciprocal(tot[0:r, :], tot[0:r, :]))
                    dve.tensor_tensor(g, g, tot[0:r, :].unsqueeze(2).to_broadcast([r, PH, TOPK]), ALU.mult).then_inc(ready, 1)
                    dve.wait_ge(ready, t + 1)
                    dve.wait_ge(turned, t + 1)
                    c = slice(t * P, t * P + r)
                    for n, dst in enumerate((gi, gj, gate)):
                        ins = dve.tensor_copy(dst[:, c], k.pb[4][:, n * P:n * P + r])
                    ins.then_inc(taken, 1)
                    dve.wait_ge(taken, t + 1)
                own.fence(dve.tensor_copy(gate_hi[:, :], gate[:, :]))
                own.fence(dve.tensor_tensor(gate_lo[:, :], gate[:, :], gate_hi[:, :].bitcast(F32), ALU.subtract))


@phase
def spread_gates(k, gi, gj, gate_hi, gate_lo, g_dram):
    nc = k.nc
    GROUPS = TB // TG
    STEPS = GROUPS // 2
    with ExitStack() as ctx:
        ahi = [k.sb(f"sg_ahi{b}", [P, TG, P], F32R, ctx) for b in range(2)]
        alo = [k.sb(f"sg_alo{b}", [P, TG, P], F32R, ctx) for b in range(2)]
        bj = [k.sb(f"sg_bj{b}", [P, TG, P], F32R, ctx) for b in range(2)]
        stage = [k.sb(f"sg_stage{b}", [P, NK, TB], F32, ctx) for b in range(2)]
        hot, mm, taken, stored = k.sem("sg_hot"), k.sem("sg_mm"), k.sem("sg_taken"), [k.sem(f"sg_stored{b}") for b in range(2)]
        FREE = 2
        with nc.Block() as block:
            @block.vector
            def _(dve):
                with dve.Fori(0, NB * STEPS) as s:
                    for b in range(2):
                        dve.wait_ge(mm, 2 * s + b + 1)
                        for n in range(TG):
                            col = (2 * s + b) * TG + n
                            one = lambda x: x[:, ds(col, 1)]
                            dve.tensor_scalar(ahi[b][:, n, :], k.iota, one(gi), one(gate_hi).bitcast(F32),
                                              ALU.is_equal, ALU.mult)
                            dve.tensor_scalar(alo[b][:, n, :], k.iota, one(gi), one(gate_lo), ALU.is_equal, ALU.mult)
                            ins = dve.tensor_scalar(bj[b][:, n, :], k.iota, one(gj), None, ALU.is_equal)
                        ins.then_inc(hot, 1)

            @block.gpsimd
            def _(pool):
                pool.sem_inc(mm, FREE)
                pool.sem_inc(taken, FREE)

            @block.tensor
            def _(pe):
                for nb in range(NB):
                    with pe.Fori(0, STEPS) as s:
                        for b in range(2):
                            u = nb * GROUPS + 2 * s + b
                            pe.wait_ge(hot, u + 1)
                            pe.wait_ge(taken, u + 1)
                            for n in range(TG):
                                out = k.pb[b][:, n * P:(n + 1) * P]
                                pe.matmul(out, alo[b][:, n, :], bj[b][:, n, :], start=True, stop=False)
                                ins = pe.matmul(out, ahi[b][:, n, :], bj[b][:, n, :], start=False, stop=True)
                            ins.then_inc(mm, 1)

            @block.scalar
            def _(act):
                for nb in range(NB):
                    if nb >= 2:
                        act.wait_ge(stored[nb % 2], 16 * (nb // 2))
                    with act.Fori(0, STEPS) as s:
                        for b in range(2):
                            u = nb * GROUPS + 2 * s + b
                            act.wait_ge(mm, FREE + u + 1)
                            act.activation(stage[nb % 2][:, :, ds((2 * s + b) * TG, TG)],
                                           k.pb[b].rearrange("p (t j) -> p j t", t=TG), ACT.Copy).then_inc(taken, 1)

            @block.sync
            def _(sp):
                for nb in range(NB):
                    sp.wait_ge(taken, FREE + (nb + 1) * GROUPS)
                    width = GJ * TB
                    sp.dma_start(g_dram[:, :, nb * width:(nb + 1) * width],
                                 stage[nb % 2][:, :, :].rearrange("p (g j) t -> p g (j t)", j=GJ)).then_inc(stored[nb % 2], 16)
                for b in range(2):
                    sp.wait_ge(stored[b], 16 * ((NB + 1 - b) // 2))


@phase
def experts(k, a, hi, lo, g_dram, acc):
    nc = k.nc
    NG = NK // GJ
    VJ = DC
    u_dram = a["peer_u"][0].rearrange("(i j) d -> i j d", j=NK)
    v_dram = a["peer_v"][0].rearrange("(i j) d -> i j d", j=NK)
    two = range(2)
    with ExitStack() as ctx:
        u_raw = [k.sb(f"u_raw{b}", [P, GJ, D], F32, ctx) for b in two]
        v_raw = [k.sb(f"v_raw{b}", [P, GJ, D], F32, ctx) for b in two]
        v_hi = [k.sb(f"v_hi{b}", [P, GJ, D], F32R, ctx) for b in two]
        v_lo = [k.sb(f"v_lo{b}", [P, GJ, D], F32R, ctx) for b in two]
        ut_hi = [k.sb(f"ut_hi{b}", [P, DC, P], F32R, ctx) for b in two]
        ut_lo = [k.sb(f"ut_lo{b}", [P, DC, P], F32R, ctx) for b in two]
        g_in = [k.sb(f"g_in{b}", [P, NB, GJ, TB], F32, ctx) for b in two]
        gelu = [k.sb(f"gelu{b}", [P, T], F32, ctx) for b in two]
        coef = [k.sb(f"coef{b}", [P, T], F32, ctx) for b in two]
        c_hi = [k.sb(f"c_hi{b}", [P, GJ, T], F32R, ctx) for b in two]
        c_lo = [k.sb(f"c_lo{b}", [P, GJ, T], F32R, ctx) for b in two]
        u_loaded, v_loaded, g_loaded = ([k.sem(f"ex_{n}_loaded{b}") for b in two] for n in "uvg")
        u_turned, u_hi_done, u_lo_done, v_hi_done, v_lo_done, u_products, gelu_done, coef_done, c_done, \
            v_products, added = (k.sem("ex_" + n) for n in ("u_turned", "u_hi_done", "u_lo_done", "v_hi_done", "v_lo_done",
            "u_products", "gelu_done", "coef_done", "c_done", "v_products", "added"))
        cleared = k.sem("ex_cleared")
        ps_t, ps_a, ps_v = k.pv[0], k.pv[1], k.pv[2:4]

        def groups(eng, group):
            group(0, 0, 0)
            with eng.Fori(0, NG // 2 - 1) as s:
                group(2 * s + 1, s, 1)
                group(2 * s + 2, s + 1, 0)
            group(NG - 1, NG // 2 - 1, 1)

        with nc.Block() as block:
            @block.sync
            def _(sp):
                def group(g, m, b):
                    wait(sp, u_turned, 4 * g - 4)
                    sp.dma_start(u_raw[b][:, :, :], u_dram[:, ds(GJ * g, GJ), :]).then_inc(u_loaded[b], 16)
                    wait(sp, v_lo_done, g - 1)
                    sp.dma_start(v_raw[b][:, :, :], v_dram[:, ds(GJ * g, GJ), :]).then_inc(v_loaded[b], 16)
                    wait(sp, coef_done, 2 * g - 2)
                    sp.dma_start(g_in[b][:, :, :, :].rearrange("p n j t -> p (n j t)").unsqueeze(1),
                                 g_dram[:, ds(g, 1), :]).then_inc(g_loaded[b], 16)

                group(0, 0, 0)
                group(1, 0, 1)
                with sp.Fori(1, NG // 2) as s:
                    group(2 * s, s, 0)
                    group(2 * s + 1, s, 1)

            @block.tensor
            def _(pe):
                def turn(n, src, j):
                    for h in two:
                        wait(pe, u_lo_done, 2 * n + h - 1)
                        for c in range(4):
                            ins = pe.transpose(ps_t[:, h, c * P:(c + 1) * P],
                                               src[:, j, (4 * h + c) * P:(4 * h + c + 1) * P], k.eye)
                        ins.then_inc(u_turned, 1)

                def times_v(g, kk, b):
                    if kk == 0:
                        pe.wait_ge(v_lo_done, g + 1)
                        pe.wait_ge(c_done, 2 * g + 2)
                    for dd in range(VJ // 2):
                        c = kk * VJ // 2 + dd
                        pe.wait_ge(added, VJ + VJ * g + c - 1)
                        for h in two:
                            ts = slice(h * HALF, (h + 1) * HALF)
                            for j in range(GJ):
                                w = slice(c * P, (c + 1) * P)
                                out = ps_v[dd % 2][:, h, 0:HALF]
                                pe.matmul(out, v_lo[b][:, j, w], c_hi[b][:, j, ts], start=(j == 0), stop=False)
                                pe.matmul(out, v_hi[b][:, j, w], c_lo[b][:, j, ts], start=False, stop=False)
                                ins = pe.matmul(out, v_hi[b][:, j, w], c_hi[b][:, j, ts], start=False, stop=(j == GJ - 1))
                        ins.then_inc(v_products, 1)

                pe.wait_ge(u_loaded[0], 16)
                turn(0, u_raw[0], 0)

                def group(g, m, b):
                    for kk in two:
                        n = 2 * g + kk
                        if kk == 0:
                            turn(n + 1, u_raw[b], 1)
                        elif not (isinstance(g, int) and g == NG - 1):
                            pe.wait_ge(u_loaded[1 - b], 16 * (m + 1 + b))
                            turn(n + 1, u_raw[1 - b], 0)
                        pe.wait_ge(u_lo_done, 2 * n + 2)
                        wait(pe, gelu_done, n)
                        for h in two:
                            ins = mm3(pe, ps_a[:, h, 0:HALF], DC, lambda x, c: x[:, c, :], ut_hi[kk], ut_lo[kk],
                                      lambda x, c: x[:, c, h * HALF:(h + 1) * HALF], hi, lo)
                        ins.then_inc(u_products, 1)
                        if not (isinstance(g, int) and g == 0):
                            times_v(g - 1, kk, 1 - b)

                groups(pe, group)
                for kk in two:
                    times_v(NG - 1, kk, 1)

            @block.scalar
            def _(act):
                def u_part(n, par):
                    for h in two:
                        act.wait_ge(u_turned, 2 * n + h + 1)
                        wait(act, u_products, n - 1)
                        act.activation(ut_hi[par][:, 4 * h:4 * h + 4, :].rearrange("p c i -> p (c i)"), ps_t[:, h, :],
                                       ACT.Copy).then_inc(u_hi_done, 1)

                u_part(0, 0)

                def group(g, m, b):
                    for kk in two:
                        n = 2 * g + kk
                        if not (isinstance(g, int) and n == NK - 1):
                            u_part(n + 1, 1 - kk)
                        if kk == 0:
                            act.wait_ge(v_loaded[b], 16 * (m + 1))
                            wait(act, v_products, VJ * g)
                            act.activation(v_hi[b][:, :, :], v_raw[b][:, :, :], ACT.Copy).then_inc(v_hi_done, 1)
                        act.wait_ge(u_products, n + 1)
                        wait(act, coef_done, n - 1)
                        act.activation(gelu[kk][:, :].rearrange("p (h t) -> p h t", h=2), ps_a[:, :, 0:HALF],
                                       ACT.Gelu).then_inc(gelu_done, 1)

                groups(act, group)

            @block.vector
            def _(dve):
                def u_part(n, par):
                    for h in two:
                        dve.wait_ge(u_hi_done, 2 * n + h + 1)
                        part = slice(4 * h, 4 * h + 4)
                        dve.tensor_tensor(ut_lo[par][:, part, :].rearrange("p c i -> p (c i)"), ps_t[:, h, :],
                                          ut_hi[par][:, part, :].rearrange("p c i -> p (c i)").bitcast(F32),
                                          ALU.subtract).then_inc(u_lo_done, 1)

                def add(g, kk):
                    for dd in range(VJ // 2):
                        c = kk * VJ // 2 + dd
                        dve.wait_ge(v_products, VJ + VJ * g + c + 1)
                        dve.wait_ge(added, VJ * g + c + 1)
                        out = acc[:, c, :].rearrange("p (h t) -> p h t", h=2)
                        dve.tensor_tensor(out, out, ps_v[dd % 2][:, :, 0:HALF], ALU.add).then_inc(added, 1)

                fence(dve, dve.memset(acc[:, :, :], 0.0), cleared, 1)
                dve.sem_inc(added, VJ)
                u_part(0, 0)

                def group(g, m, b):
                    for kk in two:
                        n = 2 * g + kk
                        if not (isinstance(g, int) and n == NK - 1):
                            u_part(n + 1, 1 - kk)
                        if kk == 0:
                            dve.wait_ge(v_hi_done, g + 1)
                            dve.tensor_tensor(v_lo[b][:, :, :], v_raw[b][:, :, :], v_hi[b][:, :, :].bitcast(F32),
                                              ALU.subtract).then_inc(v_lo_done, 1)
                        if not (isinstance(g, int) and g == 0):
                            add(g - 1, kk)

                groups(dve, group)
                for kk in two:
                    add(NG - 1, kk)
                dve.wait_ge(added, VJ + VJ * NG)

            @block.gpsimd
            def _(pool):
                def group(g, m, b):
                    for kk in two:
                        n = 2 * g + kk
                        pool.wait_ge(gelu_done, n + 1)
                        if kk == 0:
                            pool.wait_ge(g_loaded[b], 16 * (m + 1))
                        wait(pool, c_done, n - 1)
                        blocks = lambda x: x.rearrange("p (n t) -> p n t", n=NB)
                        pool.tensor_tensor(blocks(coef[kk][:, :]), blocks(gelu[kk][:, :]), g_in[b][:, :, kk, :], ALU.mult)
                        wait(pool, v_products, VJ * g)
                        fence(pool, pool.tensor_tensor(blocks(c_hi[b][:, kk, :]), blocks(gelu[kk][:, :]),
                                                       g_in[b][:, :, kk, :], ALU.mult), coef_done, n + 1)
                        pool.tensor_tensor(c_lo[b][:, kk, :], coef[kk][:, :], c_hi[b][:, kk, :].bitcast(F32),
                                           ALU.subtract).then_inc(c_done, 1)

                pool.sem_inc(v_products, VJ)
                groups(pool, group)


@phase
def finish(k, a, o, h_tok, acc):
    nc = k.nc
    with ExitStack() as ctx:
        junk = k.sb("fin_junk", [P, D], F32, ctx)
        g = k.sb("fin_gain", [P, D], F32, ctx)
        ms = k.sb("fin_ms", [P, NT], F32, ctx)
        loaded, turned, summed, squared, rooted, own_s, ready, stored = (k.sem("fin_" + n) for n in
            ("loaded", "turned", "summed", "squared", "rooted", "own", "ready", "stored"))
        with nc.Block() as block:
            @block.sync
            def _(sp):
                sp.dma_start(g[:, :], a["norm_final"].unsqueeze(0).to_broadcast([P, D])).then_inc(loaded, 16)
                sp.wait_ge(ready, 4)
                sp.dma_start(o["y_p"][0].rearrange("(t p) d -> p t d", p=P), h_tok[:, 0:4, :]).then_inc(stored, 16)
                sp.wait_ge(ready, NT)
                sp.dma_start(o["y_s"][:, 0, :], h_tok[0:NS, 4, :]).then_inc(stored, 16)
                sp.wait_ge(stored, 32)

            @block.tensor
            def _(pe):
                for t, r in enumerate(ROWS):
                    if t >= 2:
                        pe.wait_ge(summed, t - 1)
                    for c in range(DC):
                        ins = pe.transpose(k.pv[t % 2][0:r, c // 4, (c % 4) * P:(c % 4 + 1) * P], acc[:, c, t * P:t * P + r], k.eye)
                    ins.then_inc(turned, 1)

            @block.vector
            def _(dve):
                own = Own(dve, own_s)
                own.fence(dve.memset(ms[:, :], 1.0))
                for t, r in enumerate(ROWS):
                    dve.wait_ge(turned, t + 1)
                    x = h_tok[0:r, t, :].rearrange("p (n c) -> p n c", n=2)
                    dve.tensor_tensor(x, x, k.pv[t % 2][0:r, :, :], ALU.add).then_inc(summed, 1)
                dve.wait_ge(rooted, 1)
                own.fence(dve.reciprocal(ms[:, :], ms[:, :]))
                dve.wait_ge(loaded, 16)
                for t, r in enumerate(ROWS):
                    dve.scalar_tensor_tensor(h_tok[0:r, t, :], h_tok[0:r, t, :], ms[0:r, t:t + 1], g[0:r, :],
                                             ALU.mult, ALU.mult).then_inc(ready, 1)

            @block.scalar
            def _(act):
                for t, r in enumerate(ROWS):
                    act.wait_ge(summed, t + 1)
                    fence(act, act.activation(junk[0:r, :], h_tok[0:r, t, :], ACT.Square, scale=D ** -0.5,
                                              accum_out=ms[0:r, t:t + 1]), squared, t + 1)
                act.activation(ms[:, :], ms[:, :], ACT.Sqrt, bias=k.eps[:, :]).then_inc(rooted, 1)


def program(nc, a, o, g_dram, h_store):
    w_in = a["w_in"][0]
    with ExitStack() as whole:
        k = Core(nc, whole)
        k.pv = [whole.enter_context(nc.psum_tensor(f"ps{n}", [P, 2, 512], F32)) for n in range(4)]
        k.pb = [k.pv[n // 2][:, n % 2, :] for n in range(8)]
        load_constants(k, a)
        x_hi, x_lo = k.sb("x_hi", [P, DC, T], F32R), k.sb("x_lo", [P, DC, T], F32R)
        with ExitStack() as c:
            x_tok = k.sb("x_tok", [P, NT, D], F32, c)
            norm_and_turn(k, "norm1", x_tok, load_tokens(a, x_tok), k.vecs[:, 0:DC], x_hi, x_lo)
        with ExitStack() as branches:
            o_hi = k.sb("o_hi", [P, 3 * H, T], F32R, branches)
            o_lo = k.sb("o_lo", [P, 3 * H, T], F32R, branches)
            with ExitStack() as mixers:
                load_sample_consts(k, a, mixers)
                with ExitStack() as c:
                    sb = lambda n, s, dt=F32: k.sb(n, s, dt, c)
                    gate_a = sb("gate_a", [P, NT, QA])
                    ba = sb("ba", [P, NT, 2 * H])
                    beta, logd = sb("beta", [P, NT, H]), sb("logd", [P, NT, H])
                    pre = sb("pre", [P, CT, PAD + T])
                    clear_pad(k, pre)
                    stream(k, "proj_a", [
                        Job(columns(w_in, 0, CONV_CH), 3, True, x_hi, x_lo, to_channels(pre, PAD + T, PAD)),
                        Job(columns(w_in, COL_GATE_A, QA), 1, False, x_hi, x_lo, to_tokens(gate_a, QA), ACT.Silu)])
                    small_projection(k, a, x_hi, x_lo, ba)
                    decays(k, ba, beta, logd)
                    k_tok, v_tok = sb("k_tok", [P, NT, QA]), sb("v_tok", [P, NT, QA])
                    convolve(k, a, o, pre, k_tok, v_tok)
                    delta_prompt(k, a, o, pre, k_tok, v_tok, beta, logd)
                    delta_sample(k, a, o, pre, v_tok, beta, logd)
                    gate_and_turn(k, a, "gate_a", v_tok, gate_a, a["gn_a"], DK, o_hi, o_lo, 0)
                with ExitStack() as c:
                    sb = lambda n, s, dt=F32: k.sb(n, s, dt, c)
                    gate_b, v_b = sb("gate_b", [P, NT, VB]), sb("v_b", [P, NT, VB])
                    qk_b = sb("qk_b", [P, 2 * H, T])
                    stream(k, "proj_b", [
                        Job(columns(w_in, COL_QK_B, 2 * H * DK), 2, True, x_hi, x_lo, to_channels(qk_b, T)),
                        Job(columns(w_in, COL_V_B, VB), 2, False, x_hi, x_lo, to_tokens(v_b, VB)),
                        Job(columns(w_in, COL_GATE_B, VB), 2, False, x_hi, x_lo, to_tokens(gate_b, VB), ACT.Silu)])
                    kb_tok = sb("kb_tok", [P, 4, QA])
                    rotate(k, a, qk_b, kb_tok)
                    retention_prompt(k, a, o, qk_b, v_b, kb_tok)
                    retention_sample(k, a, o, qk_b, v_b)
                    gate_and_turn(k, a, "gate_b", v_b, gate_b, a["gn_b"], DV_B, o_hi, o_lo, H)
            with ExitStack() as c:
                sel_a, sel_b, br_a, br_b = (k.sb(n, [P, DC, T], F32, c) for n in ("sel_a", "sel_b", "br_a", "br_b"))
                stream(k, "branches", [
                    Job(columns(w_in, COL_SEL_A, D), 2, True, x_hi, x_lo, to_channels(sel_a, T), ACT.Sigmoid),
                    Job(columns(w_in, COL_SEL_B, D), 2, True, x_hi, x_lo, to_channels(sel_b, T), ACT.Sigmoid),
                    Job(columns(a["w_br_a"][0], 0, D), 2, True, o_hi, o_lo, to_channels(br_a, T)),
                    Job(columns(a["w_br_b"][0], 0, D), 2, True, o_hi[:, H:, :], o_lo[:, H:, :], to_channels(br_b, T))])
                merge(k, sel_a, sel_b, br_a, br_b, o_hi, o_lo)
            with ExitStack() as c:
                h_part = k.sb("h_part", [P, NT, D], F32, c)
                stream(k, "w_out", [Job(columns(a["w_out"][0], 0, D), 2, False, o_hi, o_lo, to_tokens(h_part, D))])
                add_tokens(k, a, h_part)
                halves = lambda x: [x[:, 0:4, :], x[0:NS, 4, :]]
                h_dram = [h_store[0:NP_TOK, :].rearrange("(t p) d -> p t d", p=P), h_store[NP_TOK:T, :]]
                spill(k, "h_stored", h_dram, halves(h_part))
        h_tok = k.sb("h_tok", [P, NT, D])
        spill(k, "h_loaded", halves(h_tok), h_dram)
        norm_and_turn(k, "norm2", h_tok, None, k.vecs[:, DC:2 * DC], x_hi, x_lo)
        with ExitStack() as c:
            gi, gj = k.sb("gi", [P, T], F32, c), k.sb("gj", [P, T], F32, c)
            g_hi, g_lo = k.sb("g_hi", [P, T], F32R, c), k.sb("g_lo", [P, T], F32, c)
            with ExitStack() as c2:
                q = k.sb("peer_q", [P, HP, T], F32, c2)
                stream(k, "queries", [Job(columns(a["peer_wq"][0], 0, HP * P), 4, True, x_hi, x_lo, to_channels(q, T))])
                retrieve(k, a, q, gi, gj, g_hi, g_lo)
            spread_gates(k, gi, gj, g_hi, g_lo, g_dram)
        acc = k.sb("acc", [P, DC, T])
        experts(k, a, x_hi, x_lo, g_dram, acc)
        finish(k, a, o, h_tok, acc)


INPUTS = ("x_prompt", "x_sample", "state_conv_a", "state_delta", "state_ret", "norm_mix", "w_in", "conv_w",
          "a_log", "dt_bias", "gn_a", "gn_b", "w_br_a", "w_br_b", "w_out", "norm_ffn", "peer_wq", "peer_keys",
          "peer_u", "peer_v", "norm_final")
OUTPUTS = {
    "y_p": (1, NP_TOK, D), "y_s": (NS, 1, D),
    "conv_p": (1, 1, PAD, CONV_CH), "delta_p": (1, 1, H, DK, DK), "ret_p": (1, 1, H, DK, DV_B),
    "conv_s": (1, NS, PAD, CONV_CH), "delta_s": (1, NS, H, DK, DK), "ret_s": (1, NS, H, DK, DV_B),
}


def build(nc, shapes):
    a = {n: nc.dram_tensor("in_" + n, s, F32, kind="ExternalInput").ap() for n, s in shapes.items()}
    o = {n: nc.dram_tensor("out_" + n, s, F32, kind="ExternalOutput").ap() for n, s in OUTPUTS.items()}
    g_dram = nc.dram_tensor("gates", (P, NK // GJ, NB * GJ * TB), F32, kind="Internal").ap()
    h_store = nc.dram_tensor("h_store", (T, D), F32, kind="Internal").ap()
    program(nc, a, o, g_dram, h_store)


def kernel(**inputs):
    import concourse.bacc as bacc
    from concourse.bass_utils import run_bass_kernel_spmd

    arrays = {n: np.ascontiguousarray(inputs[n]) for n in INPUTS}
    arrays.update(constants())
    nc = bacc.Bacc("TRN2", target_bir_lowering=False, num_devices=1)
    build(nc, {n: x.shape for n, x in arrays.items()})
    r = run_bass_kernel_spmd(nc, [{"in_" + n: x for n, x in arrays.items()}], core_ids=[0])
    return tuple(r.results[0]["out_" + n] for n in OUTPUTS)
```

```python
import numpy as np
from contextlib import ExitStack

import concourse.bass as bass
from concourse import mybir

F32 = mybir.dt.float32
F32R = mybir.dt.float32r
U32 = mybir.dt.uint32
ALU = mybir.AluOpType
ACT = mybir.ActivationFunctionType
AX = mybir.AxisListType
ds = bass.ds

P = 128
D = 1024
DC = D // P
NP_TOK = 512
NS = 8
T = NP_TOK + NS
HALF = T // 2
NT = 5
ROWS = [P, P, P, P, NS]
H = 4
DK = 128
DV_B = 256
QA = H * DK
CONV_W = 4
CONV_CH = 3 * QA
CT = CONV_CH // P
PAD = CONV_W - 1
VB = H * DV_B
IN_DIM = CONV_CH + QA + 2 * H + 2 * H * DK + 2 * VB + 2 * D
COL_GATE_A = CONV_CH
COL_BA = COL_GATE_A + QA
COL_QK_B = COL_BA + 2 * H
COL_V_B = COL_QK_B + 2 * H * DK
COL_GATE_B = COL_V_B + VB
COL_SEL_A = COL_GATE_B + VB
COL_SEL_B = COL_SEL_A + D
EPS = 1e-6
PAST_LEN = 4096
NK = 128
PH = 8
TOPK = 16
HP = 2 * PH
WCOLS = 256
LEVELS = 7
TB = 40
NB = T // TB
GJ = 4
UT = NK // 2
TG = 4
SIDE_CONV = 10
SIDE = 2 * H + 2 * DC
FAR = -1e30
LOWEST = -3.0e38


def gammas():
    return 1.0 - 2.0 ** (-5.0 - np.arange(H, dtype=np.float64))


def constants():
    i = np.arange(P)
    j_, i_ = i[:, None], i[None, :]
    eye = np.eye(P, dtype=np.float32)
    upto = (j_ <= i_).astype(np.float32)
    neg = np.where(j_ <= i_, 0.0, FAR).astype(np.float32)
    masks = np.zeros((P, LEVELS, P), np.float32)
    for l in range(LEVELS):
        s = 1 << l
        masks[:, l] = ((j_ // (2 * s) == i_ // (2 * s)) & (i_ % (2 * s) >= s) & (j_ % (2 * s) < s))
    half = DK // 2
    inv = (np.float32(10000.0) ** (-np.arange(half, dtype=np.float32) / np.float32(half))).astype(np.float32)
    pos = np.concatenate([np.arange(NP_TOK), np.full(NS, PAST_LEN)]).astype(np.float32)
    ang = (inv[:, None] * pos[None, :]).astype(np.float32)
    cos, sin = np.cos(ang), np.sin(ang)
    rope = np.zeros((P, 2, T), np.float32)
    rope[:half, 0], rope[half:, 0] = cos, cos
    rope[:half, 1], rope[half:, 1] = sin, -sin
    lg = np.log(gammas())
    dec = np.zeros((P, H, P), np.float32)
    qdec = np.zeros((P, H, P), np.float32)
    kdec = np.zeros((P, H), np.float32)
    for h in range(H):
        dec[:, h] = np.where(j_ <= i_, np.exp(np.minimum((i_ - j_), P) * lg[h] * (j_ <= i_)), 0.0)
        qdec[:, h] = np.exp((i_ + 1.0) * lg[h])
        kdec[:, h] = np.exp((P - 1.0 - i) * lg[h])
    sq = np.concatenate([eye, upto, neg, np.broadcast_to(np.arange(P, dtype=np.float32), (P, P)),
                         np.ones((P, P), np.float32)], axis=1)
    eye8 = np.broadcast_to(np.eye(NS, dtype=np.float32).reshape(1, -1), (P, NS * NS))
    return {
        "c_square": np.ascontiguousarray(sq, np.float32),
        "c_masks": masks.reshape(P, -1),
        "c_rope": rope.reshape(P, -1),
        "c_ret": np.ascontiguousarray(np.concatenate([dec.reshape(P, -1), qdec.reshape(P, -1), kdec, eye8], axis=1), np.float32),
    }


def fence(eng, ins, sem, value):
    ins.then_inc(sem, 1)
    eng.wait_ge(sem, value)


class Own:

    def __init__(self, eng, sem):
        self.eng, self.sem, self.n = eng, sem, 0

    def fence(self, ins):
        self.n += 1
        fence(self.eng, ins, self.sem, self.n)


def wait(eng, sem, value):
    if isinstance(value, int) and value <= 0:
        return
    eng.wait_ge(sem, value)


class Core:

    def __init__(self, nc, ctx):
        self.nc, self.ctx = nc, ctx

    def sb(self, name, shape, dt=F32, ctx=None):
        return (ctx or self.ctx).enter_context(self.nc.sbuf_tensor(name, shape, dt))

    def sem(self, name):
        self.sems.append(self.nc.alloc_semaphore(name=name))
        return self.sems[-1]


def phase(build):
    def run(k, *args, **options):
        k.sems = []
        build(k, *args, **options)
        k.nc.clear_and_free_semaphores(k.sems)
        k.nc.all_engine_barrier()
    return run


def flat(t):
    return t[:, :, :].rearrange("p a b -> p (a b)")


@phase
def load_constants(k, a):
    nc = k.nc
    k.square = k.sb("square", [P, 5 * P])
    k.eye, k.upto, k.neg = (k.square[:, n * P:(n + 1) * P] for n in range(3))
    k.iota, k.ones = (k.square[:, n * P:(n + 1) * P] for n in (3, 4))
    k.eps = k.sb("eps", [P, 1])
    nvec = 2 * DC + CONV_W * CT
    k.vecs = k.sb("vecs", [P, nvec])
    vec_rows = k.sb("vec_rows", [nvec, P])
    k.a_neg = k.sb("a_neg", [P, H])
    k.dtb = k.sb("dtb", [P, H])
    k.ba_w = k.sb("ba_w", [P, DC, 2 * H])
    n = 2 * H * P + H + NS * NS
    k.ret = k.sb("ret_tables", [P, n])
    k.ret_dec = k.ret[:, 0:H * P].rearrange("p (h t) -> p h t", h=H)
    k.ret_qdec = k.ret[:, H * P:2 * H * P].rearrange("p (h t) -> p h t", h=H)
    k.ret_kdec = k.ret[:, 2 * H * P:2 * H * P + H]
    k.eye8 = k.ret[:, 2 * H * P + H:n].rearrange("p (a b) -> p a b", a=NS)
    loaded, turned, made = k.sem("const_loaded"), k.sem("vecs_turned"), k.sem("const_made")
    with nc.Block() as block:
        @block.sync
        def _(sp):
            sp.dma_start(k.square[:, :], a["c_square"]).then_inc(loaded, 16)
            sp.dma_start(vec_rows[0:DC, :], a["norm_mix"][0].rearrange("(c p) -> c p", p=P)).then_inc(loaded, 16)
            sp.dma_start(vec_rows[DC:2 * DC, :], a["norm_ffn"][0].rearrange("(c p) -> c p", p=P)).then_inc(loaded, 16)
            sp.dma_start(vec_rows[2 * DC:nvec, :], a["conv_w"][0].rearrange("i (c p) -> (i c) p", p=P)).then_inc(loaded, 16)
            sp.dma_start(k.a_neg[:, :], a["a_log"].to_broadcast([P, H])).then_inc(loaded, 16)
            sp.dma_start(k.dtb[:, :], a["dt_bias"].to_broadcast([P, H])).then_inc(loaded, 16)

        @block.tensor
        def _(pe):
            pe.wait_ge(loaded, 96)
            pe.transpose(k.pb[0][:, 0:nvec], vec_rows[:, :], k.eye[0:nvec, 0:nvec]).then_inc(turned, 1)

        @block.vector
        def _(dve):
            dve.memset(k.eps[:, :], EPS).then_inc(made, 1)
            dve.wait_ge(turned, 1)
            dve.tensor_copy(k.vecs[:, :], k.pb[0][:, 0:nvec]).then_inc(made, 1)

        @block.scalar
        def _(act):
            act.wait_ge(loaded, 96)
            act.activation(k.a_neg[:, :], k.a_neg[:, :], ACT.Exp).then_inc(made, 1)


@phase
def norm_and_turn(k, name, src, gain, hi, lo, load=None, plus=None, stores=(), extra=()):
    nc = k.nc
    with ExitStack() as ctx:
        junk = k.sb(name + "_junk", [P, D], F32, ctx)
        ms = k.sb(name + "_ms", [P, NT], F32, ctx)
        rstd = k.sb(name + "_rstd", [P, NT], F32, ctx)
        xn = k.sb(name + "_xn", [P, 2, D], F32, ctx)
        xg = k.sb(name + "_xg", [P, 2, DC, P], F32, ctx)
        loaded = [k.sem(f"{name}_loaded{t}") for t in range(NT)] if load else []
        squared, rooted = k.sem(name + "_squared"), k.sem(name + "_rooted")
        summed, stored = k.sem(name + "_summed"), k.sem(name + "_stored")
        inverted, scaled = k.sem(name + "_inverted"), k.sem(name + "_scaled")
        turned, gained, hi_done = k.sem(name + "_turned"), k.sem(name + "_gained"), k.sem(name + "_hi_done")
        lo_done, cleared = k.sem(name + "_lo_done"), k.sem(name + "_cleared")
        with nc.Block() as block:
            @block.sync
            def _(sp):
                for t, r in enumerate(ROWS):
                    if load:
                        sp.dma_start(src[0:r, t, :], load[t]).then_inc(loaded[t], 16)
                for dst, s in extra:
                    sp.dma_start(dst, s).then_inc(stored, 16)
                for tiles, dst, s in stores:
                    sp.wait_ge(summed, tiles)
                    sp.dma_start(dst, s).then_inc(stored, 16)
                wait(sp, stored, 16 * (len(extra) + len(stores)))

            @block.scalar
            def _(act):
                act.wait_ge(cleared, 1)
                for t, r in enumerate(ROWS):
                    if load:
                        act.wait_ge(loaded[t], 16)
                    if plus is not None:
                        act.wait_ge(summed, t + 1)
                    fence(act, act.activation(junk[0:r, :], src[0:r, t, :], ACT.Square, scale=D ** -0.5,
                                              accum_out=ms[0:r, t:t + 1]), squared, t + 1)
                act.activation(ms[:, :], ms[:, :], ACT.Sqrt, bias=k.eps[:, :]).then_inc(rooted, 1)

                def scale(t):
                    r = ROWS[t]
                    if t >= 2:
                        act.wait_ge(turned, 2 * (t - 1))
                    act.activation(xn[0:r, t % 2, :], src[0:r, t, :], ACT.Copy,
                                   scale=rstd[0:r, t:t + 1]).then_inc(scaled, 1)

                act.wait_ge(inverted, 1)
                scale(0)
                scale(1)
                for t, r in enumerate(ROWS):
                    if t + 2 < NT:
                        scale(t + 2)
                    act.wait_ge(gained, 2 * t + 2)
                    act.activation(hi[:, :, t * P:t * P + r], xg[:, t % 2, :, 0:r], ACT.Copy).then_inc(hi_done, 1)

            @block.vector
            def _(dve):
                dve.memset(ms[:, :], 0.0).then_inc(cleared, 1)
                if plus is not None:
                    for t, r in enumerate(ROWS):
                        dve.tensor_tensor(src[0:r, t, :], src[0:r, t, :], plus[0:r, t, :], ALU.add).then_inc(summed, 1)
                dve.wait_ge(rooted, 1)
                dve.reciprocal(rstd[:, :], ms[:, :]).then_inc(inverted, 1)
                for t, r in enumerate(ROWS):
                    for c in range(2):
                        dve.wait_ge(turned, 2 * t + c + 1)
                        g = gain[:, 4 * c:4 * c + 4].unsqueeze(2).to_broadcast([P, 4, r])
                        src_ps = k.pb[2 * (t % 2) + c][:, :].rearrange("p (c t) -> p c t", t=P)[:, :, 0:r]
                        dve.tensor_tensor(xg[:, t % 2, 4 * c:4 * c + 4, 0:r], src_ps, g,
                                          ALU.mult).then_inc(gained, 1)
                    dve.wait_ge(gained, 2 * t + 2)
                    dve.wait_ge(hi_done, t + 1)
                    dve.tensor_tensor(lo[:, :, t * P:t * P + r], xg[:, t % 2, :, 0:r],
                                      hi[:, :, t * P:t * P + r].bitcast(F32), ALU.subtract).then_inc(lo_done, 1)
                dve.wait_ge(lo_done, NT)

            @block.tensor
            def _(pe):
                for t, r in enumerate(ROWS):
                    pe.wait_ge(scaled, t + 1)
                    if t >= 2:
                        pe.wait_ge(gained, 2 * (t - 1))
                    for c in range(DC):
                        ins = pe.transpose(k.pb[2 * (t % 2) + c // 4][:, (c % 4) * P:(c % 4) * P + r],
                                           xn[0:r, t % 2, c * P:(c + 1) * P], k.eye[0:r, 0:r])
                        if c % 4 == 3:
                            ins.then_inc(turned, 1)


class Job:

    def __init__(self, w, steps, turned, hi, lo, out, func=ACT.Copy):
        self.w, self.steps, self.turned, self.hi, self.lo, self.out, self.func = w, steps, turned, hi, lo, out, func
        self.kc = w.shape[1]
        self.results = 2 if turned else NT


@phase
def stream(k, name, jobs, extra=()):
    nc = k.nc
    with ExitStack() as ctx:
        raw = [k.sb(f"{name}_raw{b}", [P, DC, WCOLS], F32, ctx) for b in range(2)]
        whi = [k.sb(f"{name}_whi{b}", [P, DC, WCOLS], F32R, ctx) for b in range(2)]
        wlo = [k.sb(f"{name}_wlo{b}", [P, DC, WCOLS], F32R, ctx) for b in range(2)]
        w_loaded = [k.sem(f"{name}_w_loaded{b}") for b in range(2)]
        w_hi_done, w_lo_done = k.sem(name + "_w_hi_done"), k.sem(name + "_w_lo_done")
        extra_done = k.sem(name + "_extra")
        products, taken = k.sem(name + "_products"), k.sem(name + "_taken")
        FREE_RAW, FREE_PS, FREE_W = 2, 2, 2 * NT

        def plan():
            chunk0, result0, before = 0, FREE_W, 2
            for job in jobs:
                yield job, chunk0, result0, min(before, job.results)
                chunk0, result0, before = chunk0 + 2 * job.steps, result0 + 2 * job.steps * job.results, job.results

        def w_free(eng, job, result0, least, i, b):
            if b == 0:
                eng.wait_ge(products, result0 + 2 * job.results * i - least)
            else:
                eng.wait_ge(products, result0 + 2 * job.results * i)

        with nc.Block() as block:
            @block.sync
            def _(sp):
                for job, chunk0, _r, _l in plan():
                    with sp.Fori(0, job.steps) as i:
                        for b in range(2):
                            sp.wait_ge(w_lo_done, chunk0 + 2 * i + b + 1)
                            sp.dma_start(raw[b][:, 0:job.kc, :],
                                         job.w[:, :, ds((2 * i + b) * WCOLS, WCOLS)]).then_inc(w_loaded[b], 16)
                for dst, src in extra:
                    sp.dma_start(dst, src).then_inc(extra_done, 16)
                wait(sp, extra_done, 16 * len(extra))

            @block.scalar
            def _(act):
                def split(job, chunk0, result0, least, i, b):
                    act.wait_ge(w_loaded[b], 16 * (i + chunk0 // 2 + 1))
                    w_free(act, job, result0, least, i, b)
                    act.activation(whi[b][:, 0:job.kc, :], raw[b][:, 0:job.kc, :], ACT.Copy).then_inc(w_hi_done, 1)

                def step(here, i, after):
                    job, chunk0, result0, least = here
                    for b in range(2):
                        for n in range(job.results):
                            q = b * job.results + n
                            if n == job.results // 2:
                                if b == 0:
                                    split(*here, i, 1)
                                elif after is not None:
                                    split(*after)
                            act.wait_ge(products, result0 + 2 * job.results * i + q + 1)
                            ps = k.pv[q % 2]
                            if job.turned:
                                act.activation(job.out(i, q), ps[:, :, 0:HALF], job.func).then_inc(taken, 1)
                            else:
                                act.activation(job.out(i, b, n), ps[0:ROWS[n], 0, 0:WCOLS], job.func).then_inc(taken, 1)

                plans = list(plan())
                split(*plans[0], 0, 0)
                for n, here in enumerate(plans):
                    last = here[0].steps - 1
                    if last:
                        with act.Fori(0, last) as i:
                            step(here, i, (*here, i + 1, 0))
                    step(here, last, (*plans[n + 1], 0, 0) if n + 1 < len(plans) else None)

            @block.vector
            def _(dve):
                dve.sem_inc(w_lo_done, FREE_RAW)
                for job, chunk0, result0, least in plan():
                    with dve.Fori(0, job.steps) as i:
                        for b in range(2):
                            dve.wait_ge(w_hi_done, chunk0 + 2 * i + b + 1)
                            w_free(dve, job, result0, least, i, b)
                            dve.tensor_tensor(wlo[b][:, 0:job.kc, :], raw[b][:, 0:job.kc, :],
                                              whi[b][:, 0:job.kc, :].bitcast(F32), ALU.subtract).then_inc(w_lo_done, 1)

            @block.gpsimd
            def _(pool):
                pool.sem_inc(taken, FREE_PS)
                pool.sem_inc(products, FREE_W)

            @block.tensor
            def _(pe):
                for job, chunk0, result0, least in plan():
                    with pe.Fori(0, job.steps) as i:
                        for b in range(2):
                            pe.wait_ge(w_lo_done, FREE_RAW + chunk0 + 2 * i + b + 1)
                            for n in range(job.results):
                                q = b * job.results + n
                                pe.wait_ge(taken, result0 - FREE_W + 2 * job.results * i + q + 1)
                                ps = k.pv[q % 2]
                                if job.turned:
                                    for h in range(2):
                                        ins = mm3(pe, ps[:, h, 0:HALF], job.kc,
                                                  lambda x, c: x[:, c, n * P:(n + 1) * P], whi[b], wlo[b],
                                                  lambda x, c: x[:, c, h * HALF:(h + 1) * HALF], job.hi, job.lo)
                                else:
                                    r = ROWS[n]
                                    ins = mm3(pe, ps[0:r, 0, 0:WCOLS], job.kc,
                                              lambda x, c: x[:, c, n * P:n * P + r], job.hi, job.lo,
                                              lambda x, c: x[:, c, :], whi[b], wlo[b])
                                ins.then_inc(products, 1)


def mm3(pe, out, kc, left, lhi, llo, right, rhi, rlo):
    for c in range(kc):
        pe.matmul(out, left(llo, c), right(rhi, c), start=(c == 0), stop=False)
        pe.matmul(out, left(lhi, c), right(rlo, c), start=False, stop=False)
        ins = pe.matmul(out, left(lhi, c), right(rhi, c), start=False, stop=(c == kc - 1))
    return ins


class Side:

    def __init__(self, k, name, tiles, w_in, hi, lo, dram, ctx):
        self.k, self.tiles, self.w, self.hi, self.lo, self.dram = k, tiles, w_in, hi, lo, dram
        two = range(2)
        sb = lambda n, s, dt=F32: [k.sb(f"{name}_{n}{b}", s, dt, ctx) for b in two]
        self.raw, self.w_hi, self.w_lo = sb("w_raw", [P, DC, P]), sb("w_hi", [P, DC, P], F32R), sb("w_lo", [P, DC, P], F32R)
        self.result = sb("result", [P, 1, T])
        self.loaded, self.stored = ([k.sem(f"{name}_{n}{b}") for b in two] for n in ("side_loaded", "side_stored"))
        self.rounded, self.split, self.products, self.taken = (k.sem(f"{name}_side_{n}") for n in
            ("rounded", "split", "products", "taken"))
        self.quarter = 0

    def on_sync(self, sp):
        def load(n):
            wait(sp, self.split, n - 1)
            sp.dma_start(self.raw[n % 2][:, :, :],
                         columns(self.w, side_column(self.tiles[n]), P)).then_inc(self.loaded[n % 2], 16)

        load(0)
        load(1)
        for n, tile in enumerate(self.tiles):
            if n + 2 < len(self.tiles):
                load(n + 2)
            sp.wait_ge(self.taken, 2 * n + 2)
            sp.dma_start(self.dram[:, tile:tile + 1, :], self.result[n % 2][:, :, :]).then_inc(self.stored[n % 2], 16)
        for b in range(2):
            sp.wait_ge(self.stored[b], 16 * ((len(self.tiles) + 1 - b) // 2))

    def on_gpsimd(self, pool):
        for n in range(len(self.tiles)):
            pool.wait_ge(self.rounded, n + 1)
            pool.tensor_tensor(self.w_lo[n % 2][:, :, :], self.raw[n % 2][:, :, :],
                               self.w_hi[n % 2][:, :, :].bitcast(F32), ALU.subtract).then_inc(self.split, 1)

    def quarters(self, pe, count):
        for _ in range(count):
            q, part = divmod(self.quarter, 2)
            n, h = divmod(q, 2)
            ts = slice(h * HALF, (h + 1) * HALF)
            out = self.k.pb[6 + h][:, 0:HALF]
            if part == 0:
                pe.wait_ge(self.split, n + 1)
                wait(pe, self.taken, q - 1)
            for c in range(4 * part, 4 * part + 4):
                pe.matmul(out, self.w_lo[n % 2][:, c, :], self.hi[:, c, ts], start=(c == 0), stop=False)
                pe.matmul(out, self.w_hi[n % 2][:, c, :], self.lo[:, c, ts], start=False, stop=False)
                ins = pe.matmul(out, self.w_hi[n % 2][:, c, :], self.hi[:, c, ts], start=False, stop=(c == DC - 1))
            if part == 1:
                ins.then_inc(self.products, 1)
            self.quarter += 1

    def round(self, act, n):
        if n < len(self.tiles):
            act.wait_ge(self.loaded[n % 2], 16 * (n // 2 + 1))
            wait(act, self.products, 2 * n - 2)
            act.activation(self.w_hi[n % 2][:, :, :], self.raw[n % 2][:, :, :], ACT.Copy).then_inc(self.rounded, 1)

    def take(self, act, q):
        n, h = divmod(q, 2)
        act.wait_ge(self.products, q + 1)
        if h == 1:
            self.round(act, n + 2)
        wait(act, self.stored[n % 2], 16 * (n // 2))
        act.activation(self.result[n % 2][:, 0, h * HALF:(h + 1) * HALF], self.k.pb[6 + h][:, 0:HALF],
                       ACT.Copy).then_inc(self.taken, 1)


def side_column(tile):
    return COL_QK_B + tile * P if tile < 2 * H else COL_SEL_A + (tile - 2 * H) * P


def columns(w, c0, n):
    return w.rearrange("(c p) n -> p c n", p=P)[:, :, c0:c0 + n]


def to_channels(dst, stride, off=0):
    d = dst[:, :, :].rearrange("p c t -> p (c t)")
    return lambda i, q: d[:, ds((4 * i + q) * stride + off, T)].rearrange("p (h t) -> p h t", h=2)


def to_tokens(dst, width):
    d = dst[:, :, :].rearrange("p t c -> p (t c)")
    return lambda i, b, n: d[0:ROWS[n], ds((2 * i + b) * WCOLS + n * width, WCOLS)]


@phase
def small_projection(k, pre, hi, lo, beta, logd):
    nc = k.nc
    n = 2 * H
    with ExitStack() as ctx:
        whi = k.sb("ba_whi", [P, DC, n], F32R, ctx)
        wlo = k.sb("ba_wlo", [P, DC, n], F32R, ctx)
        ba = k.sb("ba", [P, NT, n], F32, ctx)
        z = k.sb("dec_z", [P, NT, H], F32, ctx)
        m = k.sb("dec_m", [P, NT, H], F32, ctx)
        split, product = k.sem("ba_split"), k.sem("ba_product")
        dve_own, act_own, z_done, ln_done = (k.sem("dec_" + n) for n in ("dve_own", "act_own", "z_done", "ln_done"))
        bc = lambda v, r, n: v[0:r, :].unsqueeze(1).to_broadcast([r, n, H])
        parts = [(P, slice(0, 4)), (NS, slice(4, 5))]
        with nc.Block() as block:
            @block.vector
            def _(dve):
                own = Own(dve, dve_own)
                fence(dve, dve.tensor_copy(whi[:, :, :], k.ba_w[:, :, :]), split, 1)
                dve.tensor_tensor(wlo[:, :, :], k.ba_w[:, :, :], whi[:, :, :].bitcast(F32), ALU.subtract).then_inc(split, 1)
                own.fence(dve.memset(pre[:, :, 0:PAD], 0.0))
                dve.wait_ge(product, 1)
                own.fence(dve.tensor_copy(ba[:, 0:4, :], k.pb[0][:, 0:4 * n].rearrange("p (t c) -> p t c", c=n)))
                own.fence(dve.tensor_copy(ba[0:NS, 4, :], k.pb[1][0:NS, 0:n]))
                for r, ts in parts:
                    w = ts.stop - ts.start
                    own.fence(dve.tensor_tensor(z[0:r, ts, :], ba[0:r, ts, H:2 * H], bc(k.dtb, r, w), ALU.add))
                    own.fence(dve.tensor_scalar(m[0:r, ts, :], z[0:r, ts, :], -1.0, None, ALU.mult))
                    own.fence(dve.tensor_tensor(m[0:r, ts, :], m[0:r, ts, :], z[0:r, ts, :], ALU.min))
                    dve.tensor_scalar(z[0:r, ts, :], z[0:r, ts, :], 0.0, None, ALU.max).then_inc(z_done, 1)
                dve.wait_ge(z_done, 2)
                dve.wait_ge(ln_done, 2)
                for r, ts in parts:
                    w = ts.stop - ts.start
                    own.fence(dve.tensor_tensor(z[0:r, ts, :], z[0:r, ts, :], m[0:r, ts, :], ALU.add))
                    own.fence(dve.scalar_tensor_tensor(logd[0:r, ts, :], z[0:r, ts, :], -1.0, bc(k.a_neg, r, w),
                                                       ALU.mult, ALU.mult))

            @block.scalar
            def _(act):
                own = Own(act, act_own)
                act.wait_ge(z_done, 2)
                for r, ts in parts:
                    act.activation(beta[0:r, ts, :], ba[0:r, ts, 0:H], ACT.Sigmoid)
                for r, ts in parts:
                    own.fence(act.activation(m[0:r, ts, :], m[0:r, ts, :], ACT.Exp))
                for r, ts in parts:
                    act.activation(m[0:r, ts, :], m[0:r, ts, :], ACT.Ln, bias=1.0).then_inc(ln_done, 1)
                act.wait_ge(ln_done, 2)

            @block.tensor
            def _(pe):
                pe.wait_ge(split, 2)
                for t, r in enumerate(ROWS):
                    out = k.pb[0][:, t * n:(t + 1) * n] if t < 4 else k.pb[1][0:r, 0:n]
                    ins = mm3(pe, out, DC, lambda x, c: x[:, c, t * P:t * P + r], hi, lo,
                              lambda x, c: x[:, c, :], whi, wlo)
                ins.then_inc(product, 1)


@phase
def convolve(k, a, o, pre, k_tok, v_tok, hi, lo, side_dram):
    nc = k.nc
    conv_w = k.vecs[:, 2 * DC:].rearrange("p (i c) -> p i c", c=CT)
    n_st = NS * PAD
    with ExitStack() as ctx:
        st = k.sb("conv_st", [n_st, CONV_CH], F32, ctx)
        stt = k.sb("conv_stt", [P, CT, NS, PAD], F32, ctx)
        taps = k.sb("conv_taps", [P, 2, NP_TOK], F32, ctx)
        samp = k.sb("conv_samp", [P, CT, NS], F32, ctx)
        part = k.sb("conv_part", [P, CT, NS], F32, ctx)
        sq = k.sb("l2_sq", [P, 2, T], F32, ctx)
        rn = k.sb("l2_rn", [P, 2, T], F32, ctx)
        last = k.sb("conv_last", [PAD + NS, CONV_CH], F32, ctx)
        loaded, st_turned, dve_own = k.sem("conv_loaded"), k.sem("conv_st_turned"), k.sem("conv_dve_own")
        conv_done, silu_done = k.sem("conv_done"), k.sem("silu_done")
        squared, summed, rooted = k.sem("l2_squared"), k.sem("l2_summed"), k.sem("l2_rooted")
        normed, tails = k.sem("l2_normed"), k.sem("conv_tails")
        tails_copied, stored = k.sem("conv_tails_copied"), k.sem("conv_stored")
        turned, copied = k.sem("kv_turned"), k.sem("kv_copied")
        side = Side(k, "cv", range(SIDE_CONV), a["w_in"][0], hi, lo, side_dram, ctx)
        FIRST = 16

        with nc.Block() as block:
            @block.sync
            def _(sp):
                sp.dma_start(st[:, :], a["state_conv_a"][0].rearrange("b i c -> (b i) c")).then_inc(loaded, 16)
                sp.dma_start(o["conv_s"][0, :, 0:PAD - 1, :], a["state_conv_a"][0, :, 1:PAD, :]).then_inc(stored, 16)
                sp.wait_ge(tails_copied, 1)
                sp.dma_start(o["conv_p"][0, 0], last[0:PAD, :]).then_inc(stored, 16)
                sp.dma_start(o["conv_s"][0, :, PAD - 1, :], last[PAD:PAD + NS, :]).then_inc(stored, 16)
                side.on_sync(sp)
                sp.wait_ge(stored, 48)

            @block.gpsimd
            def _(pool):
                side.on_gpsimd(pool)

            @block.tensor
            def _(pe):
                pe.wait_ge(loaded, 16)
                for c in range(CT):
                    ins = pe.transpose(k.pb[0][:, c * n_st:(c + 1) * n_st], st[:, c * P:(c + 1) * P],
                                       k.eye[0:n_st, 0:n_st])
                ins.then_inc(st_turned, 1)
                for c in range(CT):
                    ins = pe.transpose(k.pb[1 + c // 4][0:PAD + NS, (c % 4) * P:(c % 4 + 1) * P],
                                       pre[:, c, NP_TOK:NP_TOK + PAD + NS], k.eye[:, :])
                ins.then_inc(tails, 1)
                side.quarters(pe, 2 * FIRST)
                for n in range(2 * H):
                    pe.wait_ge(squared, n + 1)
                    if n >= 2:
                        pe.wait_ge(rooted, n - 1)
                    for h in range(2):
                        ins = pe.matmul(k.pv[1 + n % 2][:, h, 0:HALF], k.ones[:, :],
                                        sq[:, n % 2, h * HALF:(h + 1) * HALF], start=True, stop=True)
                    ins.then_inc(summed, 1)
                    side.quarters(pe, 1)
                pe.wait_ge(silu_done, CT + 1)
                pe.wait_ge(normed, 2 * H)
                for q in range(2 * NT):
                    t, r, ch = q // 2, ROWS[q // 2], (H, 2 * H)[q % 2]
                    if q >= 2:
                        pe.wait_ge(copied, q - 1)
                    for h in range(H):
                        ins = pe.transpose(k.pb[q % 2][0:r, h * P:(h + 1) * P],
                                           pre[:, ch + h, t * P:t * P + r], k.eye[:, :])
                    ins.then_inc(turned, 1)

            def divide(dve, own, n):
                dve.wait_ge(rooted, n + 1)
                own.fence(dve.reciprocal(rn[:, n % 2, :], rn[:, n % 2, :]))
                if n < H:
                    dve.scalar_tensor_tensor(pre[:, n, 0:T], pre[:, n, 0:T], DK ** -0.5, rn[:, n % 2, :],
                                             ALU.mult, ALU.mult).then_inc(normed, 1)
                else:
                    dve.tensor_tensor(pre[:, n, 0:T], pre[:, n, 0:T], rn[:, n % 2, :], ALU.mult).then_inc(normed, 1)

            @block.vector
            def _(dve):
                own = Own(dve, dve_own)
                dve.wait_ge(st_turned, 1)
                own.fence(dve.tensor_copy(stt[:, :, :, :].rearrange("p c b i -> p (c b i)"), k.pb[0][:, 0:CT * n_st]))
                for i in range(CONV_W):
                    x = stt[:, :, :, i] if i < PAD else pre[:, :, PAD + NP_TOK:PAD + T]
                    w = conv_w[:, i, :].unsqueeze(2).to_broadcast([P, CT, NS])
                    if i == 0:
                        own.fence(dve.tensor_tensor(samp[:, :, :], x, w, ALU.mult))
                    else:
                        own.fence(dve.tensor_tensor(part[:, :, :], x, w, ALU.mult))
                        own.fence(dve.tensor_tensor(samp[:, :, :], samp[:, :, :], part[:, :, :], ALU.add))
                dve.wait_ge(tails, 1)
                for c in range(3):
                    ins = dve.tensor_copy(last[:, c * 4 * P:(c + 1) * 4 * P], k.pb[1 + c][0:PAD + NS, :])
                ins.then_inc(tails_copied, 1)
                for c in range(CT):
                    if c >= 2:
                        dve.wait_ge(silu_done, c - 1)
                    y = taps[:, c % 2, :]
                    own.fence(dve.tensor_scalar(y, pre[:, c, 0:NP_TOK], conv_w[:, 0, c:c + 1], None, ALU.mult))
                    for i in range(1, CONV_W):
                        ins = dve.scalar_tensor_tensor(y, pre[:, c, i:i + NP_TOK], conv_w[:, i, c:c + 1], y,
                                                       ALU.mult, ALU.add)
                        if i < PAD:
                            own.fence(ins)
                        else:
                            ins.then_inc(conv_done, 1)
                dve.wait_ge(silu_done, CT + 1)
                for n in range(2 * H):
                    divide(dve, own, n)
                dve.wait_ge(normed, 2 * H)

            @block.scalar
            def _(act):
                side.round(act, 0)
                side.round(act, 1)
                act.wait_ge(tails_copied, 1)
                for c in range(CT):
                    act.wait_ge(conv_done, c + 1)
                    act.activation(pre[:, c, 0:NP_TOK], taps[:, c % 2, :], ACT.Silu).then_inc(silu_done, 1)
                    side.take(act, c)
                act.wait_ge(silu_done, CT)
                act.activation(pre[:, :, NP_TOK:T], samp[:, :, :], ACT.Silu).then_inc(silu_done, 1)
                act.wait_ge(silu_done, CT + 1)
                for q in range(CT, FIRST):
                    side.take(act, q)
                for n in range(2 * H + 1):
                    if n < 2 * H:
                        if n >= 2:
                            act.wait_ge(summed, n - 1)
                        act.activation(sq[:, n % 2, :], pre[:, n, 0:T], ACT.Square).then_inc(squared, 1)
                    if n == 0:
                        continue
                    m = n - 1
                    act.wait_ge(summed, m + 1)
                    if m >= 2:
                        act.wait_ge(normed, m - 1)
                    act.activation(rn[:, m % 2, :].rearrange("p (h t) -> p h t", h=2),
                                   k.pv[1 + m % 2][:, :, 0:HALF], ACT.Sqrt, bias=k.eps[:, :]).then_inc(rooted, 1)
                    if m % 2 == 1:
                        side.take(act, FIRST + m // 2)
                for q in range(2 * NT):
                    r = ROWS[q // 2]
                    act.wait_ge(turned, q + 1)
                    act.activation((k_tok, v_tok)[q % 2][0:r, q // 2, :], k.pb[q % 2][0:r, :], ACT.Copy).then_inc(copied, 1)
                act.wait_ge(copied, 2 * NT)


def head_bc(v, r, width):
    return v.unsqueeze(2).to_broadcast([r, v.shape[1], width])


@phase
def delta_prompt(k, a, o, pre, k_tok, v_tok, beta, logd, hi, lo, side_dram):
    nc = k.nc
    NCH = 4
    with ExitStack() as ctx:
        masks = k.sb("masks", [P, LEVELS, P], F32, ctx)
        LT = k.sb("LT", [P, NCH, H, P], F32, ctx)
        X = k.sb("X", [P, NCH, H, P], F32, ctx)
        XT = k.sb("XT", [P, NCH, H, P], F32, ctx)
        QK = k.sb("QK", [P, NCH, H, P], F32, ctx)
        kbg = k.sb("kbg", [P, NCH, H, P], F32, ctx)
        B = k.sb("B", [P, 2, H, P], F32, ctx)
        Y = k.sb("Y", [P, 2, H, P], F32, ctx)
        dec = k.sb("dec", [P, H, P], F32, ctx)
        eg = k.sb("eg", [P, H, P], F32, ctx)
        G = k.sb("G", [P, NCH, H], F32, ctx)
        bg = k.sb("bg", [P, NCH, H], F32, ctx)
        kdg = k.sb("kdg", [P, NCH, H], F32, ctx)
        gC = k.sb("gC", [P, NCH, H], F32, ctx)
        S = k.sb("S_delta", [P, H, P], F32, ctx)
        vn = k.sb("vn", [P, H, P], F32, ctx)
        loaded, dve_own, act_own = k.sem("dp_loaded"), k.sem("dp_dve_own"), k.sem("dp_act_own")
        g_sum, g_copied, prep, dec_in, dec_out, prep_done = (k.sem("dp_" + n) for n in
            ("g_sum", "g_copied", "prep", "dec_in", "dec_out", "prep_done"))
        b_done, y_mm, y_done, z_mm, x_done, uw_mm, uw_done = (k.sem("dp_" + n) for n in
            ("b_done", "y_mm", "y_done", "z_mm", "x_done", "uw_mm", "uw_done"))
        ws_mm, vn_done, os_mm, s_done, o_done, stored, scaled = (k.sem("dp_" + n) for n in
            ("ws_mm", "vn_done", "os_mm", "s_done", "o_done", "stored", "scaled"))
        kd_done = k.sem("dp_kd_done")
        side = Side(k, "dp", range(SIDE_CONV, SIDE), a["w_in"][0], hi, lo, side_dram, ctx)
        bank = lambda n: k.pb[n].rearrange("p (h t) -> p h t", h=H)
        tok = lambda x, t: x[:, t, :].rearrange("p (h e) -> p h e", h=H)
        with nc.Block() as block:
            @block.sync
            def _(sp):
                sp.dma_start(masks[:, :, :], a["c_masks"].rearrange("p (l t) -> p l t", l=LEVELS)).then_inc(loaded, 16)
                side.on_sync(sp)
                sp.wait_ge(s_done, NCH)
                sp.dma_start(o["delta_p"][0, 0].rearrange("h k v -> k h v"), S[:, :, :]).then_inc(stored, 16)
                sp.wait_ge(stored, 16)

            @block.gpsimd
            def _(pool):
                side.on_gpsimd(pool)

            @block.tensor
            def _(pe):
                for t in range(NCH):
                    ins = pe.matmul(k.pb[4][:, t * H:(t + 1) * H], k.upto, logd[:, t, :], start=True, stop=True)
                ins.then_inc(g_sum, 1)
                for t in range(NCH):
                    if t >= 1:
                        pe.wait_ge(prep_done, t)
                    if t == 0:
                        pe.wait_ge(g_copied, 1)
                    c = slice(t * P, (t + 1) * P)
                    for h in range(H):
                        hs = slice(h * P, (h + 1) * P)
                        kc = pre[:, H + h, c]
                        pe.matmul(k.pb[0][:, hs], logd[:, t, h:h + 1].to_broadcast([P, P]), k.upto, start=True, stop=True)
                        pe.matmul(k.pb[1][:, hs], beta[:, t, h:h + 1].to_broadcast([P, P]), k.eye, start=True, stop=True)
                        pe.matmul(k.pb[2][:, hs], kc, kc, start=True, stop=True)
                        ins = pe.matmul(k.pb[3][:, hs], kc, pre[:, h, c], start=True, stop=True)
                    ins.then_inc(prep, 1)
                    if t:
                        side.quarters(pe, 2)
                pe.wait_ge(prep_done, NCH)
                n = 0
                for l in range(LEVELS):
                    for t in range(NCH):
                        if l == 0:
                            if n >= 2:
                                pe.wait_ge(x_done, n - 1)
                            pe.wait_ge(b_done, n + 1)
                            for h in range(H):
                                ins = pe.matmul(bank(1 + 2 * (n % 2))[:, h, :], B[:, n % 2, h, :], k.eye,
                                                start=True, stop=True)
                            ins.then_inc(z_mm, 1)
                            if t < 2:
                                side.quarters(pe, 1)
                        else:
                            pe.wait_ge(b_done, n + 1)
                            pe.wait_ge(x_done, n - NCH + 1)
                            if n - NCH >= 2:
                                pe.wait_ge(y_done, n - NCH - 1)
                            for h in range(H):
                                ins = pe.matmul(bank(4 + n % 2)[:, h, :], B[:, n % 2, h, :], X[:, t, h, :],
                                                start=True, stop=True)
                            ins.then_inc(y_mm, 1)
                            side.quarters(pe, 1)
                            pe.wait_ge(y_done, n - NCH + 1)
                            pe.wait_ge(x_done, n - 1)
                            for h in range(H):
                                ins = pe.matmul(bank(2 * (n % 2))[:, h, :], Y[:, n % 2, h, :], XT[:, t, h, :],
                                                start=True, stop=True)
                                if l < LEVELS - 1:
                                    ins = pe.matmul(bank(1 + 2 * (n % 2))[:, h, :], XT[:, t, h, :], Y[:, n % 2, h, :],
                                                    start=True, stop=True)
                            ins.then_inc(z_mm, 1)
                            side.quarters(pe, 1)
                        n += 1
                pe.wait_ge(x_done, n)
                pe.wait_ge(scaled, NCH)
                for t in range(NCH):
                    if t >= 1:
                        pe.wait_ge(uw_done, 2 * t)
                    for h in range(H):
                        pe.matmul(bank(2)[:, h, :], XT[:, t, h, :], tok(v_tok, t)[:, h, :], start=True, stop=True)
                        ins = pe.matmul(bank(3)[:, h, :], kbg[:, t, h, :], XT[:, t, h, :], start=True, stop=True)
                    ins.then_inc(uw_mm, 1)
                pe.wait_ge(uw_done, 2 * NCH)
                pe.wait_ge(kd_done, NCH)
                for t in range(NCH):
                    c = slice(t * P, (t + 1) * P)
                    if t:
                        pe.wait_ge(s_done, t)
                        for h in range(H):
                            ins = pe.matmul(bank(4)[:, h, :], LT[:, t, h, :], S[:, h, :], start=True, stop=True)
                        ins.then_inc(ws_mm, 1)
                        pe.wait_ge(vn_done, t)
                        pe.wait_ge(o_done, t)
                    v = lambda h: vn[:, h, :] if t else X[:, 0, h, :]
                    for h in range(H):
                        if t:
                            pe.matmul(bank(5)[:, h, :], pre[:, h, c], S[:, h, :], start=True, stop=False)
                        pe.matmul(bank(5)[:, h, :], QK[:, t, h, :], v(h), start=not t, stop=True)
                        ins = pe.matmul(bank(0)[:, h, :], tok(k_tok, t)[:, h, :], v(h), start=True, stop=True)
                    ins.then_inc(os_mm, 1)

            @block.scalar
            def _(act):
                own = Own(act, act_own)
                act.wait_ge(g_copied, 1)
                act.activation(bg[:, :, :], G[:, :, :], ACT.Exp).then_inc(dec_out, 1)
                for t in range(NCH):
                    act.wait_ge(prep, t + 1)
                    if t >= 1:
                        act.wait_ge(prep_done, t)
                    act.activation(eg[:, :, :], bank(0), ACT.Exp).then_inc(dec_out, 1)
                    act.wait_ge(dec_in, t + 1)
                    act.activation(dec[:, :, :], dec[:, :, :], ACT.Exp).then_inc(dec_out, 1)
                    if t == 0:
                        side.round(act, 0)
                        side.round(act, 1)
                    else:
                        side.take(act, t - 1)
                act.wait_ge(prep_done, NCH)
                act.activation(kdg[:, :, :], kdg[:, :, :], ACT.Exp).then_inc(dec_out, 1)
                n = 0
                for l in range(1, LEVELS):
                    for t in range(NCH):
                        act.wait_ge(y_mm, n + 1)
                        if n >= 2:
                            act.wait_ge(z_mm, NCH + n - 1)
                        act.activation(Y[:, n % 2, :, :], bank(4 + n % 2), ACT.Copy).then_inc(y_done, 1)
                        side.take(act, NCH - 1 + n)
                        n += 1
                side.take(act, NCH - 1 + n)
                act.wait_ge(x_done, LEVELS * NCH)
                for t in range(NCH):
                    act.wait_ge(uw_mm, t + 1)
                    act.activation(X[:, t, :, :], bank(2), ACT.Copy).then_inc(uw_done, 1)
                    act.wait_ge(uw_done, 2 * t + 1)
                    act.activation(LT[:, t, :, :], bank(3), ACT.Copy).then_inc(uw_done, 1)
                for t in range(NCH):
                    act.wait_ge(os_mm, t + 1)
                    act.activation(tok(v_tok, t), bank(5), ACT.Copy).then_inc(o_done, 1)
                act.wait_ge(o_done, NCH)

            @block.vector
            def _(dve):
                own = Own(dve, dve_own)
                dve.wait_ge(g_sum, 1)
                fence(dve, dve.tensor_copy(G[:, :, :].rearrange("p t h -> p (t h)"), k.pb[4][:, 0:NCH * H]), g_copied, 1)
                for t in range(NCH):
                    c = slice(t * P, (t + 1) * P)
                    dve.wait_ge(dec_out, 2 * t + 2)
                    dve.tensor_copy(gC[:, t, :], eg[:, :, P - 1])
                    own.fence(dve.tensor_tensor(dec[:, :, :], bank(0), head_bc(G[:, t, :], P, P), ALU.subtract))
                    dve.tensor_tensor(dec[:, :, :], dec[:, :, :], k.neg.unsqueeze(1).to_broadcast([P, H, P]),
                                      ALU.add).then_inc(dec_in, 1)
                    own.fence(dve.tensor_tensor(kdg[:, t, :], bank(0)[:, :, P - 1], G[:, t, :], ALU.subtract))
                    dve.wait_ge(dec_out, 2 * t + 3)
                    own.fence(dve.tensor_tensor(LT[:, t, :, :], bank(2), dec[:, :, :], ALU.mult))
                    own.fence(dve.tensor_tensor(LT[:, t, :, :], LT[:, t, :, :], bank(1), ALU.mult))
                    own.fence(dve.tensor_tensor(pre[:, 0:H, c], pre[:, 0:H, c], eg[:, :, :], ALU.mult))
                    fence(dve, dve.tensor_tensor(QK[:, t, :, :], bank(3), dec[:, :, :], ALU.mult), prep_done, t + 1)
                dve.wait_ge(prep_done, NCH)
                own.fence(dve.tensor_tensor(bg[:, :, :], bg[:, :, :], beta[:, 0:NCH, :], ALU.mult))
                dve.wait_ge(loaded, 16)
                n = 0
                for l in range(LEVELS):
                    def coupled(n):
                        if n >= 2:
                            dve.wait_ge(z_mm, n - 1)
                        dve.tensor_tensor(B[:, n % 2, :, :], LT[:, n % NCH, :, :],
                                          masks[:, n // NCH, :].unsqueeze(1).to_broadcast([P, H, P]),
                                          ALU.mult).then_inc(b_done, 1)
                    for t in range(NCH):
                        if n == 0:
                            coupled(0)
                        if n + 1 < LEVELS * NCH:
                            coupled(n + 1)
                        dve.wait_ge(z_mm, n + 1)
                        eye_h = k.eye.unsqueeze(1).to_broadcast([P, H, P])
                        if l == 0:
                            own.fence(dve.tensor_tensor(XT[:, t, :, :], eye_h, B[:, n % 2, :, :], ALU.subtract))
                            dve.tensor_tensor(X[:, t, :, :], eye_h, bank(1 + 2 * (n % 2)), ALU.subtract).then_inc(x_done, 1)
                        elif l == LEVELS - 1:
                            dve.tensor_tensor(XT[:, t, :, :], XT[:, t, :, :], bank(2 * (n % 2)), ALU.subtract).then_inc(x_done, 1)
                        else:
                            own.fence(dve.tensor_tensor(XT[:, t, :, :], XT[:, t, :, :], bank(2 * (n % 2)), ALU.subtract))
                            dve.tensor_tensor(X[:, t, :, :], X[:, t, :, :], bank(1 + 2 * (n % 2)), ALU.subtract).then_inc(x_done, 1)
                        n += 1
                        if n == 1:
                            for u in range(NCH):
                                own.fence(dve.tensor_tensor(tok(v_tok, u), tok(v_tok, u), head_bc(beta[:, u, :], P, P), ALU.mult))
                                dve.tensor_tensor(kbg[:, u, :, :], tok(k_tok, u), head_bc(bg[:, u, :], P, P),
                                                  ALU.mult).then_inc(scaled, 1)
                            dve.wait_ge(scaled, NCH)
                dve.wait_ge(dec_out, 2 * NCH + 2)
                for u in range(NCH):
                    dve.tensor_tensor(tok(k_tok, u), tok(k_tok, u), head_bc(kdg[:, u, :], P, P),
                                      ALU.mult).then_inc(kd_done, 1)
                dve.wait_ge(uw_done, 2 * NCH)
                for t in range(NCH):
                    if t:
                        dve.wait_ge(ws_mm, t)
                        dve.tensor_tensor(vn[:, :, :], X[:, t, :, :], bank(4), ALU.subtract).then_inc(vn_done, 1)
                    dve.wait_ge(os_mm, t + 1)
                    if t:
                        own.fence(dve.tensor_tensor(S[:, :, :], S[:, :, :], head_bc(gC[:, t, :], P, P), ALU.mult))
                        dve.tensor_tensor(S[:, :, :], S[:, :, :], bank(0), ALU.add).then_inc(s_done, 1)
                    else:
                        dve.tensor_copy(S[:, :, :], bank(0)).then_inc(s_done, 1)
                    dve.wait_ge(s_done, t + 1)


@phase
def delta_sample(k, a, o, pre, v_tok, beta, logd):
    nc = k.nc
    BH = NS * H
    with ExitStack() as ctx:
        S = k.sb("S_ds", [P, NS, H, P], F32, ctx)
        bgs = k.sb("ds_bg", [NS, 2, NS, H], F32, ctx)
        bg = k.sb("ds_bgbc", [P, 2, NS, H], F32, ctx)
        eg = k.sb("ds_eg", [NS, H], F32, ctx)
        kb = k.sb("ds_kb", [P, NS, H], F32, ctx)
        qm = k.sb("ds_qm", [P, H, NS, NS], F32, ctx)
        dlt = k.sb("ds_dlt", [P, 2, H, P], F32, ctx)
        loaded, own_s, e_done, spread, sums, ready, kv, upd, dv, omm, stored, taken = (k.sem("ds_" + n) for n in
            ("loaded", "own", "e_done", "spread", "sums", "ready", "kv", "upd", "dv", "omm", "stored", "taken"))
        ch = lambda c: pre[:, c:c + H, NP_TOK:T]
        with nc.Block() as block:
            @block.sync
            def _(sp):
                sp.dma_start(S[:, :, :, :].rearrange("p b h v -> p (b h) v"),
                             a["state_delta"][0].rearrange("b h k v -> k (b h) v")).then_inc(loaded, 16)
                sp.wait_ge(upd, NS)
                sp.dma_start(o["delta_s"][0].rearrange("b h k v -> k (b h) v"),
                             S[:, :, :, :].rearrange("p b h v -> p (b h) v")).then_inc(stored, 16)
                sp.wait_ge(stored, 16)

            @block.scalar
            def _(act):
                act.activation(eg[:, :], logd[0:NS, 4, :], ACT.Exp).then_inc(e_done, 1)

            @block.vector
            def _(dve):
                own = Own(dve, own_s)
                dve.wait_ge(e_done, 1)
                for n, src in enumerate((eg[:, :], beta[0:NS, 4, :])):
                    ins = dve.tensor_tensor(bgs[:, n, :, :], src.unsqueeze(1).to_broadcast([NS, NS, H]),
                                            k.eye[0:NS, 0:NS].unsqueeze(2).to_broadcast([NS, NS, H]), ALU.mult)
                ins.then_inc(spread, 1)
                dve.wait_ge(sums, 1)
                own.fence(dve.tensor_copy(bg[:, :, :, :].rearrange("p n b h -> p (n b h)"), k.pb[0][:, 0:2 * BH]))
                own.fence(dve.tensor_tensor(kb[:, :, :], ch(H).rearrange("p h b -> p b h"), bg[:, 1, :, :], ALU.mult))
                for h in range(H):
                    own.fence(dve.tensor_tensor(qm[:, h, :, :], pre[:, h, NP_TOK:T].unsqueeze(2).to_broadcast([P, NS, NS]),
                                                k.eye8, ALU.mult))
                dve.wait_ge(loaded, 16)
                for b in range(NS):
                    dve.tensor_tensor(S[:, b, :, :], S[:, b, :, :], head_bc(bg[:, 0, b, :], P, P),
                                      ALU.mult).then_inc(ready, 1)
                for b in range(NS):
                    x = dlt[:, b % 2, :, :]
                    dve.wait_ge(kv, b + 1)
                    ks = k.pb[2 + 2 * (b % 2)].rearrange("p (h e) -> p h e", h=H)
                    vv = k.pb[3 + 2 * (b % 2)].rearrange("p (h e) -> p h e", h=H)
                    own.fence(dve.tensor_copy(x, vv))
                    fence(dve, dve.tensor_tensor(x, x, ks, ALU.subtract), dv, b + 1)
                    own.fence(dve.tensor_tensor(x, x, head_bc(kb[:, b, :], P, P), ALU.mult))
                    fence(dve, dve.tensor_tensor(S[:, b, :, :], S[:, b, :, :], x, ALU.add), upd, b + 1)
                dve.wait_ge(omm, 1)
                fence(dve, dve.tensor_copy(v_tok[0:NS, 4, :], k.pb[1][0:NS, :]), taken, 1)

            @block.tensor
            def _(pe):
                pe.wait_ge(spread, 1)
                pe.matmul(k.pb[0][:, 0:2 * BH], k.ones[0:NS, :], bgs[:, :, :, :].rearrange("p n b h -> p (n b h)"),
                          start=True, stop=True).then_inc(sums, 1)
                for b in range(NS):
                    pe.wait_ge(ready, b + 1)
                    if b >= 2:
                        pe.wait_ge(dv, b - 1)
                    for h in range(H):
                        col = pre[:, H + h, NP_TOK + b:NP_TOK + b + 1].to_broadcast([P, P])
                        pe.matmul(k.pb[2 + 2 * (b % 2)][:, h * P:(h + 1) * P], col, S[:, b, h, :], start=True, stop=True)
                    pe.matmul(k.pb[3 + 2 * (b % 2)], k.eye[0:NS, b:b + 1].to_broadcast([NS, P]), v_tok[0:NS, 4, :],
                              start=True, stop=True).then_inc(kv, 1)
                pe.wait_ge(upd, NS)
                for h in range(H):
                    for b in range(NS):
                        ins = pe.matmul(k.pb[1][0:NS, h * P:(h + 1) * P], qm[:, h, b, :], S[:, b, h, :],
                                        start=(b == 0), stop=(b == NS - 1))
                ins.then_inc(omm, 1)


@phase
def gate_and_turn(k, a, name, o_tok, gate, gn, width, hi, lo):
    nc = k.nc
    W = H * width
    nb = W // 512
    with ExitStack() as ctx:
        g = k.sb(name + "_gain", [P, width], F32, ctx)
        sq = k.sb(name + "_sq", [P, W], F32, ctx)
        ss = k.sb(name + "_ss", [P, NT, H], F32, ctx)
        loaded, gained, own_s, summed, rooted, ready, turned, hi_done, lo_done = (k.sem(name + "_" + n) for n in
            ("loaded", "gained", "own", "summed", "rooted", "ready", "turned", "hi_done", "lo_done"))
        heads = lambda x, t, r: x[0:r, t, :].rearrange("p (h e) -> p h e", h=H)
        with nc.Block() as block:
            @block.sync
            def _(sp):
                sp.dma_start(g[:, :], gn.to_broadcast([P, width])).then_inc(loaded, 16)

            @block.gpsimd
            def _(pool):
                pool.wait_ge(loaded, 16)
                for t, r in enumerate(ROWS):
                    pool.tensor_tensor(heads(gate, t, r), heads(gate, t, r),
                                       g[0:r, :].unsqueeze(1).to_broadcast([r, H, width]), ALU.mult).then_inc(gained, 1)

            @block.vector
            def _(dve):
                own = Own(dve, own_s)
                own.fence(dve.memset(ss[:, :, :], 1.0))
                for t, r in enumerate(ROWS):
                    own.fence(dve.tensor_tensor(sq[0:r, :], o_tok[0:r, t, :], o_tok[0:r, t, :], ALU.mult))
                    own.fence(dve.tensor_reduce(ss[0:r, t, :], sq[0:r, :].rearrange("p (h e) -> p h e", h=H), AX.X, ALU.add))
                dve.sem_inc(summed, 1)
                dve.wait_ge(rooted, 1)
                own.fence(dve.reciprocal(ss[:, :, :], ss[:, :, :]))
                for t, r in enumerate(ROWS):
                    own.fence(dve.tensor_tensor(heads(o_tok, t, r), heads(o_tok, t, r), head_bc(ss[0:r, t, :], r, width), ALU.mult))
                    dve.wait_ge(gained, t + 1)
                    dve.tensor_tensor(o_tok[0:r, t, :], o_tok[0:r, t, :], gate[0:r, t, :], ALU.mult).then_inc(ready, 1)
                q = 0
                for t, r in enumerate(ROWS):
                    for c in range(nb):
                        dve.wait_ge(hi_done, q + 1)
                        cc = slice(4 * c, 4 * c + 4)
                        ps = k.pb[q % 4].rearrange("p (c t) -> p c t", c=4)[:, :, 0:r]
                        dve.tensor_tensor(lo[:, cc, t * P:t * P + r], ps, hi[:, cc, t * P:t * P + r].bitcast(F32),
                                          ALU.subtract).then_inc(lo_done, 1)
                        q += 1
                dve.wait_ge(lo_done, q)

            @block.scalar
            def _(act):
                act.wait_ge(summed, 1)
                act.activation(ss[:, :, :], ss[:, :, :], ACT.Sqrt, scale=1.0 / width, bias=k.eps[:, :]).then_inc(rooted, 1)
                q = 0
                for t, r in enumerate(ROWS):
                    for c in range(nb):
                        act.wait_ge(turned, q + 1)
                        cc = slice(4 * c, 4 * c + 4)
                        act.activation(hi[:, cc, t * P:t * P + r], k.pb[q % 4].rearrange("p (c t) -> p c t", c=4)[:, :, 0:r],
                                       ACT.Copy).then_inc(hi_done, 1)
                        q += 1

            @block.tensor
            def _(pe):
                q = 0
                for t, r in enumerate(ROWS):
                    pe.wait_ge(ready, t + 1)
                    for c in range(nb):
                        if q >= 4:
                            pe.wait_ge(lo_done, q - 3)
                        for n in range(4):
                            ins = pe.transpose(k.pb[q % 4][:, n * P:n * P + r],
                                               o_tok[0:r, t, (4 * c + n) * P:(4 * c + n + 1) * P], k.eye[0:r, 0:r])
                        ins.then_inc(turned, 1)
                        q += 1


@phase
def rotate(k, a, qk_b, kb_tok):
    nc = k.nc
    with ExitStack() as ctx:
        rope = k.sb("rope", [P, 2, T], F32, ctx)
        rot = k.sb("rope_rot", [P, 2, T], F32, ctx)
        loaded, own_s, roped, turned, copied = (k.sem("rope_" + n) for n in ("loaded", "own", "roped", "turned", "copied"))
        with nc.Block() as block:
            @block.sync
            def _(sp):
                sp.dma_start(rope[:, :, :], a["c_rope"].rearrange("p (n t) -> p n t", n=2)).then_inc(loaded, 16)

            @block.vector
            def _(dve):
                own = Own(dve, own_s)
                hh = P // 2
                dve.wait_ge(loaded, 16)
                for n in range(2 * H):
                    x, sc = qk_b[:, n, :], (1.0 if n < H else DK ** -0.5)
                    dve.scalar_tensor_tensor(rot[hh:P, 0, :], qk_b[0:hh, n, :], sc, rope[0:hh, 1, :], ALU.mult, ALU.mult)
                    dve.scalar_tensor_tensor(rot[0:hh, 0, :], qk_b[hh:P, n, :], sc, rope[hh:P, 1, :], ALU.mult, ALU.mult)
                    own.fence(dve.scalar_tensor_tensor(rot[:, 1, :], x, sc, rope[:, 0, :], ALU.mult, ALU.mult))
                    fence(dve, dve.tensor_tensor(x, rot[:, 1, :], rot[:, 0, :], ALU.add), roped, n + 1)
                for t in range(4):
                    dve.wait_ge(turned, t + 1)
                    dve.tensor_tensor(kb_tok[:, t, :].rearrange("p (h d) -> p h d", h=H),
                                      k.pb[t % 2].rearrange("p (h d) -> p h d", h=H), head_bc(k.ret_kdec, P, P),
                                      ALU.mult).then_inc(copied, 1)
                dve.wait_ge(copied, 4)

            @block.tensor
            def _(pe):
                pe.wait_ge(roped, 2 * H)
                for t in range(4):
                    if t >= 2:
                        pe.wait_ge(copied, t - 1)
                    for h in range(H):
                        ins = pe.transpose(k.pb[t % 2][:, h * P:(h + 1) * P], qk_b[:, H + h, t * P:(t + 1) * P], k.eye)
                    ins.then_inc(turned, 1)


@phase
def retention_prompt(k, a, o, qk_b, v_b, kb_tok):
    nc = k.nc
    NCH = 4
    with ExitStack() as ctx:
        A = k.sb("rp_A", [P, 2, H, P], F32, ctx)
        qd = k.sb("rp_qd", [P, 2, H, P], F32, ctx)
        S = k.sb("rp_S", [P, H, DV_B], F32, ctx)
        qk_mm, a_done, own_s, os_mm, s_done, o_done, stored = (k.sem("rp_" + n) for n in
            ("qk_mm", "a_done", "own", "os_mm", "s_done", "o_done", "stored"))
        v = lambda t, h: v_b[:, t, h * DV_B:(h + 1) * DV_B]
        with nc.Block() as block:
            @block.sync
            def _(sp):
                sp.wait_ge(s_done, NCH)
                sp.dma_start(o["ret_p"][0, 0].rearrange("h k v -> k h v"), S[:, :, :]).then_inc(stored, 16)
                sp.wait_ge(stored, 16)

            @block.tensor
            def _(pe):
                def scores(t):
                    if t >= 2:
                        pe.wait_ge(a_done, t - 1)
                    for h in range(H):
                        c = slice(t * P, (t + 1) * P)
                        ins = pe.matmul(k.pb[t % 2][:, h * P:(h + 1) * P], qk_b[:, H + h, c], qk_b[:, h, c], start=True, stop=True)
                    ins.then_inc(qk_mm, 1)

                scores(0)
                for t in range(NCH):
                    if t + 1 < NCH:
                        scores(t + 1)
                    pe.wait_ge(a_done, t + 1)
                    if t:
                        pe.wait_ge(s_done, t)
                        pe.wait_ge(o_done, t)
                    for h in range(H):
                        po = k.pb[4 + h // 2][:, (h % 2) * DV_B:(h % 2 + 1) * DV_B]
                        ps = k.pb[6 + h // 2][:, (h % 2) * DV_B:(h % 2 + 1) * DV_B]
                        if t:
                            pe.matmul(po, qd[:, t % 2, h, :], S[:, h, :], start=True, stop=False)
                        pe.matmul(po, A[:, t % 2, h, :], v(t, h), start=not t, stop=True)
                        ins = pe.matmul(ps, kb_tok[:, t, h * P:(h + 1) * P], v(t, h), start=True, stop=True)
                    ins.then_inc(os_mm, 1)

            @block.vector
            def _(dve):
                own = Own(dve, own_s)
                gC = gammas() ** P

                def prep(t):
                    if t >= 2:
                        dve.wait_ge(os_mm, t - 1)
                    dve.tensor_tensor(qd[:, t % 2, :, :], qk_b[:, 0:H, t * P:(t + 1) * P], k.ret_qdec, ALU.mult)
                    dve.wait_ge(qk_mm, t + 1)
                    dve.tensor_tensor(A[:, t % 2, :, :], k.pb[t % 2].rearrange("p (h i) -> p h i", h=H), k.ret_dec,
                                      ALU.mult).then_inc(a_done, 1)

                prep(0)
                for t in range(NCH):
                    if t + 1 < NCH:
                        prep(t + 1)
                    dve.wait_ge(os_mm, t + 1)
                    for h in range(H):
                        ps = k.pb[6 + h // 2][:, (h % 2) * DV_B:(h % 2 + 1) * DV_B]
                        if t:
                            ins = dve.scalar_tensor_tensor(S[:, h, :], S[:, h, :], float(gC[h]), ps, ALU.mult, ALU.add)
                        else:
                            ins = dve.tensor_copy(S[:, h, :], ps)
                    fence(dve, ins, s_done, t + 1)

            @block.scalar
            def _(act):
                for t in range(NCH):
                    act.wait_ge(os_mm, t + 1)
                    act.activation(v_b[:, t, :].rearrange("p (n e) -> p n e", n=2), k.pv[2][:, :, :], ACT.Copy).then_inc(o_done, 1)
                act.wait_ge(o_done, NCH)


@phase
def retention_sample(k, a, o, qk_b, v_b):
    nc = k.nc
    with ExitStack() as ctx:
        S = k.sb("S_rs", [P, NS, H, DV_B], F32, ctx)
        qm = k.sb("rs_qm", [P, H, NS, NS], F32, ctx)
        x = k.sb("rs_x", [P, 2, H, DV_B], F32, ctx)
        loaded, own_s, vv, upd, xd, omm, stored, taken = (k.sem("rs_" + n) for n in
            ("loaded", "own", "vv", "upd", "xd", "omm", "stored", "taken"))
        with nc.Block() as block:
            @block.sync
            def _(sp):
                sp.dma_start(S[:, :, :, :].rearrange("p b h v -> p (b h) v"),
                             a["state_ret"][0].rearrange("b h k v -> k (b h) v")).then_inc(loaded, 16)
                sp.wait_ge(upd, NS)
                sp.dma_start(o["ret_s"][0].rearrange("b h k v -> k (b h) v"),
                             S[:, :, :, :].rearrange("p b h v -> p (b h) v")).then_inc(stored, 16)
                sp.wait_ge(stored, 16)

            @block.vector
            def _(dve):
                own = Own(dve, own_s)
                gm = gammas()
                for h in range(H):
                    own.fence(dve.tensor_tensor(qm[:, h, :, :], qk_b[:, h, NP_TOK:T].unsqueeze(2).to_broadcast([P, NS, NS]),
                                                k.eye8, ALU.mult))
                dve.wait_ge(loaded, 16)
                for h in range(H):
                    ins = dve.tensor_scalar(S[:, :, h, :], S[:, :, h, :], float(gm[h]), None, ALU.mult)
                own.fence(ins)
                for b in range(NS):
                    dve.wait_ge(vv, b + 1)
                    for n in range(2):
                        kc = head_bc(qk_b[:, H + 2 * n:H + 2 * n + 2, NP_TOK + b], P, DV_B)
                        ins = dve.tensor_tensor(x[:, b % 2, 2 * n:2 * n + 2, :],
                                                k.pv[b % 2][:, n, :].rearrange("p (h e) -> p h e", h=2), kc, ALU.mult)
                    fence(dve, ins, xd, b + 1)
                    fence(dve, dve.tensor_tensor(S[:, b, :, :], S[:, b, :, :], x[:, b % 2, :, :], ALU.add), upd, b + 1)
                dve.wait_ge(omm, 1)
                fence(dve, dve.tensor_copy(v_b[0:NS, 4, :].rearrange("p (n e) -> p n e", n=2), k.pv[2][0:NS, :, :]), taken, 1)

            @block.tensor
            def _(pe):
                for b in range(NS):
                    if b >= 2:
                        pe.wait_ge(xd, b - 1)
                    for n in range(2):
                        ins = pe.matmul(k.pv[b % 2][:, n, :], k.eye[0:NS, b:b + 1].to_broadcast([NS, P]),
                                        v_b[0:NS, 4, n * 512:(n + 1) * 512], start=True, stop=True)
                    ins.then_inc(vv, 1)
                pe.wait_ge(upd, NS)
                for h in range(H):
                    for b in range(NS):
                        ins = pe.matmul(k.pv[2][0:NS, h // 2, (h % 2) * DV_B:(h % 2 + 1) * DV_B], qm[:, h, b, :],
                                        S[:, b, h, :], start=(b == 0), stop=(b == NS - 1))
                ins.then_inc(omm, 1)


@phase
def merge(k, sa, sb_, ba_, bb, hi, lo):
    nc = k.nc
    opened, own_s, hi_s, own_p, summed, lo_done = (k.sem("mg_" + n) for n in
        ("opened", "own", "hi", "pool", "summed", "lo_done"))
    with nc.Block() as block:
        @block.vector
        def _(dve):
            def remainder(c):
                dve.wait_ge(hi_s, c + 1)
                dve.tensor_tensor(lo[:, c, :], sa[:, c, :], hi[:, c, :].bitcast(F32), ALU.subtract).then_inc(lo_done, 1)

            for c in range(DC):
                dve.wait_ge(opened, 2 * c + 1)
                fence(dve, dve.tensor_tensor(sa[:, c, :], sa[:, c, :], ba_[:, c, :], ALU.mult), own_s, c + 1)
                dve.wait_ge(own_p, c + 1)
                dve.tensor_tensor(sa[:, c, :], sa[:, c, :], sb_[:, c, :], ALU.add).then_inc(summed, 1)
                if c:
                    remainder(c - 1)
            remainder(DC - 1)
            dve.wait_ge(lo_done, DC)

        @block.scalar
        def _(act):
            for c in range(DC):
                act.activation(sa[:, c, :], sa[:, c, :], ACT.Sigmoid).then_inc(opened, 1)
                act.activation(sb_[:, c, :], sb_[:, c, :], ACT.Sigmoid).then_inc(opened, 1)
                if c >= 2:
                    act.wait_ge(summed, c - 1)
                    act.activation(hi[:, c - 2, :], sa[:, c - 2, :], ACT.Copy).then_inc(hi_s, 1)
            for c in range(DC - 2, DC):
                act.wait_ge(summed, c + 1)
                act.activation(hi[:, c, :], sa[:, c, :], ACT.Copy).then_inc(hi_s, 1)

        @block.gpsimd
        def _(pool):
            for c in range(DC):
                pool.wait_ge(opened, 2 * c + 2)
                pool.tensor_tensor(sb_[:, c, :], sb_[:, c, :], bb[:, c, :], ALU.mult).then_inc(own_p, 1)


class Activations:

    def __init__(self, k, a, name, first, hi, lo, e_dram, ctx):
        two = range(2)
        self.k, self.first, self.hi, self.lo, self.e_dram = k, first, hi, lo, e_dram
        self.u_dram = a["peer_u"][0].rearrange("(i j) d -> i j d", j=NK)
        sb = lambda n, s, dt=F32: [k.sb(f"{name}_{n}{b}", s, dt, ctx) for b in two]
        self.raw, self.ut = sb("u_raw", [P, 1, D]), sb("ut", [P, DC * P])
        self.ut_hi, self.ut_lo = sb("ut_hi", [P, DC, P], F32R), sb("ut_lo", [P, DC, P], F32R)
        self.gelu = sb("gelu", [P, 1, T])
        self.loaded, self.stored = ([k.sem(f"{name}_{n}{b}") for b in two] for n in ("u_loaded", "e_stored"))
        self.turned, self.read, self.split, self.products, self.done = (k.sem(f"{name}_{n}") for n in
            ("u_turned", "u_read", "u_split", "u_products", "gelu_done"))

    def load(self, sp, n, b):
        wait(sp, self.turned, 2 * n - 2)
        sp.dma_start(self.raw[b][:, :, :], self.u_dram[:, ds(self.first + n, 1), :]).then_inc(self.loaded[b], 16)

    def store(self, sp, n, b):
        sp.wait_ge(self.done, 2 * n + 2)
        sp.dma_start(self.e_dram[:, ds(self.first + n, 1), :], self.gelu[b][:, :, :]).then_inc(self.stored[b], 16)

    def turn(self, pe, n, m, b):
        pe.wait_ge(self.loaded[b], 16 * (m + 1))
        for h in range(2):
            wait(pe, self.read, 2 * n + h - 1)
            for c in range(4):
                ins = pe.transpose(self.k.pb[h][:, c * P:(c + 1) * P],
                                   self.raw[b][:, 0, (4 * h + c) * P:(4 * h + c + 1) * P], self.k.eye)
            ins.then_inc(self.turned, 1)

    def multiply(self, pe, n, b):
        pe.wait_ge(self.split, n + 1)
        for h in range(2):
            wait(pe, self.done, 2 * n + h - 1)
            mm3(pe, self.k.pb[2 + h][:, 0:HALF], DC, lambda x, c: x[:, c, :], self.ut_hi[b], self.ut_lo[b],
                lambda x, c: x[:, c, h * HALF:(h + 1) * HALF], self.hi, self.lo).then_inc(self.products, 1)

    def take(self, act, n, b):
        wait(act, self.products, 2 * n - 2)
        for h in range(2):
            act.wait_ge(self.turned, 2 * n + h + 1)
            act.activation(self.ut_hi[b][:, 4 * h:4 * h + 4, :].rearrange("p c i -> p (c i)"), self.k.pb[h], ACT.Copy)
            act.activation(self.ut[b][:, h * 512:(h + 1) * 512], self.k.pb[h], ACT.Copy).then_inc(self.read, 1)

    def activate(self, act, n, m, b):
        wait(act, self.stored[b], 16 * m)
        for h in range(2):
            act.wait_ge(self.products, 2 * n + h + 1)
            act.activation(self.gelu[b][:, 0, h * HALF:(h + 1) * HALF], self.k.pb[2 + h][:, 0:HALF],
                           ACT.Gelu).then_inc(self.done, 1)

    def remainder(self, pool, n, b):
        pool.wait_ge(self.read, 2 * n + 2)
        pool.tensor_tensor(self.ut_lo[b][:, :, :].rearrange("p c i -> p (c i)"), self.ut[b][:, :],
                           self.ut_hi[b][:, :, :].rearrange("p c i -> p (c i)").bitcast(F32),
                           ALU.subtract).then_inc(self.split, 1)

    def on_tensor(self, pe, s, between=None, last=False):
        for b in range(2):
            if not (last and b):
                self.turn(pe, 2 * s + b + 1, s + b, 1 - b)
            if between is not None:
                between(b)
            self.multiply(pe, 2 * s + b, b)

    def on_scalar(self, act, s, between=None, last=False):
        for b in range(2):
            if not (last and b):
                self.take(act, 2 * s + b + 1, 1 - b)
            if between is not None:
                between(b)
            self.activate(act, 2 * s + b, s, b)

    def on_gpsimd(self, pool):
        self.remainder(pool, 0, 0)
        self.remainder(pool, 1, 1)
        with pool.Fori(1, UT // 2) as s:
            for b in range(2):
                self.remainder(pool, 2 * s + b, b)

    def on_sync(self, sp):
        for n in range(3):
            self.load(sp, n, n % 2)
        with sp.Fori(0, UT // 2 - 2) as s:
            for b in range(2):
                self.load(sp, 2 * s + b + 3, 1 - b)
                self.store(sp, 2 * s + b, b)
        self.load(sp, UT - 1, 1)
        for n in range(UT - 4, UT):
            self.store(sp, n, n % 2)
        for b in range(2):
            sp.wait_ge(self.stored[b], 16 * UT // 2)


@phase
def turn_keys(k, keys, keysT):
    kt, kt_done = k.sem("keys_turned"), k.sem("keys_done")
    with k.nc.Block() as block:
        @block.tensor
        def _(pe):
            for n in range(HP):
                ins = pe.transpose(k.pb[n // 4][:, (n % 4) * P:(n % 4 + 1) * P], keys[:, n, :], k.eye)
                if n % 4 == 3:
                    ins.then_inc(kt, 1)

        @block.scalar
        def _(act):
            for n in range(HP // 4):
                act.wait_ge(kt, n + 1)
                act.activation(keysT[:, 4 * n:4 * n + 4, :].rearrange("p a b -> p (a b)"), k.pb[n],
                               ACT.Copy).then_inc(kt_done, 1)
            act.wait_ge(kt_done, HP // 4)


@phase
def retrieve(k, a, x_hi, x_lo, e_dram, q, keysT, gi, gj, gate_hi, gate_lo):
    nc = k.nc
    HK = PH * TOPK
    SEGMENTS = [8, 6, 6, 6, 6]
    with ExitStack() as ctx:
        ex = Activations(k, a, "ex0", 0, x_hi, x_lo, e_dram, ctx)
        s = k.sb("scores", [P, 2, HP, NK], F32, ctx)
        top = k.sb("top", [P, HP, TOPK], F32, ctx)
        top_i = k.sb("top_i", [P, HP, TOPK], U32, ctx)
        top_f = k.sb("top_f", [P, HP, TOPK], F32, ctx)
        cand = k.sb("cand", [P, PH, TOPK, TOPK], F32, ctx)
        best = k.sb("best", [P, PH, TOPK], F32, ctx)
        sel = k.sb("sel", [P, PH, TOPK], U32, ctx)
        pick = k.sb("pick", [P, 2, HK], U32, ctx)
        pick_f = k.sb("pick_f", [P, 2, HK], F32, ctx)
        hot = k.sb("hot", [P, PH, TOPK, TOPK], F32, ctx)
        res = k.sb("res", [P, 3, HK], F32, ctx)
        tot = k.sb("tot", [P, PH], F32, ctx)
        gate = k.sb("gate", [P, T], F32, ctx)
        s_mm, s_done, own_s, shifted, expd, ready, turned, taken, s_free = (k.sem("rt_" + n) for n in
            ("s_mm", "s_done", "own", "shifted", "expd", "ready", "turned", "taken", "s_free"))
        starts = [sum(SEGMENTS[:t]) for t in range(NT)]
        with nc.Block() as block:
            @block.sync
            def _(sp):
                ex.on_sync(sp)

            @block.gpsimd
            def _(pool):
                ex.on_gpsimd(pool)

            @block.tensor
            def _(pe):
                def scores(t):
                    for n in range(HP):
                        if n % 8 == 0 and t:
                            pe.wait_ge(s_done, 2 * t - 1 + n // 8)
                        if n == 0 and t >= 2:
                            pe.wait_ge(taken, t - 1)
                        r = ROWS[t]
                        ins = pe.matmul(k.pb[4 + n // 4][0:r, (n % 4) * P:(n % 4 + 1) * P], q[:, n, t * P:t * P + r],
                                        keysT[:, n, :], start=True, stop=True)
                        if n % 8 == 7:
                            ins.then_inc(s_mm, 1)

                def turn(t):
                    r = ROWS[t]
                    pe.wait_ge(ready, t + 1)
                    pe.wait_ge(s_done, 2 * min(t + 2, NT))
                    for n in range(3):
                        ins = pe.transpose(k.pb[4][:, n * P:n * P + r], res[0:r, n, :], k.eye[0:r, 0:r])
                    ins.then_inc(turned, 1)

                scores(0)
                scores(1)
                ex.turn(pe, 0, 0, 0)
                ex.on_tensor(pe, 0)
                for t in range(NT):
                    end = starts[t] + SEGMENTS[t]
                    last = t == NT - 1
                    with pe.Fori(max(starts[t], 1), end - last) as s_:
                        ex.on_tensor(pe, s_)
                    if last:
                        ex.on_tensor(pe, end - 1, last=True)
                    turn(t)
                    if t + 2 < NT:
                        scores(t + 2)

            @block.scalar
            def _(act):
                def copy(t):
                    r = ROWS[t]
                    for n in range(2):
                        act.wait_ge(s_mm, 2 * t + n + 1)
                        if t >= 2:
                            act.wait_ge(s_free, t - 1)
                        act.activation(s[0:r, t % 2, 8 * n:8 * n + 8, :].rearrange("p (b a) c -> p b (a c)", b=2),
                                       k.pv[2 + n][0:r, :, :], ACT.Copy).then_inc(s_done, 1)

                copy(0)
                copy(1)
                ex.take(act, 0, 0)
                ex.on_scalar(act, 0)
                for t, r in enumerate(ROWS):
                    end = starts[t] + SEGMENTS[t]
                    with act.Fori(max(starts[t], 1), end - 1) as s_:
                        ex.on_scalar(act, s_)
                    act.wait_ge(shifted, t + 1)
                    act.activation(res[0:r, 2, :].rearrange("p (h k) -> p h k", h=PH), best[0:r, :, :],
                                   ACT.Exp).then_inc(expd, 1)
                    ex.on_scalar(act, end - 1, last=t == NT - 1)
                    if t + 2 < NT:
                        copy(t + 2)

            @block.vector
            def _(dve):
                own = Own(dve, own_s)

                def two_eights(rows, n, vals, idx, src):
                    for half in (slice(0, 8), slice(8, 16)):
                        for m in range(n):
                            ins = dve.max(vals(m)[:, half], src(m))
                        own.fence(ins)
                        for m in range(n):
                            ins = dve.max_index(idx(m)[:, half], vals(m)[:, half], src(m))
                        if half.start == 0:
                            own.fence(ins)
                            for m in range(n):
                                ins = dve.match_replace(src(m), vals(m)[:, half], src(m), LOWEST)
                            own.fence(ins)
                    return ins

                for t, r in enumerate(ROWS):
                    dve.wait_ge(s_done, 2 * t + 2)
                    two_eights(r, HP, lambda m: top[0:r, m, :], lambda m: top_i[0:r, m, :],
                               lambda m: s[0:r, t % 2, m, :]).then_inc(s_free, 1)
                    dve.wait_ge(s_free, t + 1)
                    dve.tensor_copy(top_f[0:r, :, :], top_i[0:r, :, :])
                    tv = top[0:r, :, :].rearrange("p (h n) k -> p h n k", n=2)
                    own.fence(dve.tensor_tensor(cand[0:r, :, :, :],
                                                tv[:, :, 0, :].unsqueeze(3).to_broadcast([r, PH, TOPK, TOPK]),
                                                tv[:, :, 1, :].unsqueeze(2).to_broadcast([r, PH, TOPK, TOPK]), ALU.add))
                    cf = cand[0:r, :, :, :].rearrange("p h a b -> p h (a b)")
                    own.fence(two_eights(r, PH, lambda m: best[0:r, m, :], lambda m: sel[0:r, m, :], lambda m: cf[:, m, :]))
                    dve.tensor_tensor(hot[0:r, 0, :, 0:PH].rearrange("p k h -> p h k"), best[0:r, :, :],
                                      best[0:r, :, 0:1].to_broadcast([r, PH, TOPK]), ALU.subtract)
                    sf = sel[0:r, :, :].rearrange("p h k -> p (h k)")
                    dve.tensor_scalar(pick[0:r, 0, :], sf, 4, None, ALU.logical_shift_right)
                    own.fence(dve.tensor_scalar(pick[0:r, 1, :], sf, TOPK - 1, None, ALU.bitwise_and))
                    if t:
                        dve.wait_ge(turned, t)
                    dve.tensor_copy(best[0:r, :, :], hot[0:r, 0, :, 0:PH].rearrange("p k h -> p h k")).then_inc(shifted, 1)
                    dve.wait_ge(shifted, t + 1)
                    own.fence(dve.tensor_copy(pick_f[0:r, :, :], pick[0:r, :, :]))
                    tf = top_f[0:r, :, :].rearrange("p (h n) k -> p h n k", n=2)
                    for n in range(2):
                        own.fence(dve.tensor_tensor(hot[0:r, :, :, :].rearrange("p h k a -> p (h k) a"),
                                                    pick_f[0:r, n, :].unsqueeze(2).to_broadcast([r, HK, TOPK]),
                                                    k.iota[0:r, 0:TOPK].unsqueeze(1).to_broadcast([r, HK, TOPK]), ALU.is_equal))
                        own.fence(dve.tensor_tensor(hot[0:r, :, :, :], hot[0:r, :, :, :],
                                                    tf[:, :, n, :].unsqueeze(2).to_broadcast([r, PH, TOPK, TOPK]), ALU.mult))
                        own.fence(dve.tensor_reduce(res[0:r, n, :], hot[0:r, :, :, :].rearrange("p h k a -> p (h k) a"),
                                                    AX.X, ALU.add))
                    dve.wait_ge(expd, t + 1)
                    g = res[0:r, 2, :].rearrange("p (h k) -> p h k", h=PH)
                    own.fence(dve.tensor_reduce(tot[0:r, :], g, AX.X, ALU.add))
                    own.fence(dve.reciprocal(tot[0:r, :], tot[0:r, :]))
                    dve.tensor_tensor(g, g, tot[0:r, :].unsqueeze(2).to_broadcast([r, PH, TOPK]), ALU.mult).then_inc(ready, 1)
                    dve.wait_ge(ready, t + 1)
                    dve.wait_ge(turned, t + 1)
                    c = slice(t * P, t * P + r)
                    for n, dst in enumerate((gi, gj, gate)):
                        ins = dve.tensor_copy(dst[:, c], k.pb[4][:, n * P:n * P + r])
                    ins.then_inc(taken, 1)
                    dve.wait_ge(taken, t + 1)
                own.fence(dve.tensor_copy(gate_hi[:, :], gate[:, :]))
                own.fence(dve.tensor_tensor(gate_lo[:, :], gate[:, :], gate_hi[:, :].bitcast(F32), ALU.subtract))


@phase
def spread_gates(k, a, x_hi, x_lo, e_dram, gi, gj, gate_hi, gate_lo, g_dram):
    nc = k.nc
    GROUPS = TB // TG
    BODY = 4
    ALL = NB * GROUPS
    BODIES = UT // 2
    TAIL = ALL - BODY * BODIES
    with ExitStack() as ctx:
        ex = Activations(k, a, "ex1", UT, x_hi, x_lo, e_dram, ctx)
        eq = [k.sb(f"sg_eq{b}", [P, TG, P], F32, ctx) for b in range(2)]
        ai = [k.sb(f"sg_ai{b}", [P, TG, P], F32R, ctx) for b in range(2)]
        bj = [k.sb(f"sg_bj{b}", [P, TG, 2, P], F32R, ctx) for b in range(2)]
        low = [k.sb(f"sg_low{b}", [P, TG, P], F32, ctx) for b in range(2)]
        stage = [k.sb(f"sg_stage{b}", [P, NK, TB], F32, ctx) for b in range(2)]
        eq_done, hot, low_in, mm, low_out, taken = (k.sem("sg_" + n) for n in
            ("eq_done", "hot", "low_in", "mm", "low_out", "taken"))
        each = lambda x, u: x[:, ds(u * TG, TG)].unsqueeze(2).to_broadcast([P, TG, P])
        halves = lambda b, x: k.pv[2 + b][:, :, :].rearrange("p m (t x j) -> p (m t) x j", x=2, j=NK)[:, :, x, :]
        stored = [k.sem(f"sg_stored{b}") for b in range(2)]
        with nc.Block() as block:
            @block.sync
            def _(sp):
                ex.on_sync(sp)

            @block.gpsimd
            def _(pool):
                def group(u, b):
                    pool.wait_ge(eq_done, u + 1)
                    pool.tensor_tensor(bj[b][:, :, 1, :], eq[b][:, :, :], each(gate_lo, u), ALU.mult).then_inc(low_in, 1)

                def step(n, b):
                    ex.remainder(pool, n + 1, 1 - b)
                    for c in range(2):
                        group(2 * n + 2 + c, c)

                group(0, 0)
                group(1, 1)
                ex.remainder(pool, 0, 0)
                with pool.Fori(0, UT // 2 - 1) as s:
                    for b in range(2):
                        step(2 * s + b, b)
                step(UT - 2, 0)
                for u in range(2 * UT, ALL):
                    group(u, u % 2)

            @block.vector
            def _(dve):
                def group(u, b):
                    wait(dve, mm, u - 1)
                    numbers = k.iota.unsqueeze(1).to_broadcast([P, TG, P])
                    dve.tensor_tensor(eq[b][:, :, :], numbers, each(gj, u), ALU.is_equal).then_inc(eq_done, 1)
                    dve.tensor_tensor(ai[b][:, :, :], numbers, each(gi, u), ALU.is_equal)
                    dve.wait_ge(eq_done, u + 1)
                    dve.tensor_tensor(bj[b][:, :, 0, :], eq[b][:, :, :], each(gate_hi, u).bitcast(F32),
                                      ALU.mult).then_inc(hot, 1)

                def collect(u, pair, n):
                    odd, within = n // GROUPS, n % GROUPS
                    dve.wait_ge(low_out, u + 1)
                    if within == 0:
                        wait(dve, stored[odd], 16 * pair)
                    dve.tensor_tensor(stage[odd][:, :, within * TG:(within + 1) * TG].rearrange("p j t -> p t j"),
                                      halves(n % 2, 0), low[n % 2][:, :, :], ALU.add).then_inc(taken, 1)

                def pair_of_blocks(pair, count):
                    for n in range(count):
                        u = 2 * GROUPS * pair + n
                        if not isinstance(u, int) or u + 1 < ALL:
                            group(u + 1, (n + 1) % 2)
                        collect(u, pair, n)

                group(0, 0)
                pair_of_blocks(0, 2 * GROUPS)
                with dve.Fori(1, ALL // (2 * GROUPS)) as pair:
                    pair_of_blocks(pair, 2 * GROUPS)
                pair_of_blocks(ALL // (2 * GROUPS), ALL % (2 * GROUPS))

            @block.tensor
            def _(pe):
                def group(u, b):
                    pe.wait_ge(hot, u + 1)
                    pe.wait_ge(low_in, u + 1)
                    wait(pe, taken, u - 1)
                    for n in range(TG):
                        ins = pe.matmul(k.pv[2 + b][:, n // 2, (n % 2) * 2 * P:(n % 2 + 1) * 2 * P], ai[b][:, n, :],
                                        bj[b][:, n, :, :].rearrange("p x j -> p (x j)"), start=True, stop=True)
                    ins.then_inc(mm, 1)

                def body(s, last=False):
                    def between(b):
                        for c in range(2):
                            group(BODY * s + 2 * b + c, c)
                    ex.on_tensor(pe, s, between, last)

                ex.turn(pe, 0, 0, 0)
                body(0)
                with pe.Fori(1, BODIES - 1) as s:
                    body(s)
                body(BODIES - 1, last=True)
                for u in range(ALL - TAIL, ALL):
                    group(u, u % 2)

            @block.scalar
            def _(act):
                def group(u, b):
                    act.wait_ge(mm, u + 1)
                    wait(act, taken, u - 1)
                    act.activation(low[b][:, :, :], halves(b, 1), ACT.Copy).then_inc(low_out, 1)

                def body(s, last=False):
                    def between(b):
                        for c in range(2):
                            group(BODY * s + 2 * b + c, c)
                    ex.on_scalar(act, s, between, last)

                def store(pair, odd):
                    act.wait_ge(taken, 2 * GROUPS * pair + GROUPS * (odd + 1))
                    width = GJ * TB
                    act.dma_start(g_dram[:, :, ds((2 * pair + odd) * width, width)],
                                  stage[odd][:, :, :].rearrange("p (g j) t -> p g (j t)", j=GJ)).then_inc(stored[odd], 16)

                def bodies(pair, count):
                    for x in range(count):
                        s = PER * pair + x
                        body(s, last=isinstance(s, int) and s == BODIES - 1)
                        if (x + 1) * BODY >= GROUPS > x * BODY:
                            store(pair, 0)
                    if count == PER:
                        store(pair, 1)

                PER = 2 * GROUPS // BODY
                ex.take(act, 0, 0)
                bodies(0, PER)
                with act.Fori(1, BODIES // PER) as pair:
                    bodies(pair, PER)
                bodies(BODIES // PER, BODIES % PER)
                for u in range(ALL - TAIL, ALL):
                    group(u, u % 2)
                store(BODIES // PER, 0)
                for b in range(2):
                    act.wait_ge(stored[b], 16 * ((NB + 1 - b) // 2))


@phase
def combine(k, a, e_dram, g_dram, acc):
    nc = k.nc
    NG = NK // GJ
    v_dram = a["peer_v"][0].rearrange("(i j) d -> i j d", j=NK)
    two = range(2)
    with ExitStack() as ctx:
        sb = lambda n, s, dt=F32: [k.sb(f"{n}{b}", s, dt, ctx) for b in two]
        v_raw, v_hi, v_lo = sb("v_raw", [P, GJ, D]), sb("v_hi", [P, GJ, D], F32R), sb("v_lo", [P, GJ, D], F32R)
        e_in, g_in = sb("e_in", [P, GJ, T]), sb("g_in", [P, NB, GJ, TB])
        coef = sb("coef", [P, T])
        c_hi, c_lo = sb("c_hi", [P, GJ, T], F32R), sb("c_lo", [P, GJ, T], F32R)
        v_loaded, e_loaded, g_loaded = ([k.sem(f"cb_{n}_loaded{b}") for b in two] for n in "veg")
        v_hi_done, v_lo_done, coef_done, c_done, v_products, added, cleared = (k.sem("cb_" + n) for n in
            ("v_hi_done", "v_lo_done", "coef_done", "c_done", "v_products", "added", "cleared"))
        blocks = lambda x: x.rearrange("p (n t) -> p n t", n=NB)

        def groups(eng, group):
            group(0, 0, 0)
            group(1, 0, 1)
            with eng.Fori(1, NG // 2) as s:
                for b in two:
                    group(2 * s + b, s, b)

        with nc.Block() as block:
            @block.sync
            def _(sp):
                def group(g, m, b):
                    wait(sp, v_lo_done, g - 1)
                    sp.dma_start(v_raw[b][:, :, :], v_dram[:, ds(GJ * g, GJ), :]).then_inc(v_loaded[b], 16)
                    wait(sp, coef_done, GJ * (g - 1))
                    sp.dma_start(e_in[b][:, :, :], e_dram[:, ds(GJ * g, GJ), :]).then_inc(e_loaded[b], 16)
                    sp.dma_start(g_in[b][:, :, :, :].rearrange("p n j t -> p (n j t)").unsqueeze(1),
                                 g_dram[:, ds(g, 1), :]).then_inc(g_loaded[b], 16)

                groups(sp, group)

            @block.tensor
            def _(pe):
                def group(g, m, b):
                    pe.wait_ge(v_lo_done, g + 1)
                    pe.wait_ge(c_done, GJ * (g + 1))
                    for c in range(DC):
                        wait(pe, added, DC * g + c - 3)
                        w = slice(c * P, (c + 1) * P)
                        for h in two:
                            ts = slice(h * HALF, (h + 1) * HALF)
                            ins = mm3(pe, k.pv[c % 4][:, h, 0:HALF], GJ, lambda x, j: x[:, j, w], v_hi[b], v_lo[b],
                                      lambda x, j: x[:, j, ts], c_hi[b], c_lo[b])
                        ins.then_inc(v_products, 1)

                groups(pe, group)

            @block.scalar
            def _(act):
                def group(g, m, b):
                    act.wait_ge(v_loaded[b], 16 * (m + 1))
                    wait(act, v_products, DC * (g - 1))
                    act.activation(v_hi[b][:, :, :], v_raw[b][:, :, :], ACT.Copy).then_inc(v_hi_done, 1)

                groups(act, group)

            @block.vector
            def _(dve):
                def split(g, b):
                    dve.wait_ge(v_hi_done, g + 1)
                    dve.tensor_tensor(v_lo[b][:, :, :], v_raw[b][:, :, :], v_hi[b][:, :, :].bitcast(F32),
                                      ALU.subtract).then_inc(v_lo_done, 1)

                def add(g, c):
                    dve.wait_ge(v_products, DC * g + c + 1)
                    wait(dve, added, DC * (g - 1) + c + 1)
                    out = acc[:, c, :].rearrange("p (h t) -> p h t", h=2)
                    ps = k.pv[c % 4][:, :, 0:HALF]
                    if isinstance(g, int) and g == 0:
                        dve.tensor_copy(out, ps).then_inc(added, 1)
                    else:
                        dve.tensor_tensor(out, out, ps, ALU.add).then_inc(added, 1)

                def group(g, b, last=False):
                    for c in range(DC):
                        if c == 2 and not last:
                            split(g + 1, 1 - b)
                        add(g, c)

                split(0, 0)
                group(0, 0)
                with dve.Fori(0, NG // 2 - 1) as s:
                    group(2 * s + 1, 1)
                    group(2 * s + 2, 0)
                group(NG - 1, 1, last=True)
                dve.wait_ge(added, DC * NG)

            @block.gpsimd
            def _(pool):
                def group(g, m, b):
                    pool.wait_ge(e_loaded[b], 16 * (m + 1))
                    pool.wait_ge(g_loaded[b], 16 * (m + 1))
                    wait(pool, v_products, DC * (g - 1))
                    for j in range(GJ):
                        n = GJ * g + j
                        wait(pool, c_done, n - 1)
                        pool.tensor_tensor(blocks(coef[j % 2][:, :]), blocks(e_in[b][:, j, :]), g_in[b][:, :, j, :], ALU.mult)
                        fence(pool, pool.tensor_tensor(blocks(c_hi[b][:, j, :]), blocks(e_in[b][:, j, :]),
                                                       g_in[b][:, :, j, :], ALU.mult), coef_done, n + 1)
                        pool.tensor_tensor(c_lo[b][:, j, :], coef[j % 2][:, :], c_hi[b][:, j, :].bitcast(F32),
                                           ALU.subtract).then_inc(c_done, 1)

                groups(pool, group)


@phase
def finish(k, a, o, h_dram, acc):
    nc = k.nc
    with ExitStack() as ctx:
        h_tok = k.sb("fin_h", [P, NT, D], F32, ctx)
        junk = k.sb("fin_junk", [P, D], F32, ctx)
        g = k.sb("fin_gain", [P, D], F32, ctx)
        ms = k.sb("fin_ms", [P, NT], F32, ctx)
        loaded, turned, summed, squared, rooted, own_s, ready, stored = (k.sem("fin_" + n) for n in
            ("loaded", "turned", "summed", "squared", "rooted", "own", "ready", "stored"))
        with nc.Block() as block:
            @block.sync
            def _(sp):
                for dst, src in zip((h_tok[:, 0:4, :], h_tok[0:NS, 4, :]), h_dram):
                    sp.dma_start(dst, src).then_inc(loaded, 16)
                sp.dma_start(g[:, :], a["norm_final"].unsqueeze(0).to_broadcast([P, D])).then_inc(loaded, 16)
                sp.wait_ge(ready, 4)
                sp.dma_start(o["y_p"][0].rearrange("(t p) d -> p t d", p=P), h_tok[:, 0:4, :]).then_inc(stored, 16)
                sp.wait_ge(ready, NT)
                sp.dma_start(o["y_s"][:, 0, :], h_tok[0:NS, 4, :]).then_inc(stored, 16)
                sp.wait_ge(stored, 32)

            @block.tensor
            def _(pe):
                for t, r in enumerate(ROWS):
                    if t >= 2:
                        pe.wait_ge(summed, t - 1)
                    for c in range(DC):
                        ins = pe.transpose(k.pv[t % 2][0:r, c // 4, (c % 4) * P:(c % 4 + 1) * P], acc[:, c, t * P:t * P + r], k.eye)
                    ins.then_inc(turned, 1)

            @block.vector
            def _(dve):
                own = Own(dve, own_s)
                own.fence(dve.memset(ms[:, :], 1.0))
                dve.wait_ge(loaded, 48)
                for t, r in enumerate(ROWS):
                    dve.wait_ge(turned, t + 1)
                    x = h_tok[0:r, t, :].rearrange("p (n c) -> p n c", n=2)
                    dve.tensor_tensor(x, x, k.pv[t % 2][0:r, :, :], ALU.add).then_inc(summed, 1)
                dve.wait_ge(rooted, 1)
                own.fence(dve.reciprocal(ms[:, :], ms[:, :]))
                for t, r in enumerate(ROWS):
                    dve.scalar_tensor_tensor(h_tok[0:r, t, :], h_tok[0:r, t, :], ms[0:r, t:t + 1], g[0:r, :],
                                             ALU.mult, ALU.mult).then_inc(ready, 1)

            @block.scalar
            def _(act):
                for t, r in enumerate(ROWS):
                    act.wait_ge(summed, t + 1)
                    fence(act, act.activation(junk[0:r, :], h_tok[0:r, t, :], ACT.Square, scale=D ** -0.5,
                                              accum_out=ms[0:r, t:t + 1]), squared, t + 1)
                act.activation(ms[:, :], ms[:, :], ACT.Sqrt, bias=k.eps[:, :]).then_inc(rooted, 1)


def program(nc, a, o, g_dram, e_dram, h_store, side_dram):
    w_in = a["w_in"][0]
    with ExitStack() as whole:
        k = Core(nc, whole)
        k.pv = [whole.enter_context(nc.psum_tensor(f"ps{n}", [P, 2, 512], F32)) for n in range(4)]
        k.pb = [k.pv[n // 2][:, n % 2, :] for n in range(8)]
        load_constants(k, a)
        tokens = whole.enter_context(ExitStack())
        x_hi, x_lo = k.sb("x_hi", [P, DC, T], F32R, tokens), k.sb("x_lo", [P, DC, T], F32R, tokens)
        with ExitStack() as c:
            x_tok = k.sb("x_tok", [P, NT, D], F32, c)
            norm_and_turn(k, "norm1", x_tok, k.vecs[:, 0:DC], x_hi, x_lo,
                          load=[a["x_prompt"][0, t * P:(t + 1) * P, :] for t in range(4)] + [a["x_sample"][:, 0, :]],
                          extra=[(k.ret[:, :], a["c_ret"]), (k.ba_w[:, :, :], columns(w_in, COL_BA, 2 * H))])
        with ExitStack() as branches:
            oa_hi, oa_lo = (k.sb(n, [P, H, T], F32R, branches) for n in ("oa_hi", "oa_lo"))
            with ExitStack() as c:
                sb = lambda n, s, dt=F32: k.sb(n, s, dt, c)
                gate_a = sb("gate_a", [P, NT, QA])
                beta, logd = sb("beta", [P, NT, H]), sb("logd", [P, NT, H])
                pre = sb("pre", [P, CT, PAD + T])
                small_projection(k, pre, x_hi, x_lo, beta, logd)
                stream(k, "proj_a", [
                    Job(columns(w_in, 0, CONV_CH), 3, True, x_hi, x_lo, to_channels(pre, PAD + T, PAD)),
                    Job(columns(w_in, COL_GATE_A, QA), 1, False, x_hi, x_lo, to_tokens(gate_a, QA), ACT.Silu)])
                k_tok, v_tok = sb("k_tok", [P, NT, QA]), sb("v_tok", [P, NT, QA])
                convolve(k, a, o, pre, k_tok, v_tok, x_hi, x_lo, side_dram)
                delta_prompt(k, a, o, pre, k_tok, v_tok, beta, logd, x_hi, x_lo, side_dram)
                delta_sample(k, a, o, pre, v_tok, beta, logd)
                gate_and_turn(k, a, "gate_a", v_tok, gate_a, a["gn_a"], DK, oa_hi, oa_lo)
            ob_hi, ob_lo = (k.sb(n, [P, DC, T], F32R, branches) for n in ("ob_hi", "ob_lo"))
            with ExitStack() as c:
                sb = lambda n, s, dt=F32: k.sb(n, s, dt, c)
                gate_b, v_b = sb("gate_b", [P, NT, VB]), sb("v_b", [P, NT, VB])
                qk_b = sb("qk_b", [P, 2 * H, T])
                stream(k, "proj_b", [
                    Job(columns(w_in, COL_V_B, VB), 2, False, x_hi, x_lo, to_tokens(v_b, VB)),
                    Job(columns(w_in, COL_GATE_B, VB), 2, False, x_hi, x_lo, to_tokens(gate_b, VB), ACT.Silu)],
                    extra=[(qk_b[:, :, :], side_dram[:, 0:2 * H, :])])
                kb_tok = sb("kb_tok", [P, 4, QA])
                rotate(k, a, qk_b, kb_tok)
                retention_prompt(k, a, o, qk_b, v_b, kb_tok)
                retention_sample(k, a, o, qk_b, v_b)
                gate_and_turn(k, a, "gate_b", v_b, gate_b, a["gn_b"], DV_B, ob_hi, ob_lo)
            with ExitStack() as c:
                sel_a, sel_b, br_a, br_b = (k.sb(n, [P, DC, T], F32, c) for n in ("sel_a", "sel_b", "br_a", "br_b"))
                stream(k, "branches", [
                    Job(columns(a["w_br_a"][0], 0, D), 2, True, oa_hi, oa_lo, to_channels(br_a, T)),
                    Job(columns(a["w_br_b"][0], 0, D), 2, True, ob_hi, ob_lo, to_channels(br_b, T))],
                    extra=[(sel_a[:, :, :], side_dram[:, 2 * H:2 * H + DC, :]), (sel_b[:, :, :], side_dram[:, 2 * H + DC:SIDE, :])])
                merge(k, sel_a, sel_b, br_a, br_b, ob_hi, ob_lo)
            with ExitStack() as c:
                h_tok, x_tok = k.sb("h_tok", [P, NT, D], F32, c), k.sb("x_again", [P, NT, D], F32, c)
                halves = lambda x: [x[:, 0:4, :], x[0:NS, 4, :]]
                x_dram = [a["x_prompt"][0].rearrange("(t p) d -> p t d", p=P), a["x_sample"][:, 0, :]]
                h_dram = [h_store[0:NP_TOK, :].rearrange("(t p) d -> p t d", p=P), h_store[NP_TOK:T, :]]
                stream(k, "w_out", [Job(columns(a["w_out"][0], 0, D), 2, False, ob_hi, ob_lo, to_tokens(h_tok, D))],
                       extra=list(zip(halves(x_tok), x_dram)))
                norm_and_turn(k, "norm2", h_tok, k.vecs[:, DC:2 * DC], x_hi, x_lo, plus=x_tok,
                              stores=list(zip((4, NT), h_dram, halves(h_tok))))
        with ExitStack() as c:
            gi, gj = k.sb("gi", [P, T], F32, c), k.sb("gj", [P, T], F32, c)
            g_hi, g_lo = k.sb("g_hi", [P, T], F32R, c), k.sb("g_lo", [P, T], F32, c)
            with ExitStack() as c2:
                q = k.sb("peer_q", [P, HP, T], F32, c2)
                keysT = k.sb("keysT", [P, HP, NK], F32, c2)
                with ExitStack() as c3:
                    keys = k.sb("keys", [P, HP, NK], F32, c3)
                    stream(k, "queries", [Job(columns(a["peer_wq"][0], 0, HP * P), 4, True, x_hi, x_lo, to_channels(q, T))],
                           extra=[(keys[:, :, :], a["peer_keys"][0].rearrange("h p k d -> k (h p) d"))])
                    turn_keys(k, keys, keysT)
                retrieve(k, a, x_hi, x_lo, e_dram, q, keysT, gi, gj, g_hi, g_lo)
            spread_gates(k, a, x_hi, x_lo, e_dram, gi, gj, g_hi, g_lo, g_dram)
        tokens.close()
        acc = k.sb("acc", [P, DC, T])
        combine(k, a, e_dram, g_dram, acc)
        finish(k, a, o, h_dram, acc)


INPUTS = ("x_prompt", "x_sample", "state_conv_a", "state_delta", "state_ret", "norm_mix", "w_in", "conv_w",
          "a_log", "dt_bias", "gn_a", "gn_b", "w_br_a", "w_br_b", "w_out", "norm_ffn", "peer_wq", "peer_keys",
          "peer_u", "peer_v", "norm_final")
OUTPUTS = {
    "y_p": (1, NP_TOK, D), "y_s": (NS, 1, D),
    "conv_p": (1, 1, PAD, CONV_CH), "delta_p": (1, 1, H, DK, DK), "ret_p": (1, 1, H, DK, DV_B),
    "conv_s": (1, NS, PAD, CONV_CH), "delta_s": (1, NS, H, DK, DK), "ret_s": (1, NS, H, DK, DV_B),
}


def build(nc, shapes):
    a = {n: nc.dram_tensor("in_" + n, s, F32, kind="ExternalInput").ap() for n, s in shapes.items()}
    o = {n: nc.dram_tensor("out_" + n, s, F32, kind="ExternalOutput").ap() for n, s in OUTPUTS.items()}
    g_dram = nc.dram_tensor("gates", (P, NK // GJ, NB * GJ * TB), F32, kind="Internal").ap()
    side_dram = nc.dram_tensor("side", (P, SIDE, T), F32, kind="Internal").ap()
    h_store = nc.dram_tensor("h_store", (T, D), F32, kind="Internal").ap()
    e_dram = nc.dram_tensor("activations", (P, NK, T), F32, kind="Internal").ap()
    program(nc, a, o, g_dram, e_dram, h_store, side_dram)


def kernel(**inputs):
    import concourse.bacc as bacc
    from concourse.bass_utils import run_bass_kernel_spmd

    arrays = {n: np.ascontiguousarray(inputs[n]) for n in INPUTS}
    arrays.update(constants())
    nc = bacc.Bacc("TRN2", target_bir_lowering=False, num_devices=1)
    build(nc, {n: x.shape for n, x in arrays.items()})
    r = run_bass_kernel_spmd(nc, [{"in_" + n: x for n, x in arrays.items()}], core_ids=[0])
    return tuple(r.results[0]["out_" + n] for n in OUTPUTS)
```
